# Optimizing a Trainium2 kernel written in Bass

```python
import functools
import jax, jax.numpy as jnp
from jax import lax
import numpy as np

D_MODEL = 1024
BATCH = 1
SEQ = 512
DEPTH = 1
DEC_BATCH = 8
DEC_SEQ = 1
PAST_LEN = 2048
PAGE_SIZE = 128

HEAD_DIM = 64
N_HEADS = D_MODEL // HEAD_DIM
H_A = N_HEADS // 4
H_B = N_HEADS // 4
H_C = N_HEADS - H_A - H_B
W_A = H_A * HEAD_DIM
W_B = H_B * HEAD_DIM
W_C = H_C * HEAD_DIM
D_MIX = W_A + W_B + W_C
D_IN = 3 * W_A + 2 * W_B + 3 * W_C + H_C
SPLIT_OFFSETS = (W_A, 2 * W_A, 3 * W_A, 3 * W_A + W_B, 3 * W_A + 2 * W_B,
                 3 * W_A + 2 * W_B + W_C, 3 * W_A + 2 * W_B + 2 * W_C, 3 * W_A + 2 * W_B + 3 * W_C)
CONV_W = 3
CHUNK = 128
Q_BLOCK = 128
N_GROUPS = 4
EXPERTS_PER_GROUP = 8
TOP_K = 2
D_EXPERT = D_MODEL // 2
D_PLE = 256
FORGET_BIAS_LO = 3.0
FORGET_BIAS_HI = 10.0
EPS = 1e-6

kernel_name = 'hymba_conv_gmlp_fox_hmoe_step'

def rmsnorm(x, g):
    xf = x.astype(jnp.float32)
    y = xf * lax.rsqrt(jnp.mean(xf * xf, axis=-1, keepdims=True) + EPS)
    return (y * g.astype(jnp.float32)).astype(x.dtype)

def layernorm(x, g, b):
    xf = x.astype(jnp.float32)
    mu = jnp.mean(xf, axis=-1, keepdims=True)
    var = jnp.mean(jnp.square(xf - mu), axis=-1, keepdims=True)
    y = (xf - mu) * lax.rsqrt(var + EPS)
    return (y * g.astype(jnp.float32) + b.astype(jnp.float32)).astype(x.dtype)

def short_conv_mixer(b_gate, c_gate, h, conv_w, buf):
    z = c_gate * h
    L = z.shape[1]
    zp = jnp.concatenate([buf.astype(z.dtype), z], axis=1)
    y = sum(conv_w[j] * zp[:, j:j + L] for j in range(CONV_W))
    return b_gate * y, zp[:, L:]

def chunk_gmlp_mixer(u, v, ln_g, ln_b, w_s, b_s):
    vn = layernorm(v, ln_g, ln_b)
    n, L, _ = vn.shape
    c = min(L, CHUNK)
    nc = L // c
    causal = jnp.tril(jnp.ones((CHUNK, CHUNK), dtype=bool))
    ws = jnp.where(causal, w_s, 0)[:, :c, :c]
    vh = vn.reshape(n, nc, c, H_B, HEAD_DIM)
    s = jnp.einsum('hts,ncshd->ncthd', ws.astype(vh.dtype), vh) + b_s[:, :c].T[:, :, None]
    return u * s.reshape(n, L, W_B), vn

def fox_prompt(q, k, v, logf):
    n, L, h, d = q.shape
    scale = d ** -0.5
    c = jnp.cumsum(logf, axis=1)
    nb = L // Q_BLOCK
    qb = q.reshape(n, nb, Q_BLOCK, h, d).transpose(1, 0, 2, 3, 4)
    cb = c.reshape(n, nb, Q_BLOCK, h).transpose(1, 0, 2, 3)
    starts = jnp.arange(nb, dtype=jnp.int32) * Q_BLOCK
    kpos = jnp.arange(L, dtype=jnp.int32)
    c_k = c.transpose(0, 2, 1)[:, :, None, :]

    def block(args):
        qi, ci, start = args
        s = jnp.einsum('nqhd,nkhd->nhqk', qi, k).astype(jnp.float32) * scale
        s = s + ci.transpose(0, 2, 1)[..., None] - c_k
        qpos = start + jnp.arange(Q_BLOCK, dtype=jnp.int32)
        s = jnp.where(kpos[None, :] <= qpos[:, None], s, -jnp.inf)
        p = jax.nn.softmax(s, axis=-1)
        return jnp.einsum('nhqk,nkhd->nqhd', p.astype(v.dtype), v)

    o = lax.map(block, (qb, cb, starts))
    return o.transpose(1, 0, 2, 3, 4).reshape(n, L, h * d)

def fox_sample(q, k, v, logf, k_past, v_past, logf_past):
    n, L, h, d = q.shape
    P = k_past.shape[1]
    scale = d ** -0.5
    lfp = logf_past.astype(jnp.float32)
    suffix = lax.cumsum(lfp, axis=1, reverse=True) - lfp
    cnT = jnp.cumsum(logf, axis=1).transpose(0, 2, 1)
    s_past = jnp.einsum('nqhd,nkhd->nhqk', q, k_past).astype(jnp.float32) * scale
    s_past = s_past + cnT[..., None] + suffix.transpose(0, 2, 1)[:, :, None, :]
    s_new = jnp.einsum('nqhd,nkhd->nhqk', q, k).astype(jnp.float32) * scale
    s_new = s_new + cnT[..., None] - cnT[:, :, None, :]
    causal = jnp.tril(jnp.ones((L, L), dtype=bool))
    s_new = jnp.where(causal, s_new, -jnp.inf)
    p = jax.nn.softmax(jnp.concatenate([s_past, s_new], axis=-1), axis=-1).astype(v.dtype)
    o = (jnp.einsum('nhqk,nkhd->nqhd', p[..., :P], v_past)
         + jnp.einsum('nhqk,nkhd->nqhd', p[..., P:], v))
    return o.reshape(n, L, h * d)

def hier_moe(h, w_grp, b_grp, w_rt, b_rt, w_gate, w_up, w_down):
    grp_prob = jax.nn.softmax((h @ w_grp).astype(jnp.float32) + b_grp.astype(jnp.float32), axis=-1)
    p_g, g_idx = lax.top_k(grp_prob, 1)
    exp_logits = jnp.einsum('nld,dge->nlge', h, w_rt).astype(jnp.float32) + b_rt.astype(jnp.float32)
    exp_logits = jnp.take_along_axis(exp_logits, g_idx[..., None], axis=2)[:, :, 0]
    p_e, e_idx = lax.top_k(jax.nn.softmax(exp_logits, axis=-1), TOP_K)
    w = p_g * p_e / jnp.sum(p_e, axis=-1, keepdims=True)
    fine = jnp.sum(jax.nn.one_hot(e_idx, EXPERTS_PER_GROUP, dtype=jnp.float32) * w[..., None], axis=-2)
    gates = (jax.nn.one_hot(g_idx[..., 0], N_GROUPS, dtype=jnp.float32)[..., None]
             * fine[:, :, None, :]).astype(h.dtype)
    y = jnp.zeros_like(h)
    for g in range(N_GROUPS):
        a = jnp.einsum('nld,edf->nlef', h, w_gate[g])
        b = jnp.einsum('nld,edf->nlef', h, w_up[g])
        act = jax.nn.silu(a) * b * gates[:, :, g, :, None]
        y = y + jnp.einsum('nlef,efd->nld', act, w_down[g])
    return y

def trunk_layer(x, p_i, lw, conv_buf, attend):
    n, L, _ = x.shape
    h = rmsnorm(x, lw['g_mix'])
    proj = h @ lw['w_in']
    b_a, c_a, h_a, u_b, v_b, q_c, k_c, v_c, f_c = jnp.split(proj, SPLIT_OFFSETS, axis=-1)
    y_a, new_buf = short_conv_mixer(b_a, c_a, h_a, lw['conv_w'], conv_buf)
    y_b, vn = chunk_gmlp_mixer(u_b, v_b, lw['ln_g'], lw['ln_b'], lw['w_s'], lw['b_s'])
    q = q_c.reshape(n, L, H_C, HEAD_DIM)
    k = k_c.reshape(n, L, H_C, HEAD_DIM)
    v = v_c.reshape(n, L, H_C, HEAD_DIM)
    logf = jax.nn.log_sigmoid(f_c.astype(jnp.float32) + lw['b_f'].astype(jnp.float32))
    y_c = attend(q, k, v, logf)
    g = lw['g_out']
    mixed = jnp.concatenate([rmsnorm(y_a, g[:W_A]), rmsnorm(y_b, g[W_A:W_A + W_B]),
                             rmsnorm(y_c, g[W_A + W_B:])], axis=-1)
    x = x + mixed @ lw['w_o']
    x = x + hier_moe(rmsnorm(x, lw['g_ffn']), lw['w_grp'], lw['b_grp'], lw['w_rt'], lw['b_rt'],
                     lw['w_gate'], lw['w_up'], lw['w_down'])
    gate = jax.nn.sigmoid(rmsnorm(x, lw['g_ple']) @ lw['w_ple_gate'])
    x = x + (p_i.astype(x.dtype) @ lw['w_ple']) * gate
    return x, k, v, logf, new_buf, vn

def setup_inputs(seed: int = 0) -> dict:
    key = jax.random.key(seed)
    keys = jax.random.split(key, 32)

    def nrm(i, shape, scale=1.0):
        return jax.random.normal(keys[i], shape, jnp.float32) * scale

    n_pages = PAST_LEN // PAGE_SIZE
    n_used = DEC_BATCH * n_pages
    n_pool = n_used + (n_used + 3) // 4
    page_table = jax.random.permutation(keys[0], n_pool)[:n_used].reshape(DEC_BATCH, n_pages).astype(jnp.int32)
    head_bias = jnp.linspace(FORGET_BIAS_LO, FORGET_BIAS_HI, H_C, dtype=jnp.float32)
    return {
        'x_prompt': nrm(1, (BATCH, SEQ, D_MODEL)),
        'x_sample': nrm(2, (DEC_BATCH, DEC_SEQ, D_MODEL)),
        'p_prompt': nrm(3, (DEPTH, BATCH, SEQ, D_PLE)),
        'p_sample': nrm(4, (DEPTH, DEC_BATCH, DEC_SEQ, D_PLE)),
        'cache_k': nrm(5, (DEPTH, n_pool, PAGE_SIZE, H_C, HEAD_DIM)),
        'cache_v': nrm(6, (DEPTH, n_pool, PAGE_SIZE, H_C, HEAD_DIM)),
        'cache_logf': jax.nn.log_sigmoid(head_bias + nrm(7, (DEPTH, n_pool, PAGE_SIZE, H_C), 0.5)),
        'state_conv': nrm(8, (DEPTH, DEC_BATCH, CONV_W - 1, W_A)),
        'page_table': page_table,
        'g_mix': 1.0 + nrm(9, (DEPTH, D_MODEL), 0.02),
        'w_in': nrm(10, (DEPTH, D_MODEL, D_IN), D_MODEL ** -0.5),
        'conv_w': nrm(11, (DEPTH, CONV_W, W_A), CONV_W ** -0.5),
        'ln_g': 1.0 + nrm(12, (DEPTH, W_B), 0.02),
        'ln_b': nrm(13, (DEPTH, W_B), 0.02),
        'w_s': nrm(14, (DEPTH, H_B, CHUNK, CHUNK), CHUNK ** -0.5),
        'b_s': 1.0 + nrm(15, (DEPTH, H_B, CHUNK), 0.02),
        'b_f': head_bias + nrm(16, (DEPTH, H_C), 0.1),
        'g_out': 1.0 + nrm(17, (DEPTH, D_MIX), 0.02),
        'w_o': nrm(18, (DEPTH, D_MIX, D_MODEL), D_MIX ** -0.5),
        'g_ffn': 1.0 + nrm(19, (DEPTH, D_MODEL), 0.02),
        'w_grp': nrm(20, (DEPTH, D_MODEL, N_GROUPS), D_MODEL ** -0.5),
        'b_grp': nrm(21, (DEPTH, N_GROUPS), 0.01),
        'w_rt': nrm(22, (DEPTH, D_MODEL, N_GROUPS, EXPERTS_PER_GROUP), D_MODEL ** -0.5),
        'b_rt': nrm(23, (DEPTH, N_GROUPS, EXPERTS_PER_GROUP), 0.01),
        'w_gate': nrm(24, (DEPTH, N_GROUPS, EXPERTS_PER_GROUP, D_MODEL, D_EXPERT), D_MODEL ** -0.5),
        'w_up': nrm(25, (DEPTH, N_GROUPS, EXPERTS_PER_GROUP, D_MODEL, D_EXPERT), D_MODEL ** -0.5),
        'w_down': nrm(26, (DEPTH, N_GROUPS, EXPERTS_PER_GROUP, D_EXPERT, D_MODEL), D_EXPERT ** -0.5),
        'g_ple': 1.0 + nrm(27, (DEPTH, D_MODEL), 0.02),
        'w_ple': nrm(28, (DEPTH, D_PLE, D_MODEL), D_PLE ** -0.5),
        'w_ple_gate': nrm(29, (DEPTH, D_MODEL, D_MODEL), D_MODEL ** -0.5),
        'g_final': 1.0 + nrm(30, (D_MODEL,), 0.02),
    }

def reference(x_prompt, x_sample, p_prompt, p_sample, cache_k, cache_v, cache_logf, state_conv,
              page_table, g_mix, w_in, conv_w, ln_g, ln_b, w_s, b_s, b_f, g_out, w_o, g_ffn,
              w_grp, b_grp, w_rt, b_rt, w_gate, w_up, w_down, g_ple, w_ple, w_ple_gate, g_final):
    n_dec = page_table.shape[0]
    xp, xs = x_prompt, x_sample
    kp_l, vp_l, lfp_l, cvp_l = [], [], [], []
    ks_l, vs_l, lfs_l, cvs_l, chv_l = [], [], [], [], []
    for i in range(DEPTH):
        lw = dict(g_mix=g_mix[i], w_in=w_in[i], conv_w=conv_w[i], ln_g=ln_g[i], ln_b=ln_b[i],
                  w_s=w_s[i], b_s=b_s[i], b_f=b_f[i], g_out=g_out[i], w_o=w_o[i], g_ffn=g_ffn[i],
                  w_grp=w_grp[i], b_grp=b_grp[i], w_rt=w_rt[i], b_rt=b_rt[i], w_gate=w_gate[i],
                  w_up=w_up[i], w_down=w_down[i], g_ple=g_ple[i], w_ple=w_ple[i],
                  w_ple_gate=w_ple_gate[i])
        buf0 = jnp.zeros((xp.shape[0], CONV_W - 1, W_A), xp.dtype)
        xp, k, v, lf, buf, _ = trunk_layer(xp, p_prompt[i], lw, buf0, fox_prompt)
        kp_l.append(k)
        vp_l.append(v)
        lfp_l.append(lf)
        cvp_l.append(buf)
        k_past = cache_k[i, page_table].reshape(n_dec, -1, H_C, HEAD_DIM)
        v_past = cache_v[i, page_table].reshape(n_dec, -1, H_C, HEAD_DIM)
        lf_past = cache_logf[i, page_table].reshape(n_dec, -1, H_C)
        attend = functools.partial(fox_sample, k_past=k_past, v_past=v_past, logf_past=lf_past)
        xs, k, v, lf, buf, vn = trunk_layer(xs, p_sample[i], lw, state_conv[i], attend)
        ks_l.append(k)
        vs_l.append(v)
        lfs_l.append(lf)
        cvs_l.append(buf)
        chv_l.append(vn)
    y_prompt = rmsnorm(xp, g_final)
    y_sample = rmsnorm(xs, g_final)
    return (y_prompt, y_sample, jnp.stack(kp_l), jnp.stack(vp_l), jnp.stack(lfp_l), jnp.stack(cvp_l),
            jnp.stack(ks_l), jnp.stack(vs_l), jnp.stack(lfs_l), jnp.stack(cvs_l), jnp.stack(chv_l))


_drawn_inputs = setup_inputs


def setup_inputs(seed=0):
    import zlib

    import numpy as np

    out = dict(_drawn_inputs(seed))
    spreads = {}
    factors = {'ln_g': 8.899,
     'ln_b': 8.071,
     'b_s': 4.783,
     'g_out': 2.858,
     'g_ffn': 2.794,
     'b_grp': 8.0,
     'g_ple': 64.0,
     'g_final': 7.635,
     'b_rt': 7.372}
    for name, (base, spread) in spreads.items():
        noise = np.random.default_rng([zlib.crc32(name.encode()), seed]).standard_normal(out[name].shape)
        drawn = base * np.exp(spread * noise) if base else spread * noise
        out[name] = __import__('jax').numpy.asarray(drawn.astype(out[name].dtype))
    for name, factor in factors.items():
        out[name] = (out[name] * factor).astype(out[name].dtype)
    return out
```

```python
from contextlib import ExitStack

import concourse.bass as bass
from concourse import mybir

F32 = mybir.dt.float32
I32 = mybir.dt.int32
ALU = mybir.AluOpType
ACT = mybir.ActivationFunctionType
AX = mybir.AxisListType

P = 128
BANK = 512
D = 1024
DC = D // P
SEQ, NB = 512, 8
NT = SEQ + NB
QT = SEQ // P
TILES = QT + 1
HALF = NT // 2
WA, WB, WC, HC, HD = 256, 256, 512, 8, 64
MT_A, MT_U, MT_V, MT_Q, MT_K, MT_VC = 0, 6, 8, 10, 14, 18
NM = 22
GROUPS = NM // 2
FIRST = MT_Q // 2
PAGE, PAGES = 128, 16
KEYS = 4
CHUNKS = PAGE // KEYS
CW = KEYS * WC
NE, NG, DE = 32, 4, 512
FC = DE // P
SLOTS = 64
PAIRS = 2 * NT
OVER = (PAIRS - NE) // SLOTS
LIST = 48
QMAX = NT // SLOTS
DP = 256
EPS = 1e-6
BIG = 1.0e30
SCALE = HD ** -0.5
ROOT_GUESS = 0x5F3759DF

assert NE + OVER < LIST and HALF * 2 == NT


def tile_width(t):
    return P if t < QT else NB


def tile_cols(t):
    return slice(t * P, t * P + tile_width(t))


FILLS = (["params"] + [f"x{t}{s}" for t in range(TILES) for s in "ab"]
         + ["f", "qs", "ks", "vs", "qb", "ws"] + [f"{n}{t}" for t in range(QT) for n in "kv"]
         + ["suffix", "ct", "newT"]
         + ["vn01", "vn23", "vn4", "vnT", "state", "z", "gate0", "gate1"] + [f"yc{t}" for t in range(QT)]
         + ["normA", "normB", "normC", "maxT", "maxB", "maxN", "sum"]
         + [f"h{t}{s}" for t in range(QT) for s in ("a", "b", "r")]
         + ["oN", "oT", "normS"]
         + [f"h{QT}{s}" for s in ("a", "b", "r")]
         + ["rank", "p01", "p23", "p4", "list"])
AT = {name: (n % 2, n // 2) for n, name in enumerate(FILLS)}


def build(nc, a, o):
    (y_prompt, y_sample, k_prompt, v_prompt, logf_prompt, conv_prompt,
     k_sample, v_sample, logf_sample, conv_sample, chunk_v_sample) = o
    h2_dram = nc.dram_tensor("h2_rows", [NT, D], F32, kind="Internal").ap()
    moe_dram = nc.dram_tensor("moe_rows", [PAIRS, D], F32, kind="Internal").ap()

    with ExitStack() as ctx:
        arena_size = 53024
        arena = ctx.enter_context(nc.sbuf_tensor("arena", [P, arena_size], F32))
        psum = ctx.enter_context(nc.psum_tensor("psum", [P, 8, BANK], F32))

        def ints(name, n):
            return ctx.enter_context(nc.sbuf_tensor(name, [P, n], I32))

        top = [0]

        def place(n):
            top[0] += n
            assert top[0] <= arena_size, top[0]
            return top[0] - n

        def at(start, *shape):
            n = 1
            for s in shape:
                n *= s
            flat = arena[:, start:start + n]
            if len(shape) == 1:
                return flat
            if len(shape) == 2:
                return flat.rearrange("p (a b) -> p a b", a=shape[0])
            return flat.rearrange("p (a b c) -> p a b c", a=shape[0], b=shape[1])

        region_a = place(MT_V * NT + DC * D)
        region_b = place(3 * DC * BANK)
        region_c = place(DC * NT + 2 * DC * 2 * P + 4 * NT + PAGE * HC)

        projT = at(region_a, NM, NT)
        cT = at(region_a + NM * NT, SEQ)
        w_out = at(region_a + MT_V * NT, DC, D)
        ring = [at(region_b + s * CW, CW) for s in range(4)]
        b_tail = region_b + 4 * CW
        s_buf = [at(b_tail + s * SEQ, SEQ) for s in range(2)]
        pT_buf = [at(b_tail + (2 + s) * SEQ, SEQ) for s in range(2)]
        k_nat = [at(b_tail + (4 + s) * SEQ, SEQ) for s in range(2)]
        ck_bc = [at(b_tail + (6 + s) * SEQ, SEQ) for s in range(2)]
        junk = at(b_tail, D)
        ws_nat = at(b_tail + 2 * SEQ, 4, P)
        w_forget = at(b_tail + 3 * SEQ, DC, HC)
        rms_bc = at(b_tail + 6 * SEQ, SEQ)
        root_y = at(b_tail + 7 * SEQ, SEQ)
        root_m = at(b_tail + 2 * SEQ, SEQ)
        w_ple_sb = at(b_tail, 2, D)
        hT = at(region_c, DC, NT)
        mixT = hT
        c1 = region_c + DC * NT
        w_ring = [at(c1 + s * DC * 2 * P, DC, 2 * P) for s in range(2)]
        c2 = c1 + 2 * DC * 2 * P
        v_nat = at(c2, QT, WC)
        squares = at(c2, 4, SEQ)
        squares_s = at(c2 + 4 * SEQ, 4, NB)
        c3 = c2 + 4 * NT
        scores = at(c3, PAGE * HC)

        p_emb = at(region_c, TILES, D)
        c4 = region_c + TILES * D
        h2T = [at(c4 + s * D, DC, P) for s in range(2)]
        h_rows = [at(c4 + s * D, D) for s in range(2)]
        hgT = [at(c4 + 2 * D + s * DC * SLOTS, DC, SLOTS) for s in range(2)]
        sig = [at(c4 + 3 * D + s * FC * SLOTS, FC * SLOTS) for s in range(2)]
        actT = [at(c4 + 3 * D + (2 + s) * FC * SLOTS, FC, SLOTS) for s in range(2)]
        y_rows = [at(c4 + 4 * D + s * D, D) for s in range(2)]
        assert c4 + 6 * D <= c3 + PAGE * HC
        p_nat = at(c4 + 4 * D, TILES, DP)
        pT = at(c4 + 2 * D, 2, NT)

        w_gu = [[at(r + m * DC * BANK, DC, DE) for m in range(2)] for r in (region_b, region_a)]
        w_dn = [at(r + 2 * DC * BANK, FC, D) for r in (region_b, region_a)]
        w_gate_ple = at(region_b, DC, D)
        g_fin = at(region_a + 8192, D)
        pairs_in = [at(region_a + s * 2 * D, 2 * D) for s in range(2)]
        ple_gate = [at(region_a + 4 * D + s * D, D) for s in range(2)]
        xT = [at(region_a + 6 * D + s * D, DC, P) for s in range(2)]

        x = at(place(TILES * D), TILES, D)
        xn0 = place(2 * D)
        xn = [at(xn0 + s * D, D) for s in range(2)]
        y_c = at(xn0, QT, WC)
        g_ffn_bc = at(place(D), D)
        ident = at(place(P), P)
        tri = at(place(SEQ), SEQ)
        ones = tri[:, P:2 * P]
        mask = at(place(P), P)
        strict = at(place(P), P)
        later = at(place(P), P)
        row_sel = at(place(P), P)
        col_sel = at(place(NB), NB)
        roots = at(place(2 * NB), 2, NB)
        params = at(place(30), 30)
        stats = at(place(64), 64)
        small0 = place(7120)
        small_top = [small0]

        def small(*shape):
            n = 1
            for s in shape:
                n *= s
            small_top[0] += n
            assert small_top[0] <= small0 + 7120, small_top[0] - small0
            return at(small_top[0] - n, *shape)

        params_nat = small(P)
        logf_pages = small(PAGE, HC)
        decay = small(PAGE, HC)
        f_nat = small(TILES, HC)
        f_a, f_b, f_c, f_d = (small(TILES, HC) for _ in range(4))
        q_s, k_s, v_s, prod_s = (small(WC) for _ in range(4))
        q_bc = small(WC)
        wsT = small(4, P)
        bs_bc = small(2, P)
        v_norm = at(c2 - TILES * WB, TILES, WB)
        ln_g_bc, ln_b_bc = small(WB), small(WB)
        bf_bc = small(HC)
        w00 = small(2)
        state = small(2 * WA)
        z_p, z_s = q_bc[:, 0:WA], q_bc[:, WA:2 * WA]
        new_s, newT_s, mT, pnew, m_nat, sum_s = (small(HC) for _ in range(6))
        m_exp = small(P)
        max_p, max_b, sum_p = (small(HC) for _ in range(3))
        page_suf = small(HC)
        oT = small(4, NB)
        vnT = small(2, NB)
        gate_s = small(2, NB)
        conv_tmp = small(2, NB)
        bn = small(6)
        mv = small(2)
        p_exp = [at(b_tail + 4 * SEQ + s * KEYS * HC * NB, KEYS * HC, NB) for s in range(4)]
        fT = at(b_tail + 4 * SEQ, NT)
        small_top[0] = small0
        logits = small(TILES, NG + NE)
        eg = small(TILES, NG)
        gcand = small(TILES, NG)
        g_one = small(TILES, NG)
        masked = small(TILES, NE)
        m2 = small(TILES, NE)
        cand = small(TILES, NE)
        e_one = [small(TILES, NE) for _ in range(2)]
        chosen = small(TILES, NE)
        prod_r = small(TILES, NE)
        rank = small(TILES, NE)
        count = small(NE)
        cmp8 = small(NE, QMAX)
        tiles_over, over_end, over_base = small(NE), small(NE), small(NE)
        r5 = [small(TILES) for _ in range(12)]
        e_idx = [small(TILES) for _ in range(2)]
        cmp5 = small(TILES, QMAX)
        slot_one = small(2, TILES, SLOTS)
        tile_one = small(TILES, 2 * LIST)
        tile_one2 = small(TILES, 2 * LIST)
        list_f = small(2 * LIST)
        cmp_over = small(OVER, NE)
        over_f = small(OVER + 1)
        routing_end = small_top[0]
        w_keep = [at(place(TILES), TILES) for _ in range(2)]
        iota = at(place(SLOTS), SLOTS)
        tokid = at(place(TILES), TILES)
        steps = at(place(QMAX), QMAX)
        valid = at(place(TILES), TILES)
        b_route = at(place(NG + NE), NG + NE)
        w_route = at(place(DC * (NG + NE)), DC, NG + NE)
        page_f = at(place(1), 1)
        chunk_f = at(place(4), 4)
        page_id = ints("page_id", 1)
        chunk_id = [ints(f"chunk_id{s}", 1) for s in range(4)]
        tok_list, pair_list = ints("tok_list", LIST), ints("pair_list", LIST)
        tok_ix = [ints(f"tok_ix{s}", 1) for s in range(2)]
        pair_ix = [ints(f"pair_ix{s}", 1) for s in range(2)]
        over_i = ints("over_i", OVER + 1)

        def sem(name):
            return ctx.enter_context(nc.semaphore(name))

        x_in = [sem(f"x_in{t}") for t in range(TILES)]
        rows_in, consts_in, wf_in, lf_in, page_in = (sem(n) for n in ("rows_in", "consts_in", "wf_in", "lf_in", "page_in"))
        route_w_in = sem("route_w_in")
        pool_step, act_step, dve_step = sem("pool_step"), sem("act_step"), sem("dve_step")
        consts_built = sem("consts_built")
        full = [sem("fill_ready0"), sem("fill_ready1")]
        free = [sem("fill_read0"), sem("fill_read1")]
        ms_ready, xn_ready, xn_used = sem("ms_ready"), sem("xn_ready"), sem("xn_used")
        f_full, f_free = sem("f_full"), sem("f_free")
        w_in_s = [sem("w_group_in0"), sem("w_group_in1")]
        pj_full, pj_free = sem("proj_ready"), sem("proj_copied")
        kn_out, vn_ready = [sem("k_nat_stored0"), sem("k_nat_stored1")], sem("v_nat_ready")
        sample_nat = sem("sample_nat_ready")
        qb_ready = sem("q_bc_ready")
        logf_ready = sem("logf_ready")
        f_part = sem("f_part")
        kv_in = [sem(f"cache_in{s}") for s in range(4)]
        kmul, kred = sem("k_products"), sem("k_reduced")
        suf_ready = sem("suffix_parts_ready")
        ct_ready = sem("cT_ready")
        ck_full, ck_ready = sem("ck_full"), sem("ck_bc_ready")
        a_s, a_read, a_m, a_p, a_t, a_pt, a_o, a_of = (sem("att_" + n) for n in (
            "scores", "scores_read", "max", "probs", "probsT", "probsT_copied", "out", "out_copied"))
        v_ready = sem("v_norm_ready")
        z_ready = sem("z_ready")
        z_nat = sem("z_nat_ready")
        mix_ready = sem("mix_ready")
        sq_ready = sem("squares_ready")
        w_o_in = sem("w_o_in")
        wo_full, wo_free = sem("wo_full"), sem("wo_added")
        x1_ms, h2_ready, h2T_ready = sem("x1_ms"), sem("h2_ready"), sem("h2T_ready")
        h2_stored = [sem("h2_stored0"), sem("h2_stored1")]
        mix_normed, mixs_normed, new_ready = sem("mix_normed"), sem("mix_sample_normed"), sem("new_score_ready")
        smp_req, smp_exp, smp_p = sem("sample_operand"), sem("sample_exp_in"), sem("sample_exp_out")
        px_ready, pv_done, pv_read = sem("p_expanded"), sem("pv_done"), sem("pv_read")
        mixs_ready = sem("mix_sample_ready")
        route_op, route_exp_in, route_exp_out = sem("route_operand"), sem("route_exp_in"), sem("route_exp_out")
        lists_ready = sem("lists_ready")
        ple_in, pT_ready, pe_full, pe_free = sem("ple_in"), sem("pT_ready"), sem("p_emb_full"), sem("p_emb_copied")
        hg_in, y_out = [sem("rows_in0"), sem("rows_in1")], [sem("y_out0"), sem("y_out1")]
        gu_in = [[sem(f"w_{m}{s}_in") for m in ("gate", "up")] for s in range(2)]
        dn_in = [sem("w_down0_in"), sem("w_down1_in")]
        hgT_full, hgT_ready, gu_full, sig_ready, act_ready, y_full, y_left = (sem("moe_" + n) for n in (
            "rowsT_full", "rowsT_ready", "gate_up", "sigmoid", "act", "y_full", "y_left"))
        ov_m = sem("over_gated")
        moe_done, y_taken, y_right = sem("moe_done"), sem("y_taken"), sem("moe_y_right")
        ov_w, ov_rows, ov_T, ov_Tc, ov_gu, ov_sig, ov_act, ov_y, ov_yc, ov_out = (sem("over_" + n) for n in (
            "weights_in", "rows_in", "rowsT", "rowsT_ready", "gate_up", "sigmoid", "act", "y", "y_ready", "stored"))
        wpg_in, gfin_in, pairs_ready = sem("w_ple_gate_in"), sem("g_final_in"), [sem("pairs_in0"), sem("pairs_in1")]
        x2_ms, x3_ready, xT_full, xT_ready, pg_full, pg_sig, pg_free, x4_ms, y_final = (sem("post_" + n) for n in (
            "x2_ms", "xn", "xT_full", "xT", "gate_full", "gate_sigmoid", "gate_free", "x4_ms", "y"))
        x2_ready, x4_ready = sem("post_x2"), sem("post_x4")
        y_stored, out_act = [sem("y_stored0"), sem("y_stored1")], sem("stored_by_scalar")

        passed = sem("passed")

        block = ctx.enter_context(nc.Block())

        def bank(b):
            return psum[:, b, :]

        def fill(name):
            return bank(4 + AT[name][0])

        def wait_full(eng, name):
            b, n = AT[name]
            eng.wait_ge(full[b], n + 1)

        def free_of(name):
            return free[AT[name][0]]

        def wait_free(eng, name):
            b, n = AT[name]
            if n:
                eng.wait_ge(free[b], n)

        def alone(eng):
            eng.nop().then_inc(passed, 1)

        class Steps:

            def __init__(self, eng, semaphore):
                self.eng, self.sem, self.n, self.off = eng, semaphore, 0, 0

            def __call__(self, ins):
                self.n += 1
                ins.then_inc(self.sem, 1)
                self.eng.wait_ge(self.sem, self.n + self.off)
                if not isinstance(self.off, int):
                    alone(self.eng)

        def inner(ap, n):
            return ap.rearrange("p (a o) -> p a o", o=1).to_broadcast([ap.shape[0], ap.shape[1], n])

        def outer(ap, n):
            return ap.rearrange("p (o a) -> p o a", o=1).to_broadcast([ap.shape[0], n, ap.shape[1]])

        def bc_rows(src, n=P):
            return src.to_broadcast([n, src.shape[-1]])

        def finish_gate(act, t):
            w = tile_width(t)
            act.wait_ge(pg_full, t + 1)
            act.activation(ple_gate[t % 2][0:w, :].rearrange("p (a n) -> p a n", a=2), psum[0:w, 2 * (t % 2):2 * (t % 2) + 2, :],
                           ACT.Sigmoid).then_inc(pg_sig, 1)
            act.wait_ge(x4_ready, t + 1)
            act.activation(xn[t % 2][0:w, :], x[0:w, t, :], ACT.Square, accum_out=stats[0:w, 48 + t:49 + t]).then_inc(x4_ms, 1)

        @block.sync
        def _(sp):
            for t in range(QT):
                sp.dma_start(x[:, t, :], a["x_prompt"][0, t * P:(t + 1) * P, :]).then_inc(x_in[t], 16)
            sp.dma_start(x[0:NB, QT, :], a["x_sample"].rearrange("b l d -> (b l) d")).then_inc(x_in[QT], 16)
            w_in_v = a["w_in"][0].rearrange("(k p) n -> p k n", p=P)

            def w_group(n, slot):
                return w_ring[slot]

            def load_group(g, slot):
                sp.dma_start(w_ring[slot], w_in_v[:, :, bass.ds(g * (2 * P), 2 * P)]).then_inc(w_in_s[slot], 16)

            load_group(FIRST, 0)
            load_group(FIRST + 1, 1)
            with sp.Fori(1, (GROUPS - FIRST) // 2) as i:
                for s in range(2):
                    sp.wait_ge(pj_full, i * 4 + (2 * s - 2))
                    load_group(i * 2 + (FIRST + s), s)
            done = GROUPS - FIRST
            with sp.Fori(0, (GROUPS - done) // 2) as i:
                for s in range(2):
                    sp.wait_ge(pj_full, i * 4 + (2 * (done + s) - 2))
                    load_group(i * 2 + s, s)
            sp.wait_ge(pj_full, 2 * (GROUPS - 1) - 2)
            load_group(GROUPS - done - 1, 0)
            sp.wait_ge(a_o, 4 * HC)
            sp.wait_ge(full[AT["vnT"][0]], AT["vnT"][1] + 1)
            sp.dma_start(w_out, a["w_o"][0].rearrange("(k p) n -> p k n", p=P)).then_inc(w_o_in, 16)
            wg, wu, wd = (a[n][0].rearrange("g e d f -> (g e) d f") for n in ("w_gate", "w_up", "w_down"))

            def load_expert(e, s):
                sp.dma_start(w_gu[s][0], wg[bass.ds(e, 1)].rearrange("o (p k) f -> p (o k) f", k=DC)).then_inc(gu_in[s][0], 16)
                sp.dma_start(w_gu[s][1], wu[bass.ds(e, 1)].rearrange("o (p k) f -> p (o k) f", k=DC)).then_inc(gu_in[s][1], 16)

            def load_down(e, s):
                sp.dma_start(w_dn[s], wd[bass.ds(e, 1)].rearrange("o (k p) n -> p (o k) n", p=P)).then_inc(dn_in[s], 16)

            sp.wait_ge(pv_done, CHUNKS)
            load_expert(0, 0)
            sp.wait_ge(wo_full, TILES)
            load_expert(1, 1)
            load_down(1, 1)
            sp.wait_ge(pe_full, TILES)
            load_down(0, 0)
            with sp.Fori(1, NE // 2) as i:
                for s in range(2):
                    sp.wait_ge(gu_full, i * 2 + (s - 1))
                    load_expert(i * 2 + s, s)
                    sp.wait_ge(y_full, i * 2 + (s - 1))
                    load_down(i * 2 + s, s)
            sp.wait_ge(lists_ready, 1)
            sp.wait_ge(y_full, NE)
            n_over = sp.value_load(over_i[0:1, OVER:OVER + 1], min_val=0, max_val=OVER)
            with sp.If(n_over > 0):
                with sp.Fori(0, n_over) as i:
                    e = sp.value_load(over_i[0:1, bass.ds(i, 1)], min_val=0, max_val=NE - 1)
                    sp.wait_ge(ov_y, i + 1)
                    sp.dma_start(w_gu[0][0], wg[bass.ds(e, 1)].rearrange("o (p k) f -> p (o k) f", k=DC)).then_inc(ov_w, 16)
                    sp.dma_start(w_gu[0][1], wu[bass.ds(e, 1)].rearrange("o (p k) f -> p (o k) f", k=DC)).then_inc(ov_w, 16)
                    sp.dma_start(w_dn[0], wd[bass.ds(e, 1)].rearrange("o (k p) n -> p (o k) n", p=P)).then_inc(ov_w, 16)
            with sp.Else():
                sp.nop()
            sp.wait_ge(moe_done, 1)
            sp.dma_start(w_gate_ple, a["w_ple_gate"][0].rearrange("(k p) n -> p k n", p=P)).then_inc(wpg_in, 16)
            sp.dma_start(g_fin, bc_rows(a["g_final"].rearrange("(a n) -> a n", a=1))).then_inc(gfin_in, 16)
            for t in range(TILES):
                w = tile_width(t)
                if t >= 2:
                    sp.wait_ge(x2_ready, t - 1)
                rows = moe_dram[2 * t * P:2 * (t * P + w), :].rearrange("(p k) d -> p (k d)", k=2)
                sp.dma_start(pairs_in[t % 2][0:w, :], rows).then_inc(pairs_ready[t % 2], 16)
            for t in range(TILES):
                w = tile_width(t)
                sp.wait_ge(y_final, t + 1)
                dst = y_prompt[0, t * P:(t + 1) * P, :] if t < QT else y_sample.rearrange("b l d -> (b l) d")
                sp.dma_start(dst, xn[t % 2][0:w, :]).then_inc(y_stored[t % 2], 16)
            sp.wait_ge(y_stored[0], 48)
            sp.wait_ge(y_stored[1], 32)

        @block.gpsimd
        def _(pool):
            step = Steps(pool, pool_step)
            pool.dma_start(page_id[:, :], a["page_table"].rearrange("b (g o) -> (b g) o", o=1)).then_inc(page_in, 16)

            def select(out, op, fill_value, base, pattern, mult):
                step(pool.affine_select(out=out, in_=out, compare_op=op, fill=fill_value, base=base,
                                        pattern=pattern, channel_multiplier=mult))

            step(pool.memset(ident, 0.0))
            select(ident, ALU.not_equal, 1.0, 0, [[-1, P]], 1)
            step(pool.memset(tri, 1.0))
            select(tri, ALU.is_ge, 0.0, 0, [[1, SEQ]], -1)
            pool.nop().then_inc(consts_built, 1)
            pool.wait_ge(page_in, 16)
            pool.indirect_dma_start(logf_pages.rearrange("p k h -> p (k h)"), None,
                                    a["cache_logf"][0].rearrange("n k h -> n (k h)"),
                                    bass.IndirectOffsetOnAxis(ap=page_id[:, 0:1], axis=0)).then_inc(lf_in, 16)
            step(pool.tensor_copy(page_f, page_id[:, 0:1]))
            for s in range(4):
                step(pool.tensor_scalar(chunk_f[:, s:s + 1], page_f, float(CHUNKS), float(s), ALU.mult, ALU.add))
            caches = [a[n][0].rearrange("n (c k) h d -> (n c) (k h d)", k=KEYS) for n in ("cache_k", "cache_v")]

            def load_chunk(cache, s):
                step(pool.tensor_copy(chunk_id[s][:, 0:1], chunk_f[:, s:s + 1]))
                pool.indirect_dma_start(ring[s], None, caches[cache],
                                        bass.IndirectOffsetOnAxis(ap=chunk_id[s][:, 0:1], axis=0)).then_inc(kv_in[s], 16)
                step(pool.tensor_scalar(chunk_f[:, s:s + 1], chunk_f[:, s:s + 1], 4.0, None, ALU.add))

            for s in range(3):
                load_chunk(0, s)
            step(pool.memset(mask, 0.0))
            select(mask, ALU.is_ge, -BIG, 0, [[-1, P]], 1)
            step(pool.memset(strict, 1.0))
            select(strict, ALU.is_ge, 0.0, -1, [[1, P]], -1)
            lat = later.rearrange("p (b g) -> p b g", b=NB)
            step(pool.memset(later, 1.0))
            select(lat, ALU.is_ge, 0.0, -1, [[-PAGES, NB], [-1, PAGES]], 1)
            select(lat, ALU.is_ge, 0.0, PAGES - 1, [[PAGES, NB], [0, PAGES]], -1)
            rs = row_sel[0:NB, :].rearrange("p (b g) -> p b g", b=NB)
            step(pool.memset(row_sel, 0.0))
            select(rs, ALU.not_equal, 1.0, 0, [[-1, NB], [0, PAGES]], 1)
            step(pool.memset(col_sel, 1.0))
            select(col_sel, ALU.is_ge, 0.0, 0, [[-PAGES, NB]], 1)
            select(col_sel, ALU.is_ge, 0.0, PAGES - 1, [[PAGES, NB]], -1)
            step(pool.iota(iota, pattern=[[1, SLOTS]], base=0, channel_multiplier=0, allow_small_or_imprecise_dtypes=True))
            step(pool.iota(tokid, pattern=[[P, TILES]], base=0, channel_multiplier=1, allow_small_or_imprecise_dtypes=True))
            step(pool.iota(steps, pattern=[[SLOTS, QMAX]], base=SLOTS, channel_multiplier=0, allow_small_or_imprecise_dtypes=True))
            step(pool.memset(valid, 1.0))
            select(valid[:, QT:TILES], ALU.is_ge, 0.0, NB - 1, [[0, 1]], -1)
            pool.nop().then_inc(consts_built, 1)

            pool.wait_ge(qb_ready, 1)
            q_rep = q_bc.rearrange("p (o n) -> p o n", o=1).to_broadcast([P, KEYS, WC])

            def products(s, count):
                pool.wait_ge(kv_in[s], count)
                r = ring[s].rearrange("p (k n) -> p k n", k=KEYS)
                pool.tensor_tensor(r, r, q_rep, ALU.mult).then_inc(kmul, 1)

            base = step.n
            per = 8
            with pool.Fori(0, CHUNKS // 4 - 1) as i:
                step.off = i * per
                for s in range(4):
                    products(s, i * 16 + 16)
                    pool.wait_ge(kred, i * 4 + (s + 1))
                    alone(pool)
                    load_chunk(0, (s + 3) % 4)
            assert step.n == base + per
            step.n, step.off = base + per * (CHUNKS // 4 - 1), 0
            for s in range(4):
                products(s, 16 * (CHUNKS // 4))
                pool.wait_ge(kred, CHUNKS - 4 + s + 1)
                if s == 0:
                    load_chunk(0, 3)
                    for r in range(4):
                        step(pool.tensor_scalar(chunk_f[:, r:r + 1], page_f, float(CHUNKS), float(r), ALU.mult, ALU.add))
                else:
                    load_chunk(1, s - 1)
            pool.wait_ge(kred, CHUNKS + 1)
            load_chunk(1, 3)
            base = step.n
            with pool.Fori(1, CHUNKS // 4) as i:
                step.off = (i - 1) * per
                for s in range(4):
                    pool.wait_ge(pv_done, i * 4 + (s - 3))
                    alone(pool)
                    load_chunk(1, s)
            step.n, step.off = base + per * (CHUNKS // 4 - 1), 0

            pool.wait_ge(lists_ready, 1)
            pool.wait_ge(h2_stored[0], 48)
            pool.wait_ge(h2_stored[1], 32)
            pool.wait_ge(pe_full, TILES)

            def gather(e, s):
                step(pool.tensor_copy(tok_ix[s][0:SLOTS, 0:1], tok_list[0:SLOTS, bass.ds(e, 1)]))
                pool.indirect_dma_start(h_rows[s][0:SLOTS, :], None, h2_dram,
                                        bass.IndirectOffsetOnAxis(ap=tok_ix[s][0:SLOTS, 0:1], axis=0)).then_inc(hg_in[s], 16)

            def scatter(e, s):
                step(pool.tensor_copy(pair_ix[s][0:SLOTS, 0:1], pair_list[0:SLOTS, bass.ds(e, 1)]))
                return pool.indirect_dma_start(moe_dram, bass.IndirectOffsetOnAxis(ap=pair_ix[s][0:SLOTS, 0:1], axis=0),
                                               y_rows[s][0:SLOTS, :], None, bounds_check=PAIRS - 1, oob_is_err=False)

            def store(e, s, ready, stored):
                pool.wait_ge(y_left, ready)
                pool.wait_ge(y_right, ready)
                if not isinstance(ready, int):
                    alone(pool)
                scatter(e, s).then_inc(y_out[s], 16)
                pool.wait_ge(y_out[s], stored)
                pool.nop().then_inc(y_taken, 1)

            gather(0, 0)
            gather(1, 1)
            base = step.n
            with pool.Fori(1, NE // 2) as i:
                step.off = (i - 1) * 4
                for s in (1, 0):
                    pool.wait_ge(hgT_full, i * 2 - s)
                    alone(pool)
                    gather(i * 2 + (1 - s), 1 - s)
                    store(i * 2 - (s + 1), 1 - s, i * 2 - s, i * 16)
            step.n, step.off = base + 4 * (NE // 2 - 1), 0
            for s in range(2):
                store(NE - 2 + s, s, NE - 1 + s, 8 * NE)
            n_over = pool.value_load(over_i[0:1, OVER:OVER + 1], min_val=0, max_val=OVER)
            with pool.If(n_over > 0):
                base = step.n
                with pool.Fori(0, n_over) as i:
                    step.off = i * 2
                    step(pool.tensor_copy(tok_ix[0][0:SLOTS, 0:1], tok_list[0:SLOTS, bass.ds(i + NE, 1)]))
                    pool.indirect_dma_start(h_rows[0][0:SLOTS, :], None, h2_dram,
                                            bass.IndirectOffsetOnAxis(ap=tok_ix[0][0:SLOTS, 0:1], axis=0)).then_inc(ov_rows, 16)
                    pool.wait_ge(ov_yc, i * 2 + 2)
                    alone(pool)
                    scatter(i + NE, 0).then_inc(ov_out, 16)
                    pool.wait_ge(ov_out, i * 16 + 16)
                step.off = 0
            with pool.Else():
                pool.nop()
            pool.nop().then_inc(moe_done, 1)

        @block.scalar
        def _(act):
            step = Steps(act, act_step)
            for n, (name, rows) in enumerate((("g_mix", 8), ("g_out", 8))):
                act.dma_start(params_nat[8 * n:8 * n + rows, :], a[name][0].rearrange("(c p) -> c p", p=P)).then_inc(rows_in, 16)
            act.dma_start(params_nat[16:22, :], a["conv_w"][0].rearrange("j (c p) -> (j c) p", p=P)).then_inc(rows_in, 16)
            act.dma_start(params_nat[22:30, :], a["g_ple"][0].rearrange("(c p) -> c p", p=P)).then_inc(rows_in, 16)
            w_f = a["w_in"][0].rearrange("(k p) n -> p k n", p=P)[:, :, NM * P:NM * P + HC]
            act.dma_start(w_forget, w_f).then_inc(wf_in, 16)

            def square(t, m):
                w = tile_width(t)
                act.wait_ge(x_in[t], 16)
                act.activation(junk[0:w, :], x[0:w, t, :], ACT.Square, accum_out=stats[0:w, t:t + 1]).then_inc(ms_ready, 1)

            n_consts = [0]

            def const(dst, src):
                n_consts[0] += 1
                act.dma_start(dst, src).then_inc(consts_in, 16)

            const(ws_nat, a["w_s"][0].rearrange("h t s -> t h s"))
            const(bf_bc, bc_rows(a["b_f"]))
            const(ln_g_bc, bc_rows(a["ln_g"]))
            const(ln_b_bc, bc_rows(a["ln_b"]))
            for h in range(4):
                q = (h % 2) * HD
                const(bs_bc[q:q + HD, h // 2, :], bc_rows(a["b_s"][0, h:h + 1, :], HD))
                const(w00[q:q + HD, h // 2:h // 2 + 1], bc_rows(a["w_s"][0, h, 0:1, 0:1], HD))
            const(state[0:NB, :], a["state_conv"][0].rearrange("b j c -> b (j c)"))
            const(b_route[:, 0:NG], bc_rows(a["b_grp"]))
            const(b_route[:, NG:], bc_rows(a["b_rt"].rearrange("l g e -> l (g e)")))
            const(g_ffn_bc, bc_rows(a["g_ffn"]))
            act.dma_start(w_route[:, :, 0:NG], a["w_grp"][0].rearrange("(k p) n -> p k n", p=P)).then_inc(route_w_in, 16)
            act.dma_start(w_route[:, :, NG:], a["w_rt"][0].rearrange("(k p) g e -> p k (g e)", p=P)).then_inc(route_w_in, 16)
            for t in range(TILES):
                if t:
                    act.wait_ge(ms_ready, t)
                square(t, 0)
            act.wait_ge(f_full, 1)
            act.activation(fT[0:HC, :].rearrange("p (a n) -> p a n", a=2), psum[0:HC, 2:4, 0:HALF], ACT.Copy).then_inc(f_free, 1)

            def copy_proj(m, parity, ready):
                act.wait_ge(pj_full, ready)
                dst = projT[:, bass.ds(m, 1), :].rearrange("p o (a n) -> p (o a) n", a=2)
                act.activation(dst, psum[:, 2 * parity:2 * parity + 2, 0:HALF], ACT.Copy).then_inc(pj_free, 1)

            with act.Fori(0, (GROUPS - FIRST) // 2) as i:
                for q in range(4):
                    copy_proj(i * 4 + (MT_Q + q), q % 2, i * 4 + (q + 1))
            wait_full(act, "qs")
            act.activation(q_s[0:NB, :], fill("qs")[0:NB, :], ACT.Copy, scale=SCALE).then_inc(free_of("qs"), 1)
            wait_full(act, "ks")
            act.activation(k_s[0:NB, :], fill("ks")[0:NB, :], ACT.Copy).then_inc(free_of("ks"), 1)
            wait_full(act, "vs")
            act.activation(v_s[0:NB, :], fill("vs")[0:NB, :], ACT.Copy).then_inc(free_of("vs"), 1)
            wait_full(act, "qb")
            act.activation(q_bc, fill("qb"), ACT.Copy).then_inc(free_of("qb"), 1)
            act.wait_ge(free_of("qb"), AT["qb"][1] + 1)
            step(act.activation(stats[0:1, 40:41], stats[0:1, 0:1], ACT.Copy))
            act.nop().then_inc(qb_ready, 1)
            act.wait_ge(free_of("ks"), AT["ks"][1] + 1)
            act.wait_ge(free_of("vs"), AT["vs"][1] + 1)
            act.nop().then_inc(sample_nat, 1)
            flat = "l b t h d -> (l b t) (h d)"
            act.dma_start(k_sample.rearrange(flat), k_s[0:NB, :]).then_inc(out_act, 16)
            act.dma_start(v_sample.rearrange(flat), v_s[0:NB, :]).then_inc(out_act, 16)
            stored = [2]
            act.wait_ge(f_part, 1)
            act.activation(f_b, f_a, ACT.Exp, scale=-1.0).then_inc(f_part, 1)
            act.wait_ge(f_part, 3)
            act.activation(f_d, f_c, ACT.Ln).then_inc(f_part, 1)
            for t in range(QT):
                wait_full(act, f"k{t}")
                if t >= 2:
                    act.wait_ge(kn_out[t % 2], 16)
                act.activation(k_nat[t % 2], fill(f"k{t}"), ACT.Copy).then_inc(free_of(f"k{t}"), 1)
                act.wait_ge(free_of(f"k{t}"), AT[f"k{t}"][1] + 1)
                rows = slice(t * P, (t + 1) * P)
                act.dma_start(k_prompt[0, 0, rows].rearrange("t h d -> t (h d)"), k_nat[t % 2]).then_inc(kn_out[t % 2], 16)
            for t in range(QT):
                act.wait_ge(vn_ready, t + 1)
                act.dma_start(v_prompt[0, 0, t * P:(t + 1) * P].rearrange("t h d -> t (h d)"), v_nat[:, t, :]).then_inc(out_act, 16)
                stored[0] += 1
            act.wait_ge(logf_ready, 1)
            act.dma_start(logf_prompt[0, 0].rearrange("(t p) h -> p t h", p=P), f_nat[:, 0:QT, :]).then_inc(out_act, 16)
            act.dma_start(logf_sample.rearrange("l b t h -> (l b t) h"), f_nat[0:NB, QT, :]).then_inc(out_act, 16)
            stored[0] += 2
            wait_full(act, "ct")
            act.activation(cT[0:HC, :], fill("ct")[0:HC, :], ACT.Copy).then_inc(free_of("ct"), 1)
            act.wait_ge(free_of("ct"), AT["ct"][1] + 1)
            act.nop().then_inc(ct_ready, 1)
            for s in range(2):
                act.wait_ge(kn_out[s], 16 * (QT // 2))

            def copy_ck(h):
                act.wait_ge(ck_full, h + 1)
                if h >= 2:
                    act.wait_ge(a_read, 4 * (h - 1))
                act.activation(ck_bc[h % 2], bank(7), ACT.Copy).then_inc(ck_ready, 1)

            copy_ck(0)
            units = 4 * HC
            for u in range(units + 1):
                if u < units:
                    nk = P * (u % QT + 1)
                    act.wait_ge(a_m, u + 1)
                    act.activation(s_buf[u % 2][:, 0:nk], s_buf[u % 2][:, 0:nk], ACT.Exp, bias=stats[:, 8 + u % 2:9 + u % 2],
                                   accum_out=stats[:, 16 + u % 4:17 + u % 4]).then_inc(a_p, 1)
                if u >= 1:
                    w = u - 1
                    nk = P * (w % QT + 1)
                    act.wait_ge(a_t, w + 1)
                    if w >= 2:
                        act.wait_ge(a_o, w - 1)
                    act.activation(pT_buf[w % 2][:, 0:nk], bank(2 + w % 2)[:, 0:nk], ACT.Copy).then_inc(a_pt, 1)
                if u % QT == 2 and u // QT + 1 < HC:
                    copy_ck(u // QT + 1)

            with act.Fori(0, (FIRST - 1) // 2) as i:
                for q in range(4):
                    copy_proj(i * 4 + q, q % 2, i * 4 + (2 * (GROUPS - FIRST) + q + 1))
            for q in range(2):
                copy_proj(MT_V + q, q, NM - 1 + q)
            wait_full(act, "z")
            step(act.activation(z_p[0:2, :], fill("z")[0:2, 0:WA], ACT.Copy))
            act.activation(z_s[0:NB, :], fill("z")[0:NB, WA:2 * WA], ACT.Copy).then_inc(free_of("z"), 1)
            act.wait_ge(free_of("z"), AT["z"][1] + 1)
            act.dma_start(conv_prompt[0, 0], z_p[0:2, :]).then_inc(out_act, 16)
            act.dma_start(conv_sample[0, :, 0, :], state[0:NB, WA:2 * WA]).then_inc(out_act, 16)
            act.dma_start(conv_sample[0, :, 1, :], z_s[0:NB, :]).then_inc(out_act, 16)
            act.wait_ge(v_ready, TILES)
            act.dma_start(chunk_v_sample.rearrange("l b t c -> (l b t) c"), v_norm[0:NB, QT, :]).then_inc(out_act, 16)
            stored[0] += 4
            for t in range(QT):
                wait_full(act, f"yc{t}")
                act.activation(mixT[:, 4:8, t * P:(t + 1) * P], fill(f"yc{t}").rearrange("p (c n) -> p c n", c=4),
                               ACT.Copy).then_inc(free_of(f"yc{t}"), 1)
            act.wait_ge(mix_ready, 2)
            act.wait_ge(out_act, 16 * stored[0])
            act.activation(squares, mixT[:, 0:4, 0:SEQ], ACT.Square).then_inc(sq_ready, 1)
            wait_full(act, "normB")
            for t in range(QT):
                act.wait_ge(free_of(f"yc{t}"), AT[f"yc{t}"][1] + 1)
            act.activation(squares, mixT[:, 4:8, 0:SEQ], ACT.Square).then_inc(sq_ready, 1)

            act.wait_ge(smp_exp, 1)
            act.activation(scores, scores, ACT.Exp).then_inc(smp_p, 1)
            act.wait_ge(smp_exp, 2)
            act.activation(pnew[0:NB, :], new_s[0:NB, :], ACT.Exp).then_inc(smp_p, 1)
            act.dma_start(w_ple_sb, a["w_ple"][0].rearrange("(k p) n -> p k n", p=P)).then_inc(ple_in, 16)

            def second_norm(t):
                w = tile_width(t)
                act.wait_ge(wo_free, t + 1)
                act.activation(xn[t % 2][0:w, :], x[0:w, t, :], ACT.Square, accum_out=stats[0:w, 24 + t:25 + t]).then_inc(x1_ms, 1)
                act.wait_ge(h2_ready, t + 1)
                act.dma_start(h2_dram[tile_cols(t), :], xn[t % 2][0:w, :]).then_inc(h2_stored[t % 2], 16)
                for s, half in enumerate("ab"):
                    wait_full(act, f"h{t}{half}")
                    if s == 0 and t >= 2:
                        wait_full(act, f"h{t - 2}r")
                    act.activation(h2T[t % 2][:, 4 * s:4 * s + 4, 0:w],
                                   fill(f"h{t}{half}").rearrange("p (c n) -> p c n", c=4)[:, :, 0:w], ACT.Copy)\
                       .then_inc(free_of(f"h{t}{half}"), 1)
                act.wait_ge(free_of(f"h{t}b"), AT[f"h{t}b"][1] + 1)
                act.wait_ge(free_of(f"h{t}a"), AT[f"h{t}a"][1] + 1)
                act.nop().then_inc(h2T_ready, 1)

            act.wait_ge(out_act, 16 * stored[0])
            for t in range(QT):
                if t >= 2:
                    act.wait_ge(h2_stored[t % 2], 16)
                second_norm(t)
            act.wait_ge(mixs_ready, 1)
            step(act.activation(squares_s, mixT[:, 0:4, SEQ:NT], ACT.Square))
            step(act.activation(squares[:, 0, 0:4 * NB].rearrange("p (c n) -> p c n", c=4), mixT[:, 4:8, SEQ:NT], ACT.Square))
            act.nop().then_inc(sq_ready, 1)
            act.wait_ge(h2_stored[0], 32)
            second_norm(QT)
            act.wait_ge(px_ready, CHUNKS)
            act.wait_ge(pv_done, CHUNKS)
            act.dma_start(p_nat[:, 0:QT, :], a["p_prompt"][0, 0].rearrange("(t p) n -> p t n", p=P)).then_inc(ple_in, 16)
            act.dma_start(p_nat[0:NB, QT, :], a["p_sample"][0].rearrange("b l n -> (b l) n")).then_inc(ple_in, 16)
            act.wait_ge(route_exp_in, 1)
            act.activation(eg, eg, ACT.Exp).then_inc(route_exp_out, 1)
            act.wait_ge(route_exp_in, 2)
            act.activation(r5[4], r5[4], ACT.Exp).then_inc(route_exp_out, 1)
            for name, t0, n in (("p01", 0, 2), ("p23", 2, 2), ("p4", 4, 1)):
                wait_full(act, name)
                w = n * P if n == 2 else NB
                act.activation(pT[:, :, t0 * P:t0 * P + w], fill(name).rearrange("p (k n) -> p k n", k=2)[:, :, 0:w],
                               ACT.Copy).then_inc(free_of(name), 1)
            for name in ("p23", "p4"):
                act.wait_ge(free_of(name), AT[name][1] + 1)
            act.nop().then_inc(pT_ready, 1)
            for t in range(TILES):
                w = tile_width(t)
                act.wait_ge(pe_full, t + 1)
                pair = psum[0:w, 2 * (t % 2):2 * (t % 2) + 2, :]
                act.activation(p_emb[0:w, t, :].rearrange("p (a n) -> p a n", a=2), pair, ACT.Copy).then_inc(pe_free, 1)

            def copy_rows(s, ready):
                act.wait_ge(hgT_full, ready)
                act.activation(hgT[s].rearrange("p k n -> p (k n)"), bank(4), ACT.Copy).then_inc(hgT_ready, 1)

            def sigmoid(s, ready):
                act.wait_ge(gu_full, ready)
                act.activation(sig[s], psum[:, s, 0:FC * SLOTS], ACT.Sigmoid).then_inc(sig_ready, 1)

            def copy_left(s, ready, taken):
                act.wait_ge(y_full, ready)
                if taken is not None:
                    act.wait_ge(y_taken, taken)
                act.activation(y_rows[s][0:SLOTS, 0:BANK], psum[0:SLOTS, 6, :], ACT.Copy).then_inc(y_left, 1)

            copy_rows(0, 1)
            copy_rows(1, 2)
            sigmoid(0, 1)
            copy_rows(0, 3)
            sigmoid(1, 2)
            copy_left(0, 1, None)
            copy_rows(1, 4)
            sigmoid(0, 3)
            copy_left(1, 2, None)
            with act.Fori(2, NE // 2) as i:
                for s in (1, 0):
                    copy_rows(1 - s, i * 2 + (2 - s))
                    sigmoid(s, i * 2 + (1 - s))
                    copy_left(1 - s, i * 2 - s, i * 2 - (s + 2))
            sigmoid(1, NE)
            copy_left(0, NE - 1, NE - 3)
            copy_left(1, NE, NE - 2)
            n_over = act.value_load(over_i[0:1, OVER:OVER + 1], min_val=0, max_val=OVER)
            with act.If(n_over > 0):
                with act.Fori(0, n_over) as i:
                    act.wait_ge(ov_T, i + 1)
                    act.activation(hgT[0].rearrange("p k n -> p (k n)"), bank(4), ACT.Copy).then_inc(ov_Tc, 1)
                    act.wait_ge(ov_gu, i + 1)
                    act.activation(sig[0], psum[:, 0, 0:FC * SLOTS], ACT.Sigmoid).then_inc(ov_sig, 1)
                    act.wait_ge(ov_y, i + 2)
                    act.activation(y_rows[0][0:SLOTS, 0:BANK], psum[0:SLOTS, 6, :], ACT.Copy).then_inc(ov_yc, 1)
            with act.Else():
                act.nop()
            for t in range(TILES):
                w = tile_width(t)
                act.wait_ge(x2_ready, t + 1)
                if t >= 2:
                    act.wait_ge(y_stored[t % 2], 16 * (t // 2))
                act.activation(xn[t % 2][0:w, :], x[0:w, t, :], ACT.Square, accum_out=stats[0:w, 32 + t:33 + t]).then_inc(x2_ms, 1)
                if t >= 1:
                    finish_gate(act, t - 1)
            finish_gate(act, QT)
            act.wait_ge(out_act, 16 * stored[0])

        @block.tensor
        def _(pe):
            mm = nc.tensor.matmul
            tr = nc.tensor.transpose

            def done(ins, name):
                ins.then_inc(full[AT[name][0]], 1)

            pe.wait_ge(consts_built, 1)
            pe.wait_ge(rows_in, 64)
            done(tr(fill("params")[:, 0:30], params_nat[0:30, :], ident[0:30, 0:30]), "params")
            for t in range(TILES):
                w = tile_width(t)
                pe.wait_ge(xn_ready, t + 1)
                for s, half in enumerate("ab"):
                    name = f"x{t}{half}"
                    wait_free(pe, name)
                    for c in range(4):
                        k = 4 * s + c
                        last = tr(fill(name)[:, c * P:c * P + w], xn[t % 2][0:w, k * P:(k + 1) * P], ident[0:w, 0:w])
                    done(last, name)
                pe.nop().then_inc(xn_used, 1)
            pe.wait_ge(wf_in, 16)
            for s in range(2):
                pe.wait_ge(free[s], AT["x4a" if AT["x4a"][0] == s else "x4b"][1] + 1)
            for s in range(2):
                for k in range(DC):
                    last = mm(psum[0:HC, 2 + s, 0:HALF], w_forget[:, k, :], hT[:, k, s * HALF:(s + 1) * HALF],
                              start=(k == 0), stop=(k == DC - 1))
            last.then_inc(f_full, 1)

            def project(s, q, loaded, copied):
                if q == 0:
                    pe.wait_ge(w_in_s[s], loaded)
                if copied is not None:
                    pe.wait_ge(pj_free, copied)
                for half in range(2):
                    for k in range(DC):
                        last = mm(psum[:, 2 * q + half, 0:HALF], w_ring[s][:, k, q * P:(q + 1) * P],
                                  hT[:, k, half * HALF:(half + 1) * HALF], start=(k == 0), stop=(k == DC - 1))
                last.then_inc(pj_full, 1)

            pe.wait_ge(f_free, 1)
            for s in range(2):
                for q in range(2):
                    project(s, q, 16, None if s == 0 else q + 1)
            with pe.Fori(1, (GROUPS - FIRST) // 2) as i:
                for s in range(2):
                    for q in range(2):
                        project(s, q, i * 16 + 16, i * 4 + (2 * s + q - 1))
            wait_free(pe, "f")
            for t in range(TILES):
                w = tile_width(t)
                last = tr(fill("f")[0:w, t * HC:(t + 1) * HC], fT[0:HC, tile_cols(t)], ident[0:HC, 0:HC])
            done(last, "f")
            pe.wait_ge(pj_free, 2 * (GROUPS - FIRST))

            def natural(name, m, t):
                w = tile_width(t)
                wait_free(pe, name)
                for c in range(4):
                    last = tr(fill(name)[0:w, c * P:(c + 1) * P], projT[:, m + c, tile_cols(t)], ident)
                done(last, name)

            natural("qs", MT_Q, QT)
            natural("ks", MT_K, QT)
            natural("vs", MT_VC, QT)
            wait_free(pe, "qb")
            pe.wait_ge(free_of("qs"), AT["qs"][1] + 1)
            pe.wait_ge(consts_built, 2)
            done(mm(fill("qb"), row_sel[0:NB, :], q_s[0:NB, :], start=True, stop=True), "qb")
            wait_free(pe, "ws")
            pe.wait_ge(consts_in, 16 * 16)
            for h in range(4):
                last = tr(fill("ws")[:, h * P:(h + 1) * P], ws_nat[:, h, :], ident)
            done(last, "ws")
            for t in range(QT):
                natural(f"k{t}", MT_K, t)
                natural(f"v{t}", MT_VC, t)
            wait_free(pe, "suffix")
            pe.wait_ge(suf_ready, 1)
            done(mm(fill("suffix")[:, 0:HC], later, decay[:, PAGE - 1, :], start=True, stop=True), "suffix")
            wait_free(pe, "ct")
            pe.wait_ge(logf_ready, 1)
            for t in range(QT):
                last = mm(fill("ct")[0:HC, t * P:SEQ], f_nat[:, t, :], tri[:, 0:SEQ - t * P], start=(t == 0), stop=(t == QT - 1))
            done(last, "ct")
            wait_free(pe, "newT")
            pe.wait_ge(new_ready, 1)
            done(tr(fill("newT")[0:NB, 0:HC], new_s[0:NB, :], ident[0:NB, 0:NB]), "newT")

            pe.wait_ge(ct_ready, 1)

            def spread_ck(h):
                if h:
                    pe.wait_ge(ck_ready, h)
                mm(bank(7), ident[0:HC, h:h + 1].to_broadcast([HC, P]), cT[0:HC, :], start=True, stop=True).then_inc(ck_full, 1)

            spread_ck(0)
            units = 4 * HC
            for u in range(units + 2):
                if u < units:
                    h, t = u // QT, u % QT
                    c, q0 = h // 2, (h % 2) * HD
                    if u >= 2:
                        pe.wait_ge(a_read, u - 1)
                    mm(bank(u % 2)[:, 0:P * (t + 1)], projT[q0:q0 + HD, MT_Q + c, t * P:(t + 1) * P],
                       projT[q0:q0 + HD, MT_K + c, 0:P * (t + 1)], start=True, stop=True).then_inc(a_s, 1)
                if u % QT == 1 and u // QT + 1 < HC:
                    spread_ck(u // QT + 1)
                if 1 <= u <= units:
                    w = u - 1
                    t = w % QT
                    pe.wait_ge(a_p, w + 1)
                    if w >= 2:
                        pe.wait_ge(a_pt, w - 1)
                    for k in range(t + 1):
                        last = tr(bank(2 + w % 2)[:, k * P:(k + 1) * P], s_buf[w % 2][:, k * P:(k + 1) * P], ident)
                    last.then_inc(a_t, 1)
                if u >= 2:
                    w = u - 2
                    h, t = w // QT, w % QT
                    pe.wait_ge(a_pt, w + 1)
                    if w == 0:
                        pe.wait_ge(vn_ready, QT)
                    if w == 1:
                        pe.wait_ge(free[1], max(n for n, name in ((AT[m][1], m) for m in ("suffix", "ct", "newT")) if AT[name][0]) + 1)
                    if w >= 2:
                        pe.wait_ge(a_of, w - 1)
                    for k in range(t + 1):
                        last = mm(bank(6 - w % 2)[:, 0:HD], pT_buf[w % 2][:, k * P:(k + 1) * P],
                                  v_nat[:, k, h * HD:(h + 1) * HD], start=(k == 0), stop=(k == t))
                    last.then_inc(a_o, 1)

            n0 = GROUPS - FIRST
            pe.wait_ge(a_read, units)
            pe.wait_ge(a_pt, units)
            with pe.Fori(0, (FIRST - 1) // 2) as i:
                for s in range(2):
                    for q in range(2):
                        project(s, q, i * 16 + (16 * (n0 // 2) + 16), i * 4 + (2 * (n0 + s) + q - 1))
            for q in range(2):
                project(0, q, 16 * (GROUPS // 2 + 1), 2 * (GROUPS - 1) + q - 1)
            pe.wait_ge(pj_free, NM)
            pe.wait_ge(a_of, units)
            for name, tiles in (("vn01", (0, 1)), ("vn23", (2, 3)), ("vn4", (4,))):
                wait_free(pe, name)
                for n, t in enumerate(tiles):
                    w = tile_width(t)
                    for c in range(2):
                        last = tr(fill(name)[0:w, n * WB + c * P:n * WB + (c + 1) * P], projT[:, MT_V + c, tile_cols(t)], ident)
                done(last, name)
            wait_free(pe, "vnT")
            pe.wait_ge(v_ready, TILES)
            for c in range(2):
                last = tr(fill("vnT")[:, c * NB:(c + 1) * NB], v_norm[0:NB, QT, c * P:(c + 1) * P], ident[0:NB, 0:NB])
            done(last, "vnT")
            wait_free(pe, "state")
            for c in range(4):
                last = tr(fill("state")[:, c * NB:(c + 1) * NB], state[0:NB, c * P:(c + 1) * P], ident[0:NB, 0:NB])
            done(last, "state")
            wait_free(pe, "z")
            pe.wait_ge(z_ready, 1)
            for c in range(2):
                tr(fill("z")[0:2, c * P:(c + 1) * P], projT[:, 2 + c, SEQ - 2:SEQ], ident)
                last = tr(fill("z")[0:NB, WA + c * P:WA + (c + 1) * P], projT[:, 2 + c, SEQ:NT], ident)
            done(last, "z")
            for hp in range(2):
                name = f"gate{hp}"
                wait_free(pe, name)
                for t in range(QT):
                    for q in range(2):
                        h = 2 * hp + q
                        last = mm(fill(name)[q * HD:(q + 1) * HD, t * P:(t + 1) * P], v_norm[:, t, h * HD:(h + 1) * HD],
                                  wsT[:, h, :], start=True, stop=True)
                done(last, name)
            for t in range(QT):
                wait_free(pe, f"yc{t}")
                for c in range(4):
                    last = tr(fill(f"yc{t}")[:, c * P:(c + 1) * P], y_c[:, t, c * P:(c + 1) * P], ident)
                done(last, f"yc{t}")
            for name, chunks in (("normA", (0, 1)), ("normB", (2, 3)), ("normC", (0, 1, 2, 3))):
                wait_free(pe, name)
                pe.wait_ge(sq_ready, 2 if name == "normC" else 1)
                for n, c in enumerate(chunks):
                    last = mm(fill(name), ones, squares[:, c, :], start=(n == 0), stop=(n == len(chunks) - 1))
                done(last, name)
            for name, need, dst, src in (
                    ("maxT", 1, slice(0, HC), max_p), ("maxB", 2, slice(0, P), m_exp[0:HC, :]),
                    ("maxN", 2, slice(0, NB), mT[0:HC, :])):
                wait_free(pe, name)
                pe.wait_ge(smp_req, need)
                n = src.shape[0]
                done(tr(fill(name)[dst, 0:n], src, ident[0:n, 0:n]), name)
            wait_free(pe, "sum")
            pe.wait_ge(smp_req, 3)
            done(mm(fill("sum")[0:NB, 0:HC], col_sel, sum_p, start=True, stop=True), "sum")

            def mix_out(t):
                w = tile_width(t)
                if t >= 2:
                    pe.wait_ge(wo_free, t - 1)
                for n in range(2):
                    for k in range(DC):
                        last = mm(bank(2 * (t % 2) + n)[0:w, :], mixT[:, k, tile_cols(t)], w_out[:, k, n * BANK:(n + 1) * BANK],
                                  start=(k == 0), stop=(k == DC - 1))
                last.then_inc(wo_full, 1)

            def route(t):
                w = tile_width(t)
                pe.wait_ge(h2_ready, t + 1)
                for s, half in enumerate("ab"):
                    name = f"h{t}{half}"
                    wait_free(pe, name)
                    for c in range(4):
                        k = 4 * s + c
                        last = tr(fill(name)[:, c * P:c * P + w], xn[t % 2][0:w, k * P:(k + 1) * P], ident[0:w, 0:w])
                    done(last, name)
                name = f"h{t}r"
                wait_free(pe, name)
                pe.wait_ge(h2T_ready, t + 1)
                for k in range(DC):
                    last = mm(fill(name)[0:w, 0:NG + NE], h2T[t % 2][:, k, 0:w], w_route[:, k, :], start=(k == 0), stop=(k == DC - 1))
                done(last, name)

            def values(s, loaded, spread, first=False, last_one=False):
                pe.wait_ge(kv_in[s], loaded)
                pe.wait_ge(px_ready, spread)
                for k in range(KEYS):
                    for c in range(4):
                        ins = mm(bank(7)[:, c * 2 * NB:(c + 1) * 2 * NB], ring[s][:, k * WC + c * P:k * WC + (c + 1) * P],
                                 p_exp[s][:, k * HC + 2 * c:k * HC + 2 * c + 2, :],
                                 start=(first and k == 0 and c == 0), stop=(last_one and k == KEYS - 1),
                                 skip_group_check=True)
                ins.then_inc(pv_done, 1)

            k_loads = 16 * (CHUNKS // 4)

            def values_step(i, **flags):
                for s in range(4):
                    values(s, k_loads + 16 * (i + 1), 4 * i + s + 1, flags.get("first", False) and s == 0,
                           flags.get("last_one", False) and s == 3)

            pe.wait_ge(mix_normed, 1)
            pe.wait_ge(w_o_in, 16)
            pe.wait_ge(route_w_in, 32)
            mix_out(0)
            pe.wait_ge(ck_ready, HC)
            values_step(0, first=True)
            values_step(1)
            mix_out(1)
            route(0)
            for t in range(2, QT):
                with pe.Fori(2 * (t - 1), 2 * t) as i:
                    for s in range(4):
                        values(s, i * 16 + (k_loads + 16), i * 4 + (s + 1))
                mix_out(t)
                route(t - 1)
            values_step(6)
            values_step(7, last_one=True)
            route(QT - 1)
            wait_free(pe, "oN")
            pe.wait_ge(smp_req, 4)
            for c in range(4):
                last = tr(fill("oN")[0:NB, c * P:(c + 1) * P], oT[:, c, :], ident)
            done(last, "oN")
            wait_free(pe, "oT")
            pe.wait_ge(smp_req, 5)
            for c in range(4):
                last = tr(fill("oT")[:, c * NB:(c + 1) * NB], prod_s[0:NB, c * P:(c + 1) * P], ident[0:NB, 0:NB])
            done(last, "oT")
            wait_free(pe, "normS")
            pe.wait_ge(sq_ready, 3)
            for g, chunks in enumerate(((0, 1), (2, 3), (4, 5, 6, 7))):
                for n, c in enumerate(chunks):
                    sq = squares_s[:, c, :] if c < 4 else squares[:, 0, (c - 4) * NB:(c - 3) * NB]
                    last = mm(fill("normS")[:, g * NB:(g + 1) * NB], ones, sq, start=(n == 0), stop=(n == len(chunks) - 1))
            done(last, "normS")
            pe.wait_ge(mixs_normed, 1)
            mix_out(QT)
            route(QT)
            wait_free(pe, "rank")
            pe.wait_ge(route_op, 1)
            for t in range(TILES):
                for q in range(t + 1):
                    mm(fill("rank")[:, t * NE:(t + 1) * NE], ones if q < t else strict, chosen[:, q, :], start=(q == 0), stop=(q == t))
            for q in range(TILES):
                last = mm(fill("rank")[:, TILES * NE:(TILES + 1) * NE], ones, chosen[:, q, :], start=(q == 0), stop=(q == QT))
            done(last, "rank")

            pe.wait_ge(ple_in, 48)
            pes = (("p01", (0, 1)), ("p23", (2, 3)), ("p4", (4,)))
            for name, tiles in pes:
                wait_free(pe, name)
                for n, t in enumerate(tiles):
                    w = tile_width(t)
                    for k in range(2):
                        last = tr(fill(name)[:, k * 2 * P + n * P:k * 2 * P + n * P + w], p_nat[0:w, t, k * P:(k + 1) * P],
                                  ident[0:w, 0:w])
                done(last, name)
            pe.wait_ge(pT_ready, 1)
            pe.wait_ge(wo_free, TILES)
            for t in range(TILES):
                w = tile_width(t)
                if t >= 2:
                    pe.wait_ge(pe_free, t - 1)
                for n in range(2):
                    for k in range(2):
                        last = mm(bank(2 * (t % 2) + n)[0:w, :], pT[:, k, tile_cols(t)], w_ple_sb[:, k, n * BANK:(n + 1) * BANK],
                                  start=(k == 0), stop=(k == 1))
                last.then_inc(pe_full, 1)
            wait_free(pe, "list")
            pe.wait_ge(route_op, 2)
            for t in range(TILES):
                for c, one in enumerate((tile_one, tile_one2)):
                    last = mm(fill("list")[0:SLOTS, 0:2 * LIST], slot_one[:, c, t, :], one[:, t, :],
                              start=(t == 0 and c == 0), stop=(t == QT and c == 1))
            done(last, "list")

            pe.wait_ge(pe_free, TILES)
            for name in ("list", "p4"):
                pe.wait_ge(free_of(name), AT[name][1] + 1)

            def rows_T(s, loaded, copied, signal=hgT_full, src=hg_in):
                pe.wait_ge(src if src is not hg_in else hg_in[s], loaded)
                if copied is not None:
                    pe.wait_ge(hgT_ready, copied)
                if not isinstance(loaded, int):
                    alone(pe)
                hv = h_rows[s].rearrange("t (m k) -> t k m", k=DC)
                for k in range(DC):
                    last = tr(bank(4)[:, k * SLOTS:(k + 1) * SLOTS], hv[0:SLOTS, k, :], ident[0:SLOTS, 0:SLOTS])
                last.then_inc(signal, 1)

            def gate_up(s, loaded, rows, signal=gu_full):
                if rows is not None:
                    pe.wait_ge(hgT_ready, rows)
                for m in range(2):
                    if loaded is not None:
                        pe.wait_ge(gu_in[s][m], loaded)
                    for f in range(FC):
                        for k in range(DC):
                            last = mm(bank(s)[:, (m * FC + f) * SLOTS:(m * FC + f + 1) * SLOTS], w_gu[s][m][:, k, f * P:(f + 1) * P],
                                      hgT[s][:, k, :], start=(k == 0), stop=(k == DC - 1))
                last.then_inc(signal, 1)

            def down(s, loaded, ready, copied, signal=y_full):
                if ready is not None:
                    pe.wait_ge(act_ready, ready)
                    pe.wait_ge(dn_in[s], loaded)
                if copied is not None:
                    pe.wait_ge(y_left, copied)
                    pe.wait_ge(y_right, copied)
                for n in range(2):
                    for k in range(FC):
                        last = mm(bank(6 + n)[0:SLOTS, :], actT[s][:, k, :], w_dn[s][:, k, n * BANK:(n + 1) * BANK],
                                  start=(k == 0), stop=(k == FC - 1))
                last.then_inc(signal, 1)

            rows_T(0, 16, None)
            rows_T(1, 16, 1)
            gate_up(0, 16, 1)
            rows_T(0, 32, 2)
            gate_up(1, 16, 2)
            down(0, 16, 1, None)
            rows_T(1, 32, 3)
            gate_up(0, 32, 3)
            down(1, 16, 2, 1)
            with pe.Fori(2, NE // 2) as i:
                for s in (1, 0):
                    rows_T(1 - s, i * 16 + (0 if s else 16) + (16 if s else 0), i * 2 + (1 - s))
                    gate_up(s, i * 16 + (0 if s else 16), i * 2 + (1 - s))
                    down(1 - s, i * 16, i * 2 - s, i * 2 - (s + 1))
            gate_up(1, 8 * NE, NE)
            down(0, 8 * NE, NE - 1, NE - 2)
            down(1, 8 * NE, NE, NE - 1)
            pe.nop().then_inc(ov_y, 1)
            pe.wait_ge(y_left, NE)
            pe.wait_ge(y_right, NE)
            n_over = pe.value_load(over_i[0:1, OVER:OVER + 1], min_val=0, max_val=OVER)
            with pe.If(n_over > 0):
                with pe.Fori(0, n_over) as i:
                    pe.wait_ge(ov_w, i * 48 + 48)
                    rows_T(0, i * 16 + 16, None, ov_T, ov_rows)
                    pe.wait_ge(ov_Tc, i + 1)
                    gate_up(0, None, None, ov_gu)
                    pe.wait_ge(ov_act, i + 1)
                    down(0, None, None, None, ov_y)
            with pe.Else():
                pe.nop()
            pe.wait_ge(wpg_in, 16)
            for t in range(TILES):
                w = tile_width(t)
                pe.wait_ge(x3_ready, t + 1)
                for s in range(2):
                    if 2 * t + s >= 2:
                        pe.wait_ge(xT_ready, 2 * t + s - 1)
                    for c in range(4):
                        k = 4 * s + c
                        last = tr(bank(4 + s)[:, c * P:c * P + w], xn[t % 2][0:w, k * P:(k + 1) * P], ident[0:w, 0:w])
                    last.then_inc(xT_full, 1)
                pe.wait_ge(xT_ready, 2 * t + 2)
                if t >= 2:
                    pe.wait_ge(pg_sig, t - 1)
                for n in range(2):
                    for k in range(DC):
                        last = mm(bank(2 * (t % 2) + n)[0:w, :], xT[t % 2][:, k, 0:w], w_gate_ple[:, k, n * BANK:(n + 1) * BANK],
                                  start=(k == 0), stop=(k == DC - 1))
                last.then_inc(pg_full, 1)

        @block.vector
        def _(dve):
            step = Steps(dve, dve_step)
            v = nc.vector

            def tell(semaphore):
                dve.nop().then_inc(semaphore, 1)

            def root(dst, src, n):
                few = dst.shape[1] <= NB
                m, y = (r[0:dst.shape[0], 0:dst.shape[1]] for r in ((roots[:, 0, :], roots[:, 1, :]) if few else (root_m, root_y)))
                step(v.tensor_scalar(dst, src, 1.0 / n, EPS, ALU.mult, ALU.add))
                step(v.tensor_scalar(m, dst, -0.5, None, ALU.mult))
                step(v.tensor_scalar(y.bitcast(I32), dst.bitcast(I32), 1, None, ALU.logical_shift_right))
                step(v.tensor_scalar(y.bitcast(I32), y.bitcast(I32), -1, ROOT_GUESS, ALU.mult, ALU.add))
                for last in (False, False, False, True):
                    step(v.tensor_tensor(dst, y, y, ALU.mult))
                    step(v.tensor_tensor(dst, dst, m, ALU.mult))
                    step(v.scalar_tensor_tensor(out=dst if last else y, in0=dst, scalar=1.5, in1=y, op0=ALU.add, op1=ALU.mult))

            tell(kred)
            step(v.memset(f_nat, 0.0))
            wait_full(dve, "params")
            step(v.tensor_copy(params, fill("params")[:, 0:30]))
            dve.nop().then_inc(free_of("params"), 1)

            def norm_rows(t):
                w = tile_width(t)
                dve.wait_ge(ms_ready, t + 1)
                root(stats[0:w, 56 + t:57 + t], stats[0:w, t:t + 1], D)
                if t >= 2:
                    dve.wait_ge(xn_used, t - 1)
                v.tensor_scalar(xn[t % 2][0:w, :], x[0:w, t, :], stats[0:w, 56 + t:57 + t], None, ALU.mult).then_inc(xn_ready, 1)

            def copy_xT(t):
                w = tile_width(t)
                for s, half in enumerate("ab"):
                    name = f"x{t}{half}"
                    wait_full(dve, name)
                    src = fill(name).rearrange("p (c n) -> p c n", c=4)[:, :, 0:w]
                    v.tensor_tensor(hT[:, 4 * s:4 * s + 4, tile_cols(t)], src, inner(params[:, 4 * s:4 * s + 4], w), ALU.mult)\
                     .then_inc(free_of(name), 1)

            for t in range(TILES):
                norm_rows(t)
                if t:
                    copy_xT(t - 1)
            copy_xT(QT)
            wait_full(dve, "f")
            dve.wait_ge(consts_in, 16 * 16)
            step(v.tensor_tensor(f_nat[:, 0:QT, :], fill("f")[:, 0:QT * HC].rearrange("p (t h) -> p t h", h=HC), outer(bf_bc, QT), ALU.add))
            step(v.tensor_tensor(f_nat[0:NB, QT, :], fill("f")[0:NB, QT * HC:TILES * HC], bf_bc[0:NB, :], ALU.add))
            dve.nop().then_inc(free_of("f"), 1)
            step(v.tensor_scalar(f_a, f_nat, -1.0, None, ALU.mult))
            step(v.tensor_tensor(f_a, f_nat, f_a, ALU.max))
            tell(f_part)
            wait_full(dve, "ws")
            v.tensor_tensor(wsT, fill("ws").rearrange("p (h n) -> p h n", h=4), outer(tri[:, 0:P], 4), ALU.mult)\
             .then_inc(free_of("ws"), 1)
            dve.wait_ge(f_part, 2)
            step(v.tensor_scalar(f_c, f_b, 1.0, None, ALU.add))
            tell(f_part)
            step(v.tensor_scalar(f_a, f_c, -1.0, None, ALU.add))
            dve.wait_ge(f_part, 4)
            step(v.tensor_scalar(f_c, f_a, 0.0, None, ALU.is_equal))
            step(v.tensor_tensor(f_a, f_a, f_c, ALU.add))
            step(v.reciprocal(f_a, f_a))
            step(v.tensor_tensor(f_d, f_d, f_b, ALU.mult))
            step(v.tensor_tensor(f_d, f_d, f_a, ALU.mult))
            step(v.tensor_tensor(f_c, f_c, f_b, ALU.mult))
            step(v.tensor_tensor(f_d, f_d, f_c, ALU.add))
            step(v.scalar_tensor_tensor(out=f_nat, in0=f_nat, scalar=0.0, in1=f_d, op0=ALU.min, op1=ALU.subtract))
            tell(logf_ready)
            dve.wait_ge(sample_nat, 1)
            step(v.tensor_tensor(prod_s[0:NB, :], q_s[0:NB, :], k_s[0:NB, :], ALU.mult))
            step(v.tensor_reduce(new_s[0:NB, :], prod_s[0:NB, :].rearrange("p (h d) -> p h d", h=HC), AX.X, ALU.add))
            step(v.tensor_tensor(new_s[0:NB, :], new_s[0:NB, :], f_nat[0:NB, QT, :], ALU.subtract))
            tell(new_ready)
            for t in range(QT):
                wait_full(dve, f"v{t}")
                step(v.tensor_copy(v_nat[:, t, :], fill(f"v{t}")))
                dve.nop().then_inc(free_of(f"v{t}"), 1)
                tell(vn_ready)
            dve.wait_ge(lf_in, 16)
            for h in range(HC):
                ins = v.tensor_tensor_scan(decay[:, :, h], ones, logf_pages[:, :, h], 0.0, ALU.mult, ALU.add)
                step(ins)
            tell(suf_ready)
            wait_full(dve, "suffix")
            step(v.tensor_tensor(page_suf, fill("suffix")[:, 0:HC], decay[:, PAGE - 1, :], ALU.add))
            dve.nop().then_inc(free_of("suffix"), 1)
            step(v.tensor_tensor(decay, outer(page_suf, PAGE), decay, ALU.subtract))
            wait_full(dve, "newT")
            v.tensor_copy(newT_s[0:HC, :], fill("newT")[0:HC, 0:NB]).then_inc(free_of("newT"), 1)

            def reduce_keys(s, chunk_words, ready):
                dve.wait_ge(kmul, ready)
                v.tensor_reduce(chunk_words, ring[s].rearrange("p (a d) -> p a d", d=HD), AX.X, ALU.add).then_inc(kred, 1)

            units = 4 * HC
            for u in range(units + 3):
                if u < units:
                    h, t = u // QT, u % QT
                    nk = P * (t + 1)
                    sb = s_buf[u % 2]
                    dve.wait_ge(a_s, u + 1)
                    dve.wait_ge(ck_ready, h + 1)
                    if u >= 2:
                        dve.wait_ge(a_t, u - 1)
                    v.scalar_tensor_tensor(out=sb[:, 0:nk], in0=bank(u % 2)[:, 0:nk], scalar=SCALE, in1=ck_bc[h % 2][:, 0:nk],
                                           op0=ALU.mult, op1=ALU.subtract).then_inc(a_read, 1)
                    dve.wait_ge(a_read, u + 1)
                    step(v.tensor_tensor(sb[:, nk - P:nk], sb[:, nk - P:nk], mask, ALU.add))
                    v.tensor_reduce(stats[:, 8 + u % 2:9 + u % 2], sb[:, 0:nk], AX.X, ALU.max, negate=True).then_inc(a_m, 1)
                if u >= 3:
                    w = u - 3
                    h, t = w // QT, w % QT
                    dve.wait_ge(a_o, w + 1)
                    if w >= 2:
                        dve.wait_ge(a_of, w - 1)
                    step(v.reciprocal(stats[:, 20 + w % 2:21 + w % 2], stats[:, 16 + w % 4:17 + w % 4]))
                    v.tensor_scalar(y_c[:, t, h * HD:(h + 1) * HD], bank(6 - w % 2)[:, 0:HD], stats[:, 20 + w % 2:21 + w % 2], None,
                                    ALU.mult).then_inc(a_of, 1)
                if u % 4 == 3 and u < units:
                    j = u // 4
                    reduce_keys(j % 4, scores[:, j * KEYS * HC:(j + 1) * KEYS * HC], j + 1)
            with dve.Fori(2, CHUNKS // 4) as i:
                for s in range(4):
                    reduce_keys(s, scores[:, bass.ds(i * (4 * KEYS * HC) + s * KEYS * HC, KEYS * HC)], i * 4 + (s + 1))

            for name, tiles in (("vn01", (0, 1)), ("vn23", (2, 3)), ("vn4", (4,))):
                wait_full(dve, name)
                for n, t in enumerate(tiles):
                    w = tile_width(t)
                    src = fill(name)[0:w, n * WB:(n + 1) * WB]
                    step(v.bn_stats(bn[0:w, :], src))
                    step(v.bn_aggr(mv[0:w, :], bn[0:w, :]))
                    root(mv[0:w, 1:2], mv[0:w, 1:2], 1)
                    step(v.tensor_scalar(v_norm[0:w, t, :], src, mv[0:w, 0:1], mv[0:w, 1:2], ALU.subtract, ALU.mult))
                    if n == len(tiles) - 1:
                        dve.nop().then_inc(free_of(name), 1)
                    step(v.tensor_tensor(v_norm[0:w, t, :], v_norm[0:w, t, :], ln_g_bc[0:w, :], ALU.mult))
                    step(v.tensor_tensor(v_norm[0:w, t, :], v_norm[0:w, t, :], ln_b_bc[0:w, :], ALU.add))
                    tell(v_ready)
            wait_full(dve, "vnT")
            for hp in range(2):
                step(v.tensor_scalar(gate_s[:, hp, :], fill("vnT")[:, hp * NB:(hp + 1) * NB], w00[:, hp:hp + 1], bs_bc[:, hp, 0:1],
                                     ALU.mult, ALU.add))
            dve.nop().then_inc(free_of("vnT"), 1)
            step(v.tensor_tensor(mixT[:, 2:4, SEQ:NT], gate_s, projT[:, MT_U:MT_U + 2, SEQ:NT], ALU.mult))
            z = projT[:, 2:4, :]
            step(v.tensor_tensor(z, z, projT[:, 4:6, :], ALU.mult))
            tell(z_ready)
            wait_full(dve, "state")

            def tap(j, c):
                return params[:, 16 + 2 * j + c:17 + 2 * j + c]

            for c in range(2):
                y = mixT[:, c, :]
                step(v.tensor_scalar(y, z[:, c, :], tap(2, c), None, ALU.mult))
                for j in (1, 0):
                    d = 2 - j
                    step(v.scalar_tensor_tensor(out=y[:, d:SEQ], in0=z[:, c, 0:SEQ - d], scalar=tap(j, c), in1=y[:, d:SEQ],
                                                op0=ALU.mult, op1=ALU.add))
                    step(v.scalar_tensor_tensor(out=y[:, SEQ:NT], in0=fill("state")[:, (2 * j + c) * NB:(2 * j + c + 1) * NB],
                                                scalar=tap(j, c), in1=y[:, SEQ:NT], op0=ALU.mult, op1=ALU.add))
            dve.nop().then_inc(free_of("state"), 1)
            step(v.tensor_tensor(mixT[:, 0:2, :], mixT[:, 0:2, :], projT[:, 0:2, :], ALU.mult))
            tell(mix_ready)
            for hp in range(2):
                wait_full(dve, f"gate{hp}")
                y = mixT[:, 2 + hp, 0:SEQ]
                step(v.tensor_tensor(y.rearrange("p (t n) -> p t n", t=QT), fill(f"gate{hp}").rearrange("p (t n) -> p t n", t=QT),
                                     outer(bs_bc[:, hp, :], QT), ALU.add))
                dve.nop().then_inc(free_of(f"gate{hp}"), 1)
                step(v.tensor_tensor(y, y, projT[:, MT_U + hp, 0:SEQ], ALU.mult))
            tell(mix_ready)
            for name, width, chunks in (("normA", WA, (0, 1)), ("normB", WB, (2, 3)), ("normC", WC, (4, 5, 6, 7))):
                wait_full(dve, name)
                root(rms_bc, fill(name), width)
                dve.nop().then_inc(free_of(name), 1)
                for c in chunks:
                    ins = v.scalar_tensor_tensor(out=mixT[:, c, 0:SEQ], in0=mixT[:, c, 0:SEQ], scalar=params[:, 8 + c:9 + c],
                                                 in1=rms_bc, op0=ALU.mult, op1=ALU.mult)
                    step(ins)
            tell(mix_normed)

            dve.wait_ge(kred, CHUNKS + 1)
            s3 = scores.rearrange("p (k h) -> p k h", h=HC)
            by_head = scores.rearrange("p (k h) -> p h k", h=HC)
            step(v.tensor_tensor(s3, s3, decay, ALU.add))
            step(v.tensor_reduce(max_p, by_head, AX.X, ALU.max))
            tell(smp_req)
            wait_full(dve, "maxT")
            step(v.tensor_reduce(mT[0:HC, :], fill("maxT")[0:HC, 0:P].rearrange("p (b g) -> p b g", b=NB), AX.X, ALU.max))
            dve.nop().then_inc(free_of("maxT"), 1)
            step(v.tensor_tensor(mT[0:HC, :], mT[0:HC, :], newT_s[0:HC, :], ALU.max))
            step(v.tensor_copy(m_exp[0:HC, :].rearrange("p (b g) -> p b g", b=NB), inner(mT[0:HC, :], PAGES)))
            tell(smp_req)
            wait_full(dve, "maxB")
            step(v.tensor_copy(max_b, fill("maxB")[:, 0:HC]))
            dve.nop().then_inc(free_of("maxB"), 1)
            step(v.tensor_tensor(s3, s3, outer(max_b, PAGE), ALU.subtract))
            tell(smp_exp)
            wait_full(dve, "maxN")
            step(v.tensor_tensor(new_s[0:NB, :], new_s[0:NB, :], fill("maxN")[0:NB, 0:HC], ALU.subtract))
            dve.nop().then_inc(free_of("maxN"), 1)
            tell(smp_exp)
            dve.wait_ge(smp_p, 1)
            step(v.tensor_reduce(sum_p, by_head, AX.X, ALU.add))
            tell(smp_req)

            def spread_p(s, words, used):
                if used is not None:
                    dve.wait_ge(pv_done, used)
                v.tensor_tensor(p_exp[s], inner(words, NB), outer(col_sel, KEYS * HC), ALU.mult).then_inc(px_ready, 1)

            W = KEYS * HC

            def spread_step(i):
                for s in range(4):
                    spread_p(s, scores[:, (4 * i + s) * W:(4 * i + s + 1) * W], 4 * i + s - 3 if i else None)

            def add_out(t):
                w = tile_width(t)
                dve.wait_ge(wo_full, t + 1)
                pair = psum[0:w, 2 * (t % 2):2 * (t % 2) + 2, :]
                v.tensor_tensor(x[0:w, t, :].rearrange("p (a n) -> p a n", a=2), x[0:w, t, :].rearrange("p (a n) -> p a n", a=2), pair,
                                ALU.add).then_inc(wo_free, 1)

            def second_norm(t):
                w = tile_width(t)
                dve.wait_ge(x1_ms, t + 1)
                root(stats[0:w, 56:57], stats[0:w, 24 + t:25 + t], D)
                v.scalar_tensor_tensor(out=xn[t % 2][0:w, :], in0=x[0:w, t, :], scalar=stats[0:w, 56:57], in1=g_ffn_bc[0:w, :],
                                       op0=ALU.mult, op1=ALU.mult).then_inc(h2_ready, 1)

            def take_logits(t):
                w = tile_width(t)
                wait_full(dve, f"h{t}r")
                v.tensor_tensor(logits[0:w, t, :], fill(f"h{t}r")[0:w, 0:NG + NE], b_route[0:w, :], ALU.add)\
                 .then_inc(free_of(f"h{t}r"), 1)

            step(v.memset(logits, 0.0))
            spread_step(0)
            wait_full(dve, "sum")
            dve.wait_ge(smp_p, 2)
            step(v.tensor_tensor(sum_s[0:NB, :], fill("sum")[0:NB, 0:HC], pnew[0:NB, :], ALU.add))
            dve.nop().then_inc(free_of("sum"), 1)
            step(v.reciprocal(sum_s[0:NB, :], sum_s[0:NB, :]))
            add_out(0)
            second_norm(0)
            spread_step(1)
            add_out(1)
            second_norm(1)
            take_logits(0)
            for t in range(2, QT):
                with dve.Fori(2 * (t - 1), 2 * t) as i:
                    for s in range(4):
                        spread_p(s, scores[:, bass.ds(i * (4 * W) + s * W, W)], i * 4 + (s - 3))
                add_out(t)
                second_norm(t)
                take_logits(t - 1)
            spread_step(6)
            spread_step(7)
            take_logits(QT - 1)
            dve.wait_ge(pv_done, CHUNKS)
            pv = bank(7)[:, 0:4 * 2 * NB].rearrange("p (c q b) -> p c q b", c=4, q=2)
            step(v.tensor_copy(oT[0:HD, :, :], pv[0:HD, :, 0, :]))
            step(v.tensor_copy(oT[HD:P, :, :], pv[HD:P, :, 1, :]))
            tell(smp_req)
            q3, v3, o3 = (m[0:NB, :].rearrange("p (h d) -> p h d", h=HC) for m in (q_s, v_s, prod_s))
            step(v.tensor_tensor(q3, v3, inner(pnew[0:NB, :], HD), ALU.mult))
            wait_full(dve, "oN")
            step(v.tensor_tensor(prod_s[0:NB, :], fill("oN")[0:NB, :], q_s[0:NB, :], ALU.add))
            dve.nop().then_inc(free_of("oN"), 1)
            step(v.tensor_tensor(o3, o3, inner(sum_s[0:NB, :], HD), ALU.mult))
            tell(smp_req)
            wait_full(dve, "oT")
            step(v.tensor_copy(mixT[:, 4:8, SEQ:NT], fill("oT")[:, 0:4 * NB].rearrange("p (c b) -> p c b", c=4)))
            dve.nop().then_inc(free_of("oT"), 1)
            tell(mixs_ready)
            wait_full(dve, "normS")
            for g, (width, chunks) in enumerate(((WA, (0, 1)), (WB, (2, 3)), (WC, (4, 5, 6, 7)))):
                root(rms_bc[:, g * NB:(g + 1) * NB], fill("normS")[:, g * NB:(g + 1) * NB], width)
                for c in chunks:
                    step(v.scalar_tensor_tensor(out=mixT[:, c, SEQ:NT], in0=mixT[:, c, SEQ:NT], scalar=params[:, 8 + c:9 + c],
                                                in1=rms_bc[:, g * NB:(g + 1) * NB], op0=ALU.mult, op1=ALU.mult))
            dve.nop().then_inc(free_of("normS"), 1)
            tell(mixs_normed)
            add_out(QT)
            second_norm(QT)
            take_logits(QT)
            dve.wait_ge(free_of(f"h{QT}r"), AT[f"h{QT}r"][1] + 1)

            def first_of(one, scratch, index, src, top_value, n):
                step(v.tensor_tensor(scratch, src, inner(top_value, n), ALU.is_equal))
                step(v.tensor_scalar(scratch, scratch, -1.0, -BIG, ALU.add, ALU.mult))
                step(v.tensor_tensor(scratch, scratch, outer(iota[:, 0:n], TILES), ALU.add))
                step(v.tensor_reduce(index, scratch, AX.X, ALU.min))
                step(v.tensor_tensor(one, outer(iota[:, 0:n], TILES), inner(index, n), ALU.is_equal))

            grp, exp_ = logits[:, :, 0:NG], logits[:, :, NG:]
            g_top, g_idx, g_sum, p_g, gap, l1, l2, share, q_num, r_pos, base_e, t_num = r5
            step(v.tensor_reduce(g_top, grp, AX.X, ALU.max))
            step(v.tensor_tensor(eg, grp, inner(g_top, NG), ALU.subtract))
            tell(route_exp_in)
            first_of(g_one, gcand, g_idx, grp, g_top, NG)
            by_group = "p t (g e) -> p t g e"
            step(v.tensor_scalar(gcand, g_one, -1.0, BIG, ALU.add, ALU.mult))
            for t in range(TILES):
                dst = masked[:, t, :].rearrange("p (g e) -> p g e", g=NG)
                src = exp_[:, t, :].rearrange("p (g e) -> p g e", g=NG)
                step(v.tensor_tensor(dst, src, inner(g_one[:, t, :], NE // NG), ALU.mult))
                step(v.tensor_tensor(dst, dst, inner(gcand[:, t, :], NE // NG), ALU.add))
            step(v.tensor_reduce(l1, masked, AX.X, ALU.max))
            first_of(e_one[0], cand, e_idx[0], masked, l1, NE)
            step(v.tensor_scalar(cand, e_one[0], -BIG, None, ALU.mult))
            step(v.tensor_tensor(m2, masked, cand, ALU.add))
            step(v.tensor_reduce(l2, m2, AX.X, ALU.max))
            first_of(e_one[1], cand, e_idx[1], m2, l2, NE)
            step(v.tensor_tensor(gap, l2, l1, ALU.subtract))
            tell(route_exp_in)
            for e in e_one:
                step(v.tensor_tensor(e, e, inner(valid, NE), ALU.mult))
            step(v.tensor_tensor(chosen, e_one[0], e_one[1], ALU.add))
            tell(route_op)
            dve.wait_ge(route_exp_out, 2)
            step(v.tensor_reduce(g_sum, eg, AX.X, ALU.add))
            step(v.tensor_scalar(share, gap, 1.0, None, ALU.add))
            step(v.tensor_tensor(share, share, g_sum, ALU.mult))
            step(v.reciprocal(w_keep[0], share))
            step(v.tensor_tensor(w_keep[1], w_keep[0], gap, ALU.mult))
            wait_full(dve, "rank")
            step(v.tensor_copy(rank, fill("rank")[:, 0:TILES * NE].rearrange("p (t e) -> p t e", e=NE)))
            step(v.tensor_copy(count, fill("rank")[:, TILES * NE:(TILES + 1) * NE]))
            dve.nop().then_inc(free_of("rank"), 1)
            step(v.tensor_tensor(cmp8, inner(count, QMAX), outer(steps, NE), ALU.is_gt))
            step(v.tensor_reduce(tiles_over, cmp8, AX.X, ALU.add))
            step(v.tensor_tensor_scan(over_end, ones[:, 0:NE], tiles_over, 0.0, ALU.mult, ALU.add))
            step(v.tensor_tensor(over_base, over_end, tiles_over, ALU.subtract))
            for c, (one, tiles) in enumerate(zip(e_one, (tile_one, tile_one2))):
                step(v.tensor_tensor(prod_r, rank, one, ALU.mult))
                step(v.tensor_reduce(r_pos, prod_r, AX.X, ALU.add))
                step(v.tensor_tensor(prod_r, outer(over_base, TILES), one, ALU.mult))
                step(v.tensor_reduce(base_e, prod_r, AX.X, ALU.add))
                step(v.tensor_tensor(cmp5, inner(r_pos, QMAX), outer(steps, TILES), ALU.is_ge))
                step(v.tensor_reduce(q_num, cmp5, AX.X, ALU.add))
                step(v.scalar_tensor_tensor(out=r_pos, in0=q_num, scalar=-float(SLOTS), in1=r_pos, op0=ALU.mult, op1=ALU.add))
                step(v.tensor_tensor(slot_one[:, c, :, :], outer(iota, TILES), inner(r_pos, SLOTS), ALU.is_equal))
                step(v.tensor_tensor(base_e, base_e, q_num, ALU.add))
                step(v.tensor_scalar(base_e, base_e, float(NE - 1), None, ALU.add))
                step(v.tensor_tensor(base_e, base_e, e_idx[c], ALU.subtract))
                step(v.tensor_scalar(t_num, q_num, 0.0, None, ALU.is_gt))
                step(v.tensor_tensor(t_num, t_num, base_e, ALU.mult))
                step(v.tensor_tensor(t_num, t_num, e_idx[c], ALU.add))
                hit = tiles[:, :, 0:LIST]
                step(v.tensor_tensor(hit, outer(iota[:, 0:LIST], TILES), inner(t_num, LIST), ALU.is_equal))
                step(v.tensor_tensor(hit, hit, inner(valid, LIST), ALU.mult))
                step(v.tensor_tensor(tiles[:, :, LIST:], hit, inner(tokid, LIST), ALU.mult))
                step(v.tensor_scalar(share, tokid, 2.0, float(c + 1), ALU.mult, ALU.add))
                step(v.tensor_tensor(hit, hit, inner(share, LIST), ALU.mult))
            tell(route_op)
            step(v.tensor_tensor(cmp_over, outer(over_end, OVER), inner(iota[:, 0:OVER], NE), ALU.is_le))
            step(v.tensor_reduce(over_f[:, 0:OVER], cmp_over, AX.X, ALU.add))
            step(v.tensor_scalar(over_f[:, 0:OVER], over_f[:, 0:OVER], float(NE - 1), None, ALU.min))
            step(v.tensor_copy(over_f[:, OVER:OVER + 1], over_end[:, NE - 1:NE]))
            step(v.tensor_copy(over_i[:, 0:OVER + 1], over_f))
            wait_full(dve, "list")
            step(v.tensor_copy(list_f[0:SLOTS, :], fill("list")[0:SLOTS, 0:2 * LIST]))
            dve.nop().then_inc(free_of("list"), 1)
            step(v.tensor_copy(tok_list[0:SLOTS, :], list_f[0:SLOTS, LIST:]))
            step(v.tensor_scalar(list_f[0:SLOTS, LIST:], list_f[0:SLOTS, 0:LIST], 0.0, float(2 * PAIRS), ALU.is_equal, ALU.mult))
            step(v.scalar_tensor_tensor(out=list_f[0:SLOTS, 0:LIST], in0=list_f[0:SLOTS, 0:LIST], scalar=-1.0,
                                        in1=list_f[0:SLOTS, LIST:], op0=ALU.add, op1=ALU.add))
            step(v.tensor_copy(pair_list[0:SLOTS, :], list_f[0:SLOTS, 0:LIST]))
            dve.nop().then_inc(lists_ready, 1)

            half = FC * SLOTS

            def activate(s, ready, semaphore=sig_ready, signal=act_ready):
                dve.wait_ge(semaphore, ready)
                step(v.tensor_tensor(sig[s], sig[s], bank(s)[:, 0:half], ALU.mult))
                v.tensor_tensor(actT[s].rearrange("p k n -> p (k n)"), sig[s], bank(s)[:, half:2 * half], ALU.mult).then_inc(signal, 1)

            def copy_right(s, ready, taken):
                dve.wait_ge(y_full, ready)
                if taken is not None:
                    dve.wait_ge(y_taken, taken)
                v.tensor_copy(y_rows[s][0:SLOTS, BANK:2 * BANK], psum[0:SLOTS, 7, :]).then_inc(y_right, 1)

            activate(0, 1)
            activate(1, 2)
            copy_right(0, 1, None)
            activate(0, 3)
            copy_right(1, 2, None)
            base = step.n
            with dve.Fori(2, NE // 2) as i:
                step.off = (i - 2) * 2
                for s in (1, 0):
                    activate(s, i * 2 + (1 - s))
                    copy_right(1 - s, i * 2 - s, i * 2 - (s + 2))
            step.n, step.off = base + 2 * (NE // 2 - 2), 0
            activate(1, NE)
            copy_right(0, NE - 1, NE - 3)
            copy_right(1, NE, NE - 2)
            n_over = dve.value_load(over_i[0:1, OVER:OVER + 1], min_val=0, max_val=OVER)
            with dve.If(n_over > 0):
                with dve.Fori(0, n_over) as i:
                    dve.wait_ge(ov_sig, i + 1)
                    v.tensor_tensor(sig[1], sig[0], bank(0)[:, 0:half], ALU.mult).then_inc(ov_m, 1)
                    dve.wait_ge(ov_m, i + 1)
                    v.tensor_tensor(actT[0].rearrange("p k n -> p (k n)"), sig[1], bank(0)[:, half:2 * half], ALU.mult).then_inc(ov_act, 1)
                    dve.wait_ge(ov_y, i + 2)
                    v.tensor_copy(y_rows[0][0:SLOTS, BANK:2 * BANK], psum[0:SLOTS, 7, :]).then_inc(ov_yc, 1)
            with dve.Else():
                dve.nop()

            def add_experts(t):
                w = tile_width(t)
                dve.wait_ge(pairs_ready[t % 2], 16 * (t // 2 + 1))
                for c in range(2):
                    step(v.scalar_tensor_tensor(out=x[0:w, t, :], in0=pairs_in[t % 2][0:w, c * D:(c + 1) * D],
                                                scalar=w_keep[c][0:w, t:t + 1], in1=x[0:w, t, :], op0=ALU.mult, op1=ALU.add))
                tell(x2_ready)
                dve.wait_ge(x2_ms, t + 1)
                root(stats[0:w, 57:58], stats[0:w, 32 + t:33 + t], D)
                v.tensor_scalar(xn[t % 2][0:w, :], x[0:w, t, :], stats[0:w, 57:58], None, ALU.mult).then_inc(x3_ready, 1)
                for s in range(2):
                    dve.wait_ge(xT_full, 2 * t + s + 1)
                    src = bank(4 + s).rearrange("p (c n) -> p c n", c=4)[:, :, 0:w]
                    v.tensor_tensor(xT[t % 2][:, 4 * s:4 * s + 4, 0:w], src, inner(params[:, 22 + 4 * s:26 + 4 * s], w), ALU.mult)\
                     .then_inc(xT_ready, 1)

            def finish(t):
                w = tile_width(t)
                dve.wait_ge(pg_sig, t + 1)
                g = ple_gate[t % 2][0:w, :]
                step(v.tensor_tensor(g, g, p_emb[0:w, t, :], ALU.mult))
                step(v.tensor_tensor(x[0:w, t, :], x[0:w, t, :], g, ALU.add))
                tell(x4_ready)
                dve.wait_ge(x4_ms, t + 1)
                root(stats[0:w, 58:59], stats[0:w, 48 + t:49 + t], D)
                v.scalar_tensor_tensor(out=xn[t % 2][0:w, :], in0=x[0:w, t, :], scalar=stats[0:w, 58:59], in1=g_fin[0:w, :],
                                       op0=ALU.mult, op1=ALU.mult).then_inc(y_final, 1)

            dve.wait_ge(gfin_in, 16)
            for t in range(TILES):
                add_experts(t)
                if t:
                    finish(t - 1)
            finish(QT)


INPUTS = ["x_prompt", "x_sample", "p_prompt", "p_sample", "cache_k", "cache_v", "cache_logf", "state_conv", "page_table",
          "g_mix", "w_in", "conv_w", "ln_g", "ln_b", "w_s", "b_s", "b_f", "g_out", "w_o", "g_ffn", "w_grp", "b_grp",
          "w_rt", "b_rt", "w_gate", "w_up", "w_down", "g_ple", "w_ple", "w_ple_gate", "g_final"]
OUTPUTS = [(1, SEQ, D), (NB, 1, D), (1, 1, SEQ, HC, HD), (1, 1, SEQ, HC, HD), (1, 1, SEQ, HC), (1, 1, 2, WA),
           (1, NB, 1, HC, HD), (1, NB, 1, HC, HD), (1, NB, 1, HC), (1, NB, 2, WA), (1, NB, 1, WB)]


def kernel(**inputs):
    import numpy as _np
    import concourse.bacc as _bacc
    from concourse.bass_utils import run_bass_kernel_spmd as _run

    nc = _bacc.Bacc("TRN2", target_bir_lowering=False, num_devices=1)
    arrays, a = {}, {}
    for name in INPUTS:
        arrays[f"in_{name}"] = _np.ascontiguousarray(inputs[name])
        dt = mybir.dt.from_np(arrays[f"in_{name}"].dtype)
        a[name] = nc.dram_tensor(f"in_{name}", arrays[f"in_{name}"].shape, dt, kind="ExternalInput").ap()
    o = [nc.dram_tensor(f"out_{i}", shape, F32, kind="ExternalOutput").ap() for i, shape in enumerate(OUTPUTS)]
    build(nc, a, o)
    r = _run(nc, [arrays], core_ids=[0])
    return tuple(r.results[0][f"out_{i}"] for i in range(len(OUTPUTS)))
```

```python
from contextlib import ExitStack

import concourse.bass as bass
from concourse import mybir

F32 = mybir.dt.float32
I32 = mybir.dt.int32
ALU = mybir.AluOpType
ACT = mybir.ActivationFunctionType
AX = mybir.AxisListType

P = 128
BANK = 512
D = 1024
DC = D // P
SEQ, NB = 512, 8
NT = SEQ + NB
QT = SEQ // P
TILES = QT + 1
HALF = NT // 2
WA, WB, WC, HC, HD = 256, 256, 512, 8, 64
MT_A, MT_U, MT_V, MT_Q, MT_K, MT_VC = 0, 6, 8, 10, 14, 18
NM = 22
GROUPS = NM // 2
FIRST = MT_Q // 2
PAGE, PAGES = 128, 16
KEYS = 4
CHUNKS = PAGE // KEYS
CW = KEYS * WC
NE, NG, DE = 32, 4, 512
FC = DE // P
SLOTS = 64
PAIRS = 2 * NT
OVER = (PAIRS - NE) // SLOTS
LIST = 48
QMAX = NT // SLOTS
RING = 4
DP = 256
EPS = 1e-6
BIG = 1.0e30
SCALE = HD ** -0.5
ROOT_GUESS = 0x5F3759DF

LEAD = RING + 1

assert NE + OVER < LIST and HALF * 2 == NT


def tile_width(t):
    return P if t < QT else NB


def tile_cols(t):
    return slice(t * P, t * P + tile_width(t))


FILLS = (["params"] + [f"x{t}{s}" for t in range(TILES) for s in "ab"]
         + ["f", "qs", "ks", "vs", "qb", "ws"] + [f"{n}{t}" for t in range(QT) for n in "kv"]
         + ["suffix", "ct", "newT"]
         + ["vn01", "vn23", "vn4", "vnT", "state", "z", "gate0", "gate1"] + [f"yc{t}" for t in range(QT)]
         + ["normA", "normB", "normC", "maxT", "maxB", "maxN", "sum"]
         + [f"h{t}{s}" for t in range(QT) for s in ("a", "b", "r")]
         + ["oN", "oT", "normS"]
         + [f"h{QT}{s}" for s in ("a", "b", "r")]
         + ["rank", "p01", "p23", "p4", "list"])
AT = {name: (n % 2, n // 2) for n, name in enumerate(FILLS)}


def build(nc, a, o):
    (y_prompt, y_sample, k_prompt, v_prompt, logf_prompt, conv_prompt,
     k_sample, v_sample, logf_sample, conv_sample, chunk_v_sample) = o
    h2_dram = nc.dram_tensor("h2_rows", [NT, D], F32, kind="Internal").ap()
    moe_dram = nc.dram_tensor("moe_rows", [2 * PAIRS, BANK], F32, kind="Internal").ap()

    with ExitStack() as ctx:
        arena_size = 53024
        arena = ctx.enter_context(nc.sbuf_tensor("arena", [P, arena_size], F32))
        psum = ctx.enter_context(nc.psum_tensor("psum", [P, 8, BANK], F32))

        def ints(name, n):
            return ctx.enter_context(nc.sbuf_tensor(name, [P, n], I32))

        top = [0]

        def place(n):
            top[0] += n
            assert top[0] <= arena_size, top[0]
            return top[0] - n

        def at(start, *shape):
            n = 1
            for s in shape:
                n *= s
            flat = arena[:, start:start + n]
            if len(shape) == 1:
                return flat
            if len(shape) == 2:
                return flat.rearrange("p (a b) -> p a b", a=shape[0])
            return flat.rearrange("p (a b c) -> p a b c", a=shape[0], b=shape[1])

        region_a = place(MT_V * NT + DC * D)
        region_b = place(3 * DC * BANK)
        region_c = place(DC * NT + 2 * DC * 2 * P + 4 * NT + PAGE * HC)

        projT = at(region_a, NM, NT)
        cT = at(region_a + NM * NT, SEQ)
        w_out = at(region_a + MT_V * NT, DC, D)
        ring = [at(region_b + s * CW, CW) for s in range(4)]
        b_tail = region_b + 4 * CW
        s_buf = [at(b_tail + s * SEQ, SEQ) for s in range(2)]
        pT_buf = [at(b_tail + (2 + s) * SEQ, SEQ) for s in range(2)]
        k_nat = [at(b_tail + (4 + s) * SEQ, SEQ) for s in range(2)]
        ck_bc = [at(b_tail + (6 + s) * SEQ, SEQ) for s in range(2)]
        junk = at(b_tail, D)
        ws_nat = at(b_tail + 2 * SEQ, 4, P)
        w_forget = at(b_tail + 3 * SEQ, DC, HC)
        rms_bc = at(b_tail + 6 * SEQ, SEQ)
        root_y = at(b_tail + 7 * SEQ, SEQ)
        root_m = at(b_tail + 2 * SEQ, SEQ)
        w_ple_sb = at(b_tail, 2, D)
        hT = at(region_c, DC, NT)
        mixT = hT
        c1 = region_c + DC * NT
        w_ring = [at(c1 + s * DC * 2 * P, DC, 2 * P) for s in range(2)]
        c2 = c1 + 2 * DC * 2 * P
        v_nat = at(c2, QT, WC)
        squares = at(c2, 4, SEQ)
        squares_s = at(c2 + 4 * SEQ, 4, NB)
        c3 = c2 + 4 * NT
        scores = at(c3, PAGE * HC)

        p_emb = at(region_c, TILES, D)
        c4 = region_c + TILES * D
        h2T = [at(c4 + s * D, DC, P) for s in range(2)]
        hgT = [at(c4 + 2 * D + s * DC * SLOTS, DC, SLOTS) for s in range(2)]
        silu = at(c4 + 3 * D, DE)
        act_nat = at(c4 + 3 * D + DE, DE)
        actT = [at(c4 + 4 * D + s * FC * SLOTS, FC, SLOTS) for s in range(2)]
        assert c4 + 6 * D <= c3 + PAGE * HC
        p_nat = at(c4 + 4 * D, TILES, DP)
        pT = at(c4 + 2 * D, 2, NT)

        w_gu = [[at(r + m * DC * BANK, DC, DE) for m in range(2)] for r in (region_b, region_a)]
        w_dn = [at(r + 2 * DC * BANK, FC, D) for r in (region_b, region_a)]
        w_gate_ple = at(region_b, DC, D)
        g_fin = at(region_a + 8192, D)
        pairs_in = [at(region_a + s * 2 * D, 2 * D) for s in range(2)]
        ple_gate = [at(region_a + 4 * D + s * D, D) for s in range(2)]
        xT = [at(region_a + 6 * D + s * D, DC, P) for s in range(2)]

        x = at(place(TILES * D), TILES, D)
        xn0 = place(2 * D)
        xn = [at(xn0 + s * D, D) for s in range(2)]
        y_c = at(xn0, QT, WC)
        g_ffn_bc = at(place(D), D)
        h_rows = [at(c4 + s * D, D) for s in range(2)] + [at(xn0 + s * D, D) for s in range(2)]
        y_rows = [at(c4 + 5 * D + s * BANK, BANK) for s in range(2)] + [g_ffn_bc[:, s * BANK:(s + 1) * BANK] for s in range(2)]
        ident = at(place(P), P)
        tri = at(place(SEQ), SEQ)
        ones = tri[:, P:2 * P]
        mask = at(place(P), P)
        strict = at(place(P), P)
        later = at(place(P), P)
        row_sel = at(place(P), P)
        col_sel = at(place(NB), NB)
        roots = at(place(2 * NB), 2, NB)
        params = at(place(30), 30)
        stats = at(place(64), 64)
        small0 = place(7120)
        small_top = [small0]

        def small(*shape):
            n = 1
            for s in shape:
                n *= s
            small_top[0] += n
            assert small_top[0] <= small0 + 7120, small_top[0] - small0
            return at(small_top[0] - n, *shape)

        params_nat = small(P)
        logf_pages = small(PAGE, HC)
        decay = small(PAGE, HC)
        f_nat = small(TILES, HC)
        f_a, f_b, f_c, f_d = (small(TILES, HC) for _ in range(4))
        q_s, k_s, v_s, prod_s = (small(WC) for _ in range(4))
        q_bc = small(WC)
        wsT = small(4, P)
        bs_bc = small(2, P)
        v_norm = at(c2 - TILES * WB, TILES, WB)
        ln_g_bc, ln_b_bc = small(WB), small(WB)
        bf_bc = small(HC)
        w00 = small(2)
        state = small(2 * WA)
        z_p, z_s = q_bc[:, 0:WA], q_bc[:, WA:2 * WA]
        new_s, newT_s, mT, pnew, m_nat, sum_s = (small(HC) for _ in range(6))
        m_exp = small(P)
        max_p, max_b, sum_p = (small(HC) for _ in range(3))
        page_suf = small(HC)
        oT = small(4, NB)
        vnT = small(2, NB)
        gate_s = small(2, NB)
        conv_tmp = small(2, NB)
        bn = small(6)
        mv = small(2)
        p_exp = [at(b_tail + 4 * SEQ + s * KEYS * HC * NB, KEYS * HC, NB) for s in range(4)]
        fT = at(b_tail + 4 * SEQ, NT)
        small_top[0] = small0
        logits = small(TILES, NG + NE)
        eg = small(TILES, NG)
        gcand = small(TILES, NG)
        g_one = small(TILES, NG)
        masked = small(TILES, NE)
        m2 = small(TILES, NE)
        cand = small(TILES, NE)
        e_one = [small(TILES, NE) for _ in range(2)]
        chosen = small(TILES, NE)
        prod_r = small(TILES, NE)
        rank = small(TILES, NE)
        count = small(NE)
        cmp8 = small(NE, QMAX)
        tiles_over, over_end, over_base = small(NE), small(NE), small(NE)
        r5 = [small(TILES) for _ in range(12)]
        e_idx = [small(TILES) for _ in range(2)]
        cmp5 = small(TILES, QMAX)
        slot_one = small(2, TILES, SLOTS)
        tile_one = small(TILES, 2 * LIST)
        tile_one2 = small(TILES, 2 * LIST)
        list_f = small(2 * LIST)
        cmp_over = small(OVER, NE)
        over_f = small(OVER + 1)
        routing_end = small_top[0]
        w_keep = [at(place(TILES), TILES) for _ in range(2)]
        iota = at(place(SLOTS), SLOTS)
        tokid = at(place(TILES), TILES)
        steps = at(place(QMAX), QMAX)
        valid = at(place(TILES), TILES)
        b_route = at(place(NG + NE), NG + NE)
        w_route = at(place(DC * (NG + NE)), DC, NG + NE)
        half_row = at(place(1), 1)
        page_f = at(place(1), 1)
        chunk_f = at(place(4), 4)
        indices = ints("indices", 5 + 2 * RING)
        page_id = indices[:, 0:1]
        chunk_id = [indices[:, 1 + s:2 + s] for s in range(4)]
        tok_list, row_list = ints("tok_list", LIST), ints("row_list", LIST)
        tok_ix = [indices[:, 5 + s:6 + s] for s in range(RING)]
        row_ix = [indices[:, 5 + RING + s:6 + RING + s] for s in range(RING)]
        over_i = ints("over_i", OVER + 1)

        def sem(name):
            return ctx.enter_context(nc.semaphore(name))

        x_in = [sem(f"x_in{t}") for t in range(TILES)]
        rows_in, consts_in, wf_in, lf_in, page_in = (sem(n) for n in ("rows_in", "consts_in", "wf_in", "lf_in", "page_in"))
        route_w_in = sem("route_w_in")
        pool_step, act_step, dve_step = sem("pool_step"), sem("act_step"), sem("dve_step")
        consts_built = sem("consts_built")
        full = [sem("fill_ready0"), sem("fill_ready1")]
        free = [sem("fill_read0"), sem("fill_read1")]
        ms_ready, xn_ready, xn_used = sem("ms_ready"), sem("xn_ready"), sem("xn_used")
        f_full, f_free = sem("f_full"), sem("f_free")
        w_in_s = [sem("w_group_in0"), sem("w_group_in1")]
        pj_full, pj_free = sem("proj_ready"), sem("proj_copied")
        kn_out, vn_ready = [sem("k_nat_stored0"), sem("k_nat_stored1")], sem("v_nat_ready")
        sample_nat = sem("sample_nat_ready")
        qb_ready = sem("q_bc_ready")
        logf_ready = sem("logf_ready")
        f_part = sem("f_part")
        kv_in = [sem(f"cache_in{s}") for s in range(4)]
        kmul, kred = sem("k_products"), sem("k_reduced")
        suf_ready = sem("suffix_parts_ready")
        ct_ready = sem("cT_ready")
        ck_full, ck_ready = sem("ck_full"), sem("ck_bc_ready")
        a_s, a_read, a_m, a_p, a_t, a_pt, a_o, a_of = (sem("att_" + n) for n in (
            "scores", "scores_read", "max", "probs", "probsT", "probsT_copied", "out", "out_copied"))
        v_ready = sem("v_norm_ready")
        z_ready = sem("z_ready")
        z_nat = sem("z_nat_ready")
        mix_ready = sem("mix_ready")
        sq_ready = sem("squares_ready")
        w_o_in = sem("w_o_in")
        wo_full, wo_free = sem("wo_full"), sem("wo_added")
        x1_ms, h2_ready, h2T_ready = sem("x1_ms"), sem("h2_ready"), sem("h2T_ready")
        h2_stored = [sem("h2_stored0"), sem("h2_stored1")]
        mix_normed, mixs_normed, new_ready = sem("mix_normed"), sem("mix_sample_normed"), sem("new_score_ready")
        smp_req, smp_exp, smp_p = sem("sample_operand"), sem("sample_exp_in"), sem("sample_exp_out")
        px_ready, pv_done, pv_read = sem("p_expanded"), sem("pv_done"), sem("pv_read")
        mixs_ready = sem("mix_sample_ready")
        route_op, route_exp_in, route_exp_out = sem("route_operand"), sem("route_exp_in"), sem("route_exp_out")
        lists_ready = sem("lists_ready")
        ple_in, pT_ready, pe_full, pe_free = sem("ple_in"), sem("pT_ready"), sem("p_emb_full"), sem("p_emb_copied")
        hg_in, y_out = ([sem(f"{n}{s}") for s in range(RING)] for n in ("rows_in", "y_out"))
        gu_in = [[sem(f"w_{m}{s}_in") for m in ("gate", "up")] for s in range(2)]
        dn_in = [sem("w_down0_in"), sem("w_down1_in")]
        hgT_full, hgT_ready, gu_full, silu_ready, act_ready, actT_full, actT_ready, y_full, y_copied = (sem("moe_" + n) for n in (
            "rowsT_full", "rowsT_ready", "gate_up", "silu", "act", "actT_full", "actT_ready", "y_full", "y_copied"))
        moe_done = sem("moe_done")
        ov_w, ov_rows, ov_T, ov_Tc, ov_gu, ov_silu, ov_act, ov_aT, ov_aTc, ov_y, ov_yc, ov_out = (sem("over_" + n) for n in (
            "weights_in", "rows_in", "rowsT", "rowsT_ready", "gate_up", "silu", "act", "actT", "actT_ready", "y", "y_ready", "stored"))
        wpg_in, gfin_in, pairs_ready = sem("w_ple_gate_in"), sem("g_final_in"), [sem("pairs_in0"), sem("pairs_in1")]
        x2_ms, x3_ready, xT_full, xT_ready, pg_full, pg_sig, pg_free, x4_ms, y_final = (sem("post_" + n) for n in (
            "x2_ms", "xn", "xT_full", "xT", "gate_full", "gate_sigmoid", "gate_free", "x4_ms", "y"))
        x2_ready, x4_ready = sem("post_x2"), sem("post_x4")
        y_stored, out_act = [sem("y_stored0"), sem("y_stored1")], sem("stored_by_scalar")

        passed = sem("passed")

        block = ctx.enter_context(nc.Block())

        def bank(b):
            return psum[:, b, :]

        def fill(name):
            return bank(4 + AT[name][0])

        def wait_full(eng, name):
            b, n = AT[name]
            eng.wait_ge(full[b], n + 1)

        def free_of(name):
            return free[AT[name][0]]

        def wait_free(eng, name):
            b, n = AT[name]
            if n:
                eng.wait_ge(free[b], n)

        def alone(eng):
            eng.nop().then_inc(passed, 1)

        class Steps:

            def __init__(self, eng, semaphore):
                self.eng, self.sem, self.n, self.off = eng, semaphore, 0, 0

            def __call__(self, ins):
                self.n += 1
                ins.then_inc(self.sem, 1)
                self.eng.wait_ge(self.sem, self.n + self.off)
                if not isinstance(self.off, int):
                    alone(self.eng)

        def inner(ap, n):
            return ap.rearrange("p (a o) -> p a o", o=1).to_broadcast([ap.shape[0], ap.shape[1], n])

        def outer(ap, n):
            return ap.rearrange("p (o a) -> p o a", o=1).to_broadcast([ap.shape[0], n, ap.shape[1]])

        def num(i, c):
            return i * RING + c

        def loads(i, c, ring):
            return i * (16 * RING // ring) + 16 * (c // ring + 1)

        def exists(i, c):
            return not isinstance(i, int) or RING * i + c >= 0

        def bc_rows(src, n=P):
            return src.to_broadcast([n, src.shape[-1]])

        def finish_gate(act, t):
            w = tile_width(t)
            act.wait_ge(pg_full, t + 1)
            act.activation(ple_gate[t % 2][0:w, :].rearrange("p (a n) -> p a n", a=2), psum[0:w, 2 * (t % 2):2 * (t % 2) + 2, :],
                           ACT.Sigmoid).then_inc(pg_sig, 1)
            act.wait_ge(x4_ready, t + 1)
            act.activation(xn[t % 2][0:w, :], x[0:w, t, :], ACT.Square, accum_out=stats[0:w, 48 + t:49 + t]).then_inc(x4_ms, 1)

        @block.sync
        def _(sp):
            for t in range(QT):
                sp.dma_start(x[:, t, :], a["x_prompt"][0, t * P:(t + 1) * P, :]).then_inc(x_in[t], 16)
            sp.dma_start(x[0:NB, QT, :], a["x_sample"].rearrange("b l d -> (b l) d")).then_inc(x_in[QT], 16)
            w_in_v = a["w_in"][0].rearrange("(k p) n -> p k n", p=P)

            def w_group(n, slot):
                return w_ring[slot]

            def load_group(g, slot):
                sp.dma_start(w_ring[slot], w_in_v[:, :, bass.ds(g * (2 * P), 2 * P)]).then_inc(w_in_s[slot], 16)

            load_group(FIRST, 0)
            load_group(FIRST + 1, 1)
            with sp.Fori(1, (GROUPS - FIRST) // 2) as i:
                for s in range(2):
                    sp.wait_ge(pj_full, i * 4 + (2 * s - 2))
                    load_group(i * 2 + (FIRST + s), s)
            done = GROUPS - FIRST
            with sp.Fori(0, (GROUPS - done) // 2) as i:
                for s in range(2):
                    sp.wait_ge(pj_full, i * 4 + (2 * (done + s) - 2))
                    load_group(i * 2 + s, s)
            sp.wait_ge(pj_full, 2 * (GROUPS - 1) - 2)
            load_group(GROUPS - done - 1, 0)
            sp.wait_ge(a_o, 4 * HC)
            sp.wait_ge(full[AT["vnT"][0]], AT["vnT"][1] + 1)
            sp.dma_start(w_out, a["w_o"][0].rearrange("(k p) n -> p k n", p=P)).then_inc(w_o_in, 16)
            wg, wu, wd = (a[n][0].rearrange("g e d f -> (g e) d f") for n in ("w_gate", "w_up", "w_down"))

            def load_expert(e, s):
                sp.dma_start(w_gu[s][0], wg[bass.ds(e, 1)].rearrange("o (p k) f -> p (o k) f", k=DC)).then_inc(gu_in[s][0], 16)
                sp.dma_start(w_gu[s][1], wu[bass.ds(e, 1)].rearrange("o (p k) f -> p (o k) f", k=DC)).then_inc(gu_in[s][1], 16)

            def load_down(e, s):
                sp.dma_start(w_dn[s], wd[bass.ds(e, 1)].rearrange("o (p k) n -> p (o k) n", k=FC)).then_inc(dn_in[s], 16)

            sp.wait_ge(pv_done, CHUNKS)
            load_expert(0, 0)
            sp.wait_ge(wo_full, TILES)
            load_expert(1, 1)
            load_down(1, 1)
            sp.wait_ge(pe_full, TILES)
            load_down(0, 0)
            sp.wait_ge(gu_full, 1)
            load_expert(2, 0)
            with sp.Fori(2, NE // 2) as i:
                for s in range(2):
                    sp.wait_ge(gu_full, i * 2 + (s - 2))
                    load_expert(i * 2 + (s - 1), 1 - s)
                    sp.wait_ge(y_full, i * 2 + (s - 3))
                    load_down(i * 2 + (s - 2), s)
            sp.wait_ge(gu_full, NE - 2)
            load_expert(NE - 1, 1)
            for e in (NE - 2, NE - 1):
                sp.wait_ge(y_full, e - 1)
                load_down(e, e % 2)
            sp.wait_ge(lists_ready, 1)
            sp.wait_ge(y_full, NE)
            n_over = sp.value_load(over_i[0:1, OVER:OVER + 1], min_val=0, max_val=OVER)
            with sp.If(n_over > 0):
                with sp.Fori(0, n_over) as i:
                    e = sp.value_load(over_i[0:1, bass.ds(i, 1)], min_val=0, max_val=NE - 1)
                    sp.wait_ge(ov_y, i + 1)
                    sp.dma_start(w_gu[0][0], wg[bass.ds(e, 1)].rearrange("o (p k) f -> p (o k) f", k=DC)).then_inc(ov_w, 16)
                    sp.dma_start(w_gu[0][1], wu[bass.ds(e, 1)].rearrange("o (p k) f -> p (o k) f", k=DC)).then_inc(ov_w, 16)
                    sp.dma_start(w_dn[0], wd[bass.ds(e, 1)].rearrange("o (p k) n -> p (o k) n", k=FC)).then_inc(ov_w, 16)
            with sp.Else():
                sp.nop()
            sp.wait_ge(moe_done, 1)
            sp.dma_start(w_gate_ple, a["w_ple_gate"][0].rearrange("(k p) n -> p k n", p=P)).then_inc(wpg_in, 16)
            sp.dma_start(g_fin, bc_rows(a["g_final"].rearrange("(a n) -> a n", a=1))).then_inc(gfin_in, 16)
            for t in range(TILES):
                w = tile_width(t)
                if t >= 2:
                    sp.wait_ge(x2_ready, t - 1)
                rows = moe_dram[4 * t * P:4 * (t * P + w), :].rearrange("(p k) d -> p (k d)", k=4)
                sp.dma_start(pairs_in[t % 2][0:w, :], rows).then_inc(pairs_ready[t % 2], 16)
            for t in range(TILES):
                w = tile_width(t)
                sp.wait_ge(y_final, t + 1)
                dst = y_prompt[0, t * P:(t + 1) * P, :] if t < QT else y_sample.rearrange("b l d -> (b l) d")
                sp.dma_start(dst, xn[t % 2][0:w, :]).then_inc(y_stored[t % 2], 16)
            sp.wait_ge(y_stored[0], 48)
            sp.wait_ge(y_stored[1], 32)

        @block.gpsimd
        def _(pool):
            step = Steps(pool, pool_step)
            pool.dma_start(page_id[:, :], a["page_table"].rearrange("b (g o) -> (b g) o", o=1)).then_inc(page_in, 16)

            def select(out, op, fill_value, base, pattern, mult):
                step(pool.affine_select(out=out, in_=out, compare_op=op, fill=fill_value, base=base,
                                        pattern=pattern, channel_multiplier=mult))

            step(pool.memset(ident, 0.0))
            select(ident, ALU.not_equal, 1.0, 0, [[-1, P]], 1)
            step(pool.memset(tri, 1.0))
            select(tri, ALU.is_ge, 0.0, 0, [[1, SEQ]], -1)
            pool.nop().then_inc(consts_built, 1)
            pool.wait_ge(page_in, 16)
            pool.indirect_dma_start(logf_pages.rearrange("p k h -> p (k h)"), None,
                                    a["cache_logf"][0].rearrange("n k h -> n (k h)"),
                                    bass.IndirectOffsetOnAxis(ap=page_id[:, 0:1], axis=0)).then_inc(lf_in, 16)
            step(pool.tensor_copy(page_f, page_id[:, 0:1]))
            for s in range(4):
                step(pool.tensor_scalar(chunk_f[:, s:s + 1], page_f, float(CHUNKS), float(s), ALU.mult, ALU.add))
            caches = [a[n][0].rearrange("n (c k) h d -> (n c) (k h d)", k=KEYS) for n in ("cache_k", "cache_v")]

            def load_chunk(cache, s):
                step(pool.tensor_copy(chunk_id[s][:, 0:1], chunk_f[:, s:s + 1]))
                pool.indirect_dma_start(ring[s], None, caches[cache],
                                        bass.IndirectOffsetOnAxis(ap=chunk_id[s][:, 0:1], axis=0)).then_inc(kv_in[s], 16)
                step(pool.tensor_scalar(chunk_f[:, s:s + 1], chunk_f[:, s:s + 1], 4.0, None, ALU.add))

            for s in range(3):
                load_chunk(0, s)
            step(pool.memset(mask, 0.0))
            select(mask, ALU.is_ge, -BIG, 0, [[-1, P]], 1)
            step(pool.memset(strict, 1.0))
            select(strict, ALU.is_ge, 0.0, -1, [[1, P]], -1)
            lat = later.rearrange("p (b g) -> p b g", b=NB)
            step(pool.memset(later, 1.0))
            select(lat, ALU.is_ge, 0.0, -1, [[-PAGES, NB], [-1, PAGES]], 1)
            select(lat, ALU.is_ge, 0.0, PAGES - 1, [[PAGES, NB], [0, PAGES]], -1)
            rs = row_sel[0:NB, :].rearrange("p (b g) -> p b g", b=NB)
            step(pool.memset(row_sel, 0.0))
            select(rs, ALU.not_equal, 1.0, 0, [[-1, NB], [0, PAGES]], 1)
            step(pool.memset(col_sel, 1.0))
            select(col_sel, ALU.is_ge, 0.0, 0, [[-PAGES, NB]], 1)
            select(col_sel, ALU.is_ge, 0.0, PAGES - 1, [[PAGES, NB]], -1)
            step(pool.iota(iota, pattern=[[1, SLOTS]], base=0, channel_multiplier=0, allow_small_or_imprecise_dtypes=True))
            step(pool.iota(tokid, pattern=[[P, TILES]], base=0, channel_multiplier=1, allow_small_or_imprecise_dtypes=True))
            step(pool.iota(steps, pattern=[[SLOTS, QMAX]], base=SLOTS, channel_multiplier=0, allow_small_or_imprecise_dtypes=True))
            step(pool.memset(half_row, -2.0))
            select(half_row, ALU.is_ge, -1.0, SLOTS - 1, [[0, 1]], -1)
            step(pool.memset(valid, 1.0))
            select(valid[:, QT:TILES], ALU.is_ge, 0.0, NB - 1, [[0, 1]], -1)
            pool.nop().then_inc(consts_built, 1)

            pool.wait_ge(qb_ready, 1)
            q_rep = q_bc.rearrange("p (o n) -> p o n", o=1).to_broadcast([P, KEYS, WC])

            def products(s, count):
                pool.wait_ge(kv_in[s], count)
                r = ring[s].rearrange("p (k n) -> p k n", k=KEYS)
                pool.tensor_tensor(r, r, q_rep, ALU.mult).then_inc(kmul, 1)

            base = step.n
            per = 8
            with pool.Fori(0, CHUNKS // 4 - 1) as i:
                step.off = i * per
                for s in range(4):
                    products(s, i * 16 + 16)
                    pool.wait_ge(kred, i * 4 + (s + 1))
                    alone(pool)
                    load_chunk(0, (s + 3) % 4)
            assert step.n == base + per
            step.n, step.off = base + per * (CHUNKS // 4 - 1), 0
            for s in range(4):
                products(s, 16 * (CHUNKS // 4))
                pool.wait_ge(kred, CHUNKS - 4 + s + 1)
                if s == 0:
                    load_chunk(0, 3)
                    for r in range(4):
                        step(pool.tensor_scalar(chunk_f[:, r:r + 1], page_f, float(CHUNKS), float(r), ALU.mult, ALU.add))
                else:
                    load_chunk(1, s - 1)
            pool.wait_ge(kred, CHUNKS + 1)
            load_chunk(1, 3)
            base = step.n
            with pool.Fori(1, CHUNKS // 4) as i:
                step.off = (i - 1) * per
                for s in range(4):
                    pool.wait_ge(pv_done, i * 4 + (s - 3))
                    alone(pool)
                    load_chunk(1, s)
            step.n, step.off = base + per * (CHUNKS // 4 - 1), 0

            pool.wait_ge(lists_ready, 1)
            pool.wait_ge(h2_stored[0], 48)
            pool.wait_ge(h2_stored[1], 32)
            pool.wait_ge(pe_full, TILES)

            def gather(i, c):
                s, e = c % RING, num(i, c)
                step(pool.tensor_copy(tok_ix[s][0:SLOTS, 0:1], tok_list[0:SLOTS, bass.ds(e, 1)]))
                pool.indirect_dma_start(h_rows[s][0:SLOTS, :], None, h2_dram,
                                        bass.IndirectOffsetOnAxis(ap=tok_ix[s][0:SLOTS, 0:1], axis=0)).then_inc(hg_in[s], 16)

            def scatter(e, s):
                step(pool.tensor_copy(row_ix[s][:, 0:1], row_list[:, bass.ds(e, 1)]))
                return pool.indirect_dma_start(moe_dram, bass.IndirectOffsetOnAxis(ap=row_ix[s][:, 0:1], axis=0),
                                               y_rows[s], None, bounds_check=2 * PAIRS - 1, oob_is_err=False)

            def move_rows(i, c, last=False):
                if not last:
                    pool.wait_ge(hgT_full, num(i, c + 1))
                    if not isinstance(i, int):
                        alone(pool)
                    gather(i, c + RING)
                if exists(i, c - 2):
                    pool.wait_ge(y_copied, num(i, c - 1))
                    if not isinstance(i, int):
                        alone(pool)
                    scatter(num(i, c - 2), (c - 2) % RING).then_inc(y_out[(c - 2) % RING], 16)

            for c in range(RING):
                gather(0, c)
            for c in range(RING):
                move_rows(0, c)
            base = step.n
            with pool.Fori(1, NE // RING - 1) as i:
                step.off = (i - 1) * (2 * RING)
                for c in range(RING):
                    move_rows(i, c)
            step.n, step.off = base + 2 * RING * (NE // RING - 2), 0
            for e in range(NE - RING, NE + 2):
                move_rows(0, e, last=True)
            for s in range(RING):
                pool.wait_ge(y_out[s], 16 * (NE // RING))
            n_over = pool.value_load(over_i[0:1, OVER:OVER + 1], min_val=0, max_val=OVER)
            with pool.If(n_over > 0):
                with pool.Fori(0, n_over) as i:
                    step.off = i * 2
                    step(pool.tensor_copy(tok_ix[0][0:SLOTS, 0:1], tok_list[0:SLOTS, bass.ds(i + NE, 1)]))
                    pool.indirect_dma_start(h_rows[0][0:SLOTS, :], None, h2_dram,
                                            bass.IndirectOffsetOnAxis(ap=tok_ix[0][0:SLOTS, 0:1], axis=0)).then_inc(ov_rows, 16)
                    pool.wait_ge(ov_yc, i + 1)
                    alone(pool)
                    scatter(i + NE, 0).then_inc(ov_out, 16)
                    pool.wait_ge(ov_out, i * 16 + 16)
                step.off = 0
            with pool.Else():
                pool.nop()
            pool.nop().then_inc(moe_done, 1)

        @block.scalar
        def _(act):
            step = Steps(act, act_step)
            for n, (name, rows) in enumerate((("g_mix", 8), ("g_out", 8))):
                act.dma_start(params_nat[8 * n:8 * n + rows, :], a[name][0].rearrange("(c p) -> c p", p=P)).then_inc(rows_in, 16)
            act.dma_start(params_nat[16:22, :], a["conv_w"][0].rearrange("j (c p) -> (j c) p", p=P)).then_inc(rows_in, 16)
            act.dma_start(params_nat[22:30, :], a["g_ple"][0].rearrange("(c p) -> c p", p=P)).then_inc(rows_in, 16)
            w_f = a["w_in"][0].rearrange("(k p) n -> p k n", p=P)[:, :, NM * P:NM * P + HC]
            act.dma_start(w_forget, w_f).then_inc(wf_in, 16)

            def square(t, m):
                w = tile_width(t)
                act.wait_ge(x_in[t], 16)
                act.activation(junk[0:w, :], x[0:w, t, :], ACT.Square, accum_out=stats[0:w, t:t + 1]).then_inc(ms_ready, 1)

            n_consts = [0]

            def const(dst, src):
                n_consts[0] += 1
                act.dma_start(dst, src).then_inc(consts_in, 16)

            const(ws_nat, a["w_s"][0].rearrange("h t s -> t h s"))
            const(bf_bc, bc_rows(a["b_f"]))
            const(ln_g_bc, bc_rows(a["ln_g"]))
            const(ln_b_bc, bc_rows(a["ln_b"]))
            for h in range(4):
                q = (h % 2) * HD
                const(bs_bc[q:q + HD, h // 2, :], bc_rows(a["b_s"][0, h:h + 1, :], HD))
                const(w00[q:q + HD, h // 2:h // 2 + 1], bc_rows(a["w_s"][0, h, 0:1, 0:1], HD))
            const(state[0:NB, :], a["state_conv"][0].rearrange("b j c -> b (j c)"))
            const(b_route[:, 0:NG], bc_rows(a["b_grp"]))
            const(b_route[:, NG:], bc_rows(a["b_rt"].rearrange("l g e -> l (g e)")))
            const(g_ffn_bc, bc_rows(a["g_ffn"]))
            act.dma_start(w_route[:, :, 0:NG], a["w_grp"][0].rearrange("(k p) n -> p k n", p=P)).then_inc(route_w_in, 16)
            act.dma_start(w_route[:, :, NG:], a["w_rt"][0].rearrange("(k p) g e -> p k (g e)", p=P)).then_inc(route_w_in, 16)
            for t in range(TILES):
                if t:
                    act.wait_ge(ms_ready, t)
                square(t, 0)
            act.wait_ge(f_full, 1)
            act.activation(fT[0:HC, :].rearrange("p (a n) -> p a n", a=2), psum[0:HC, 2:4, 0:HALF], ACT.Copy).then_inc(f_free, 1)

            def copy_proj(m, parity, ready):
                act.wait_ge(pj_full, ready)
                dst = projT[:, bass.ds(m, 1), :].rearrange("p o (a n) -> p (o a) n", a=2)
                act.activation(dst, psum[:, 2 * parity:2 * parity + 2, 0:HALF], ACT.Copy).then_inc(pj_free, 1)

            with act.Fori(0, (GROUPS - FIRST) // 2) as i:
                for q in range(4):
                    copy_proj(i * 4 + (MT_Q + q), q % 2, i * 4 + (q + 1))
            wait_full(act, "qs")
            act.activation(q_s[0:NB, :], fill("qs")[0:NB, :], ACT.Copy, scale=SCALE).then_inc(free_of("qs"), 1)
            wait_full(act, "ks")
            act.activation(k_s[0:NB, :], fill("ks")[0:NB, :], ACT.Copy).then_inc(free_of("ks"), 1)
            wait_full(act, "vs")
            act.activation(v_s[0:NB, :], fill("vs")[0:NB, :], ACT.Copy).then_inc(free_of("vs"), 1)
            wait_full(act, "qb")
            act.activation(q_bc, fill("qb"), ACT.Copy).then_inc(free_of("qb"), 1)
            act.wait_ge(free_of("qb"), AT["qb"][1] + 1)
            step(act.activation(stats[0:1, 40:41], stats[0:1, 0:1], ACT.Copy))
            act.nop().then_inc(qb_ready, 1)
            act.wait_ge(free_of("ks"), AT["ks"][1] + 1)
            act.wait_ge(free_of("vs"), AT["vs"][1] + 1)
            act.nop().then_inc(sample_nat, 1)
            flat = "l b t h d -> (l b t) (h d)"
            act.dma_start(k_sample.rearrange(flat), k_s[0:NB, :]).then_inc(out_act, 16)
            act.dma_start(v_sample.rearrange(flat), v_s[0:NB, :]).then_inc(out_act, 16)
            stored = [2]
            act.wait_ge(f_part, 1)
            act.activation(f_b, f_a, ACT.Exp, scale=-1.0).then_inc(f_part, 1)
            act.wait_ge(f_part, 3)
            act.activation(f_d, f_c, ACT.Ln).then_inc(f_part, 1)
            for t in range(QT):
                wait_full(act, f"k{t}")
                if t >= 2:
                    act.wait_ge(kn_out[t % 2], 16)
                act.activation(k_nat[t % 2], fill(f"k{t}"), ACT.Copy).then_inc(free_of(f"k{t}"), 1)
                act.wait_ge(free_of(f"k{t}"), AT[f"k{t}"][1] + 1)
                rows = slice(t * P, (t + 1) * P)
                act.dma_start(k_prompt[0, 0, rows].rearrange("t h d -> t (h d)"), k_nat[t % 2]).then_inc(kn_out[t % 2], 16)
            for t in range(QT):
                act.wait_ge(vn_ready, t + 1)
                act.dma_start(v_prompt[0, 0, t * P:(t + 1) * P].rearrange("t h d -> t (h d)"), v_nat[:, t, :]).then_inc(out_act, 16)
                stored[0] += 1
            act.wait_ge(logf_ready, 1)
            act.dma_start(logf_prompt[0, 0].rearrange("(t p) h -> p t h", p=P), f_nat[:, 0:QT, :]).then_inc(out_act, 16)
            act.dma_start(logf_sample.rearrange("l b t h -> (l b t) h"), f_nat[0:NB, QT, :]).then_inc(out_act, 16)
            stored[0] += 2
            wait_full(act, "ct")
            act.activation(cT[0:HC, :], fill("ct")[0:HC, :], ACT.Copy).then_inc(free_of("ct"), 1)
            act.wait_ge(free_of("ct"), AT["ct"][1] + 1)
            act.nop().then_inc(ct_ready, 1)
            for s in range(2):
                act.wait_ge(kn_out[s], 16 * (QT // 2))

            def copy_ck(h):
                act.wait_ge(ck_full, h + 1)
                if h >= 2:
                    act.wait_ge(a_read, 4 * (h - 1))
                act.activation(ck_bc[h % 2], bank(7), ACT.Copy).then_inc(ck_ready, 1)

            copy_ck(0)
            units = 4 * HC
            for u in range(units + 1):
                if u < units:
                    nk = P * (u % QT + 1)
                    act.wait_ge(a_m, u + 1)
                    act.activation(s_buf[u % 2][:, 0:nk], s_buf[u % 2][:, 0:nk], ACT.Exp, bias=stats[:, 8 + u % 2:9 + u % 2],
                                   accum_out=stats[:, 16 + u % 4:17 + u % 4]).then_inc(a_p, 1)
                if u >= 1:
                    w = u - 1
                    nk = P * (w % QT + 1)
                    act.wait_ge(a_t, w + 1)
                    if w >= 2:
                        act.wait_ge(a_o, w - 1)
                    act.activation(pT_buf[w % 2][:, 0:nk], bank(2 + w % 2)[:, 0:nk], ACT.Copy).then_inc(a_pt, 1)
                if u % QT == 2 and u // QT + 1 < HC:
                    copy_ck(u // QT + 1)

            with act.Fori(0, (FIRST - 1) // 2) as i:
                for q in range(4):
                    copy_proj(i * 4 + q, q % 2, i * 4 + (2 * (GROUPS - FIRST) + q + 1))
            for q in range(2):
                copy_proj(MT_V + q, q, NM - 1 + q)
            wait_full(act, "z")
            step(act.activation(z_p[0:2, :], fill("z")[0:2, 0:WA], ACT.Copy))
            act.activation(z_s[0:NB, :], fill("z")[0:NB, WA:2 * WA], ACT.Copy).then_inc(free_of("z"), 1)
            act.wait_ge(free_of("z"), AT["z"][1] + 1)
            act.dma_start(conv_prompt[0, 0], z_p[0:2, :]).then_inc(out_act, 16)
            act.dma_start(conv_sample[0, :, 0, :], state[0:NB, WA:2 * WA]).then_inc(out_act, 16)
            act.dma_start(conv_sample[0, :, 1, :], z_s[0:NB, :]).then_inc(out_act, 16)
            act.wait_ge(v_ready, TILES)
            act.dma_start(chunk_v_sample.rearrange("l b t c -> (l b t) c"), v_norm[0:NB, QT, :]).then_inc(out_act, 16)
            stored[0] += 4
            for t in range(QT):
                wait_full(act, f"yc{t}")
                act.activation(mixT[:, 4:8, t * P:(t + 1) * P], fill(f"yc{t}").rearrange("p (c n) -> p c n", c=4),
                               ACT.Copy).then_inc(free_of(f"yc{t}"), 1)
            act.wait_ge(mix_ready, 2)
            act.wait_ge(out_act, 16 * stored[0])
            act.activation(squares, mixT[:, 0:4, 0:SEQ], ACT.Square).then_inc(sq_ready, 1)
            wait_full(act, "normB")
            for t in range(QT):
                act.wait_ge(free_of(f"yc{t}"), AT[f"yc{t}"][1] + 1)
            act.activation(squares, mixT[:, 4:8, 0:SEQ], ACT.Square).then_inc(sq_ready, 1)

            act.wait_ge(smp_exp, 1)
            act.activation(scores, scores, ACT.Exp).then_inc(smp_p, 1)
            act.wait_ge(smp_exp, 2)
            act.activation(pnew[0:NB, :], new_s[0:NB, :], ACT.Exp).then_inc(smp_p, 1)
            act.dma_start(w_ple_sb, a["w_ple"][0].rearrange("(k p) n -> p k n", p=P)).then_inc(ple_in, 16)

            def second_norm(t):
                w = tile_width(t)
                act.wait_ge(wo_free, t + 1)
                act.activation(xn[t % 2][0:w, :], x[0:w, t, :], ACT.Square, accum_out=stats[0:w, 24 + t:25 + t]).then_inc(x1_ms, 1)
                act.wait_ge(h2_ready, t + 1)
                act.dma_start(h2_dram[tile_cols(t), :], xn[t % 2][0:w, :]).then_inc(h2_stored[t % 2], 16)
                for s, half in enumerate("ab"):
                    wait_full(act, f"h{t}{half}")
                    if s == 0 and t >= 2:
                        wait_full(act, f"h{t - 2}r")
                    act.activation(h2T[t % 2][:, 4 * s:4 * s + 4, 0:w],
                                   fill(f"h{t}{half}").rearrange("p (c n) -> p c n", c=4)[:, :, 0:w], ACT.Copy)\
                       .then_inc(free_of(f"h{t}{half}"), 1)
                act.wait_ge(free_of(f"h{t}b"), AT[f"h{t}b"][1] + 1)
                act.wait_ge(free_of(f"h{t}a"), AT[f"h{t}a"][1] + 1)
                act.nop().then_inc(h2T_ready, 1)

            act.wait_ge(out_act, 16 * stored[0])
            for t in range(QT):
                if t >= 2:
                    act.wait_ge(h2_stored[t % 2], 16)
                second_norm(t)
            act.wait_ge(mixs_ready, 1)
            step(act.activation(squares_s, mixT[:, 0:4, SEQ:NT], ACT.Square))
            step(act.activation(squares[:, 0, 0:4 * NB].rearrange("p (c n) -> p c n", c=4), mixT[:, 4:8, SEQ:NT], ACT.Square))
            act.nop().then_inc(sq_ready, 1)
            act.wait_ge(h2_stored[0], 32)
            second_norm(QT)
            act.wait_ge(px_ready, CHUNKS)
            act.wait_ge(pv_done, CHUNKS)
            act.dma_start(p_nat[:, 0:QT, :], a["p_prompt"][0, 0].rearrange("(t p) n -> p t n", p=P)).then_inc(ple_in, 16)
            act.dma_start(p_nat[0:NB, QT, :], a["p_sample"][0].rearrange("b l n -> (b l) n")).then_inc(ple_in, 16)
            act.wait_ge(route_exp_in, 1)
            act.activation(eg, eg, ACT.Exp).then_inc(route_exp_out, 1)
            act.wait_ge(route_exp_in, 2)
            act.activation(r5[4], r5[4], ACT.Exp).then_inc(route_exp_out, 1)
            for name, t0, n in (("p01", 0, 2), ("p23", 2, 2), ("p4", 4, 1)):
                wait_full(act, name)
                w = n * P if n == 2 else NB
                act.activation(pT[:, :, t0 * P:t0 * P + w], fill(name).rearrange("p (k n) -> p k n", k=2)[:, :, 0:w],
                               ACT.Copy).then_inc(free_of(name), 1)
            for name in ("p23", "p4"):
                act.wait_ge(free_of(name), AT[name][1] + 1)
            act.nop().then_inc(pT_ready, 1)
            for t in range(TILES):
                w = tile_width(t)
                act.wait_ge(pe_full, t + 1)
                pair = psum[0:w, 2 * (t % 2):2 * (t % 2) + 2, :]
                act.activation(p_emb[0:w, t, :].rearrange("p (a n) -> p a n", a=2), pair, ACT.Copy).then_inc(pe_free, 1)

            def copy_rows(i, c):
                act.wait_ge(hgT_full, num(i, c + 1))
                act.activation(hgT[c % 2].rearrange("p k n -> p (k n)"), bank(4), ACT.Copy).then_inc(hgT_ready, 1)

            def gate(i, c):
                act.wait_ge(gu_full, num(i, c + 1))
                if exists(i, c - 1):
                    act.wait_ge(act_ready, num(i, c))
                act.activation(silu[SLOTS:2 * SLOTS, :], bank(c % 2)[0:SLOTS, :], ACT.Silu).then_inc(silu_ready, 1)

            def copy_y(i, c):
                act.wait_ge(y_full, num(i, c + 1))
                if exists(i, c - RING):
                    act.wait_ge(y_out[c % RING], loads(i, c - RING, RING))
                act.activation(y_rows[c % RING], bank(6 + c % 2), ACT.Copy).then_inc(y_copied, 1)

            def expert(i, c, last=False):
                if not last:
                    copy_rows(i, c + 1)
                gate(i, c)
                if exists(i, c - 1):
                    copy_y(i, c - 1)

            copy_rows(0, 0)
            for e in range(LEAD):
                expert(0, e)
            with act.Fori(1, NE // RING - 1) as i:
                for q in range(RING):
                    expert(i, 1 + q)
            for e in range(NE - RING + 1, NE):
                expert(0, e, last=e == NE - 1)
            copy_y(0, NE - 1)
            n_over = act.value_load(over_i[0:1, OVER:OVER + 1], min_val=0, max_val=OVER)
            with act.If(n_over > 0):
                with act.Fori(0, n_over) as i:
                    act.wait_ge(ov_T, i + 1)
                    act.activation(hgT[0].rearrange("p k n -> p (k n)"), bank(4), ACT.Copy).then_inc(ov_Tc, 1)
                    act.wait_ge(ov_gu, i + 1)
                    act.activation(silu[SLOTS:2 * SLOTS, :], bank(0)[0:SLOTS, :], ACT.Silu).then_inc(ov_silu, 1)
                    act.wait_ge(ov_y, i + 2)
                    act.activation(y_rows[0], bank(6), ACT.Copy).then_inc(ov_yc, 1)
            with act.Else():
                act.nop()
            for t in range(TILES):
                w = tile_width(t)
                act.wait_ge(x2_ready, t + 1)
                if t >= 2:
                    act.wait_ge(y_stored[t % 2], 16 * (t // 2))
                act.activation(xn[t % 2][0:w, :], x[0:w, t, :], ACT.Square, accum_out=stats[0:w, 32 + t:33 + t]).then_inc(x2_ms, 1)
                if t >= 1:
                    finish_gate(act, t - 1)
            finish_gate(act, QT)
            act.wait_ge(out_act, 16 * stored[0])

        @block.tensor
        def _(pe):
            mm = nc.tensor.matmul
            tr = nc.tensor.transpose

            def done(ins, name):
                ins.then_inc(full[AT[name][0]], 1)

            pe.wait_ge(consts_built, 1)
            pe.wait_ge(rows_in, 64)
            done(tr(fill("params")[:, 0:30], params_nat[0:30, :], ident[0:30, 0:30]), "params")
            for t in range(TILES):
                w = tile_width(t)
                pe.wait_ge(xn_ready, t + 1)
                for s, half in enumerate("ab"):
                    name = f"x{t}{half}"
                    wait_free(pe, name)
                    for c in range(4):
                        k = 4 * s + c
                        last = tr(fill(name)[:, c * P:c * P + w], xn[t % 2][0:w, k * P:(k + 1) * P], ident[0:w, 0:w])
                    done(last, name)
                pe.nop().then_inc(xn_used, 1)
            pe.wait_ge(wf_in, 16)
            for s in range(2):
                pe.wait_ge(free[s], AT["x4a" if AT["x4a"][0] == s else "x4b"][1] + 1)
            for s in range(2):
                for k in range(DC):
                    last = mm(psum[0:HC, 2 + s, 0:HALF], w_forget[:, k, :], hT[:, k, s * HALF:(s + 1) * HALF],
                              start=(k == 0), stop=(k == DC - 1))
            last.then_inc(f_full, 1)

            def project(s, q, loaded, copied):
                if q == 0:
                    pe.wait_ge(w_in_s[s], loaded)
                if copied is not None:
                    pe.wait_ge(pj_free, copied)
                for half in range(2):
                    for k in range(DC):
                        last = mm(psum[:, 2 * q + half, 0:HALF], w_ring[s][:, k, q * P:(q + 1) * P],
                                  hT[:, k, half * HALF:(half + 1) * HALF], start=(k == 0), stop=(k == DC - 1))
                last.then_inc(pj_full, 1)

            pe.wait_ge(f_free, 1)
            for s in range(2):
                for q in range(2):
                    project(s, q, 16, None if s == 0 else q + 1)
            with pe.Fori(1, (GROUPS - FIRST) // 2) as i:
                for s in range(2):
                    for q in range(2):
                        project(s, q, i * 16 + 16, i * 4 + (2 * s + q - 1))
            wait_free(pe, "f")
            for t in range(TILES):
                w = tile_width(t)
                last = tr(fill("f")[0:w, t * HC:(t + 1) * HC], fT[0:HC, tile_cols(t)], ident[0:HC, 0:HC])
            done(last, "f")
            pe.wait_ge(pj_free, 2 * (GROUPS - FIRST))

            def natural(name, m, t):
                w = tile_width(t)
                wait_free(pe, name)
                for c in range(4):
                    last = tr(fill(name)[0:w, c * P:(c + 1) * P], projT[:, m + c, tile_cols(t)], ident)
                done(last, name)

            natural("qs", MT_Q, QT)
            natural("ks", MT_K, QT)
            natural("vs", MT_VC, QT)
            wait_free(pe, "qb")
            pe.wait_ge(free_of("qs"), AT["qs"][1] + 1)
            pe.wait_ge(consts_built, 2)
            done(mm(fill("qb"), row_sel[0:NB, :], q_s[0:NB, :], start=True, stop=True), "qb")
            wait_free(pe, "ws")
            pe.wait_ge(consts_in, 16 * 16)
            for h in range(4):
                last = tr(fill("ws")[:, h * P:(h + 1) * P], ws_nat[:, h, :], ident)
            done(last, "ws")
            for t in range(QT):
                natural(f"k{t}", MT_K, t)
                natural(f"v{t}", MT_VC, t)
            wait_free(pe, "suffix")
            pe.wait_ge(suf_ready, 1)
            done(mm(fill("suffix")[:, 0:HC], later, decay[:, PAGE - 1, :], start=True, stop=True), "suffix")
            wait_free(pe, "ct")
            pe.wait_ge(logf_ready, 1)
            for t in range(QT):
                last = mm(fill("ct")[0:HC, t * P:SEQ], f_nat[:, t, :], tri[:, 0:SEQ - t * P], start=(t == 0), stop=(t == QT - 1))
            done(last, "ct")
            wait_free(pe, "newT")
            pe.wait_ge(new_ready, 1)
            done(tr(fill("newT")[0:NB, 0:HC], new_s[0:NB, :], ident[0:NB, 0:NB]), "newT")

            pe.wait_ge(ct_ready, 1)

            def spread_ck(h):
                if h:
                    pe.wait_ge(ck_ready, h)
                mm(bank(7), ident[0:HC, h:h + 1].to_broadcast([HC, P]), cT[0:HC, :], start=True, stop=True).then_inc(ck_full, 1)

            spread_ck(0)
            units = 4 * HC
            for u in range(units + 2):
                if u < units:
                    h, t = u // QT, u % QT
                    c, q0 = h // 2, (h % 2) * HD
                    if u >= 2:
                        pe.wait_ge(a_read, u - 1)
                    mm(bank(u % 2)[:, 0:P * (t + 1)], projT[q0:q0 + HD, MT_Q + c, t * P:(t + 1) * P],
                       projT[q0:q0 + HD, MT_K + c, 0:P * (t + 1)], start=True, stop=True).then_inc(a_s, 1)
                if u % QT == 1 and u // QT + 1 < HC:
                    spread_ck(u // QT + 1)
                if 1 <= u <= units:
                    w = u - 1
                    t = w % QT
                    pe.wait_ge(a_p, w + 1)
                    if w >= 2:
                        pe.wait_ge(a_pt, w - 1)
                    for k in range(t + 1):
                        last = tr(bank(2 + w % 2)[:, k * P:(k + 1) * P], s_buf[w % 2][:, k * P:(k + 1) * P], ident)
                    last.then_inc(a_t, 1)
                if u >= 2:
                    w = u - 2
                    h, t = w // QT, w % QT
                    pe.wait_ge(a_pt, w + 1)
                    if w == 0:
                        pe.wait_ge(vn_ready, QT)
                    if w == 1:
                        pe.wait_ge(free[1], max(n for n, name in ((AT[m][1], m) for m in ("suffix", "ct", "newT")) if AT[name][0]) + 1)
                    if w >= 2:
                        pe.wait_ge(a_of, w - 1)
                    for k in range(t + 1):
                        last = mm(bank(6 - w % 2)[:, 0:HD], pT_buf[w % 2][:, k * P:(k + 1) * P],
                                  v_nat[:, k, h * HD:(h + 1) * HD], start=(k == 0), stop=(k == t))
                    last.then_inc(a_o, 1)

            n0 = GROUPS - FIRST
            pe.wait_ge(a_read, units)
            pe.wait_ge(a_pt, units)
            with pe.Fori(0, (FIRST - 1) // 2) as i:
                for s in range(2):
                    for q in range(2):
                        project(s, q, i * 16 + (16 * (n0 // 2) + 16), i * 4 + (2 * (n0 + s) + q - 1))
            for q in range(2):
                project(0, q, 16 * (GROUPS // 2 + 1), 2 * (GROUPS - 1) + q - 1)
            pe.wait_ge(pj_free, NM)
            pe.wait_ge(a_of, units)
            for name, tiles in (("vn01", (0, 1)), ("vn23", (2, 3)), ("vn4", (4,))):
                wait_free(pe, name)
                for n, t in enumerate(tiles):
                    w = tile_width(t)
                    for c in range(2):
                        last = tr(fill(name)[0:w, n * WB + c * P:n * WB + (c + 1) * P], projT[:, MT_V + c, tile_cols(t)], ident)
                done(last, name)
            wait_free(pe, "vnT")
            pe.wait_ge(v_ready, TILES)
            for c in range(2):
                last = tr(fill("vnT")[:, c * NB:(c + 1) * NB], v_norm[0:NB, QT, c * P:(c + 1) * P], ident[0:NB, 0:NB])
            done(last, "vnT")
            wait_free(pe, "state")
            for c in range(4):
                last = tr(fill("state")[:, c * NB:(c + 1) * NB], state[0:NB, c * P:(c + 1) * P], ident[0:NB, 0:NB])
            done(last, "state")
            wait_free(pe, "z")
            pe.wait_ge(z_ready, 1)
            for c in range(2):
                tr(fill("z")[0:2, c * P:(c + 1) * P], projT[:, 2 + c, SEQ - 2:SEQ], ident)
                last = tr(fill("z")[0:NB, WA + c * P:WA + (c + 1) * P], projT[:, 2 + c, SEQ:NT], ident)
            done(last, "z")
            for hp in range(2):
                name = f"gate{hp}"
                wait_free(pe, name)
                for t in range(QT):
                    for q in range(2):
                        h = 2 * hp + q
                        last = mm(fill(name)[q * HD:(q + 1) * HD, t * P:(t + 1) * P], v_norm[:, t, h * HD:(h + 1) * HD],
                                  wsT[:, h, :], start=True, stop=True)
                done(last, name)
            for t in range(QT):
                wait_free(pe, f"yc{t}")
                for c in range(4):
                    last = tr(fill(f"yc{t}")[:, c * P:(c + 1) * P], y_c[:, t, c * P:(c + 1) * P], ident)
                done(last, f"yc{t}")
            for name, chunks in (("normA", (0, 1)), ("normB", (2, 3)), ("normC", (0, 1, 2, 3))):
                wait_free(pe, name)
                pe.wait_ge(sq_ready, 2 if name == "normC" else 1)
                for n, c in enumerate(chunks):
                    last = mm(fill(name), ones, squares[:, c, :], start=(n == 0), stop=(n == len(chunks) - 1))
                done(last, name)
            for name, need, dst, src in (
                    ("maxT", 1, slice(0, HC), max_p), ("maxB", 2, slice(0, P), m_exp[0:HC, :]),
                    ("maxN", 2, slice(0, NB), mT[0:HC, :])):
                wait_free(pe, name)
                pe.wait_ge(smp_req, need)
                n = src.shape[0]
                done(tr(fill(name)[dst, 0:n], src, ident[0:n, 0:n]), name)
            wait_free(pe, "sum")
            pe.wait_ge(smp_req, 3)
            done(mm(fill("sum")[0:NB, 0:HC], col_sel, sum_p, start=True, stop=True), "sum")

            def mix_out(t):
                w = tile_width(t)
                if t >= 2:
                    pe.wait_ge(wo_free, t - 1)
                for n in range(2):
                    for k in range(DC):
                        last = mm(bank(2 * (t % 2) + n)[0:w, :], mixT[:, k, tile_cols(t)], w_out[:, k, n * BANK:(n + 1) * BANK],
                                  start=(k == 0), stop=(k == DC - 1))
                last.then_inc(wo_full, 1)

            def route(t):
                w = tile_width(t)
                pe.wait_ge(h2_ready, t + 1)
                for s, half in enumerate("ab"):
                    name = f"h{t}{half}"
                    wait_free(pe, name)
                    for c in range(4):
                        k = 4 * s + c
                        last = tr(fill(name)[:, c * P:c * P + w], xn[t % 2][0:w, k * P:(k + 1) * P], ident[0:w, 0:w])
                    done(last, name)
                name = f"h{t}r"
                wait_free(pe, name)
                pe.wait_ge(h2T_ready, t + 1)
                for k in range(DC):
                    last = mm(fill(name)[0:w, 0:NG + NE], h2T[t % 2][:, k, 0:w], w_route[:, k, :], start=(k == 0), stop=(k == DC - 1))
                done(last, name)

            def values(s, loaded, spread, first=False, last_one=False):
                pe.wait_ge(kv_in[s], loaded)
                pe.wait_ge(px_ready, spread)
                for k in range(KEYS):
                    for c in range(4):
                        ins = mm(bank(7)[:, c * 2 * NB:(c + 1) * 2 * NB], ring[s][:, k * WC + c * P:k * WC + (c + 1) * P],
                                 p_exp[s][:, k * HC + 2 * c:k * HC + 2 * c + 2, :],
                                 start=(first and k == 0 and c == 0), stop=(last_one and k == KEYS - 1),
                                 skip_group_check=True)
                ins.then_inc(pv_done, 1)

            k_loads = 16 * (CHUNKS // 4)

            def values_step(i, **flags):
                for s in range(4):
                    values(s, k_loads + 16 * (i + 1), 4 * i + s + 1, flags.get("first", False) and s == 0,
                           flags.get("last_one", False) and s == 3)

            pe.wait_ge(mix_normed, 1)
            pe.wait_ge(w_o_in, 16)
            pe.wait_ge(route_w_in, 32)
            mix_out(0)
            pe.wait_ge(ck_ready, HC)
            values_step(0, first=True)
            values_step(1)
            mix_out(1)
            route(0)
            for t in range(2, QT):
                with pe.Fori(2 * (t - 1), 2 * t) as i:
                    for s in range(4):
                        values(s, i * 16 + (k_loads + 16), i * 4 + (s + 1))
                mix_out(t)
                route(t - 1)
            values_step(6)
            values_step(7, last_one=True)
            route(QT - 1)
            wait_free(pe, "oN")
            pe.wait_ge(smp_req, 4)
            for c in range(4):
                last = tr(fill("oN")[0:NB, c * P:(c + 1) * P], oT[:, c, :], ident)
            done(last, "oN")
            wait_free(pe, "oT")
            pe.wait_ge(smp_req, 5)
            for c in range(4):
                last = tr(fill("oT")[:, c * NB:(c + 1) * NB], prod_s[0:NB, c * P:(c + 1) * P], ident[0:NB, 0:NB])
            done(last, "oT")
            wait_free(pe, "normS")
            pe.wait_ge(sq_ready, 3)
            for g, chunks in enumerate(((0, 1), (2, 3), (4, 5, 6, 7))):
                for n, c in enumerate(chunks):
                    sq = squares_s[:, c, :] if c < 4 else squares[:, 0, (c - 4) * NB:(c - 3) * NB]
                    last = mm(fill("normS")[:, g * NB:(g + 1) * NB], ones, sq, start=(n == 0), stop=(n == len(chunks) - 1))
            done(last, "normS")
            pe.wait_ge(mixs_normed, 1)
            mix_out(QT)
            route(QT)
            wait_free(pe, "rank")
            pe.wait_ge(route_op, 1)
            for t in range(TILES):
                for q in range(t + 1):
                    mm(fill("rank")[:, t * NE:(t + 1) * NE], ones if q < t else strict, chosen[:, q, :], start=(q == 0), stop=(q == t))
            for q in range(TILES):
                last = mm(fill("rank")[:, TILES * NE:(TILES + 1) * NE], ones, chosen[:, q, :], start=(q == 0), stop=(q == QT))
            done(last, "rank")

            pe.wait_ge(ple_in, 48)
            pes = (("p01", (0, 1)), ("p23", (2, 3)), ("p4", (4,)))
            for name, tiles in pes:
                wait_free(pe, name)
                for n, t in enumerate(tiles):
                    w = tile_width(t)
                    for k in range(2):
                        last = tr(fill(name)[:, k * 2 * P + n * P:k * 2 * P + n * P + w], p_nat[0:w, t, k * P:(k + 1) * P],
                                  ident[0:w, 0:w])
                done(last, name)
            pe.wait_ge(pT_ready, 1)
            pe.wait_ge(wo_free, TILES)
            for t in range(TILES):
                w = tile_width(t)
                if t >= 2:
                    pe.wait_ge(pe_free, t - 1)
                for n in range(2):
                    for k in range(2):
                        last = mm(bank(2 * (t % 2) + n)[0:w, :], pT[:, k, tile_cols(t)], w_ple_sb[:, k, n * BANK:(n + 1) * BANK],
                                  start=(k == 0), stop=(k == 1))
                last.then_inc(pe_full, 1)
            wait_free(pe, "list")
            pe.wait_ge(route_op, 2)
            for t in range(TILES):
                for c, one in enumerate((tile_one, tile_one2)):
                    for half in range(2):
                        last = mm(fill("list")[half * SLOTS:(half + 1) * SLOTS, 0:2 * LIST], slot_one[:, c, t, :], one[:, t, :],
                                  start=(t == 0 and c == 0), stop=(t == QT and c == 1))
            done(last, "list")

            pe.wait_ge(pe_free, TILES)
            for name in ("list", "p4"):
                pe.wait_ge(free_of(name), AT[name][1] + 1)

            def rows_T(rows, signal):
                hv = rows.rearrange("t (m k) -> t k m", k=DC)
                for k in range(DC):
                    last = tr(bank(4)[:, k * SLOTS:(k + 1) * SLOTS], hv[0:SLOTS, k, :], ident[0:SLOTS, 0:SLOTS])
                last.then_inc(signal, 1)

            def gate_up(s, signal):
                for k in range(DC):
                    for m in range(2):
                        last = mm(bank(s)[m * SLOTS:(m + 1) * SLOTS, :], hgT[s][:, k, :], w_gu[s][m][:, k, :],
                                  start=(k == 0), stop=(k == DC - 1))
                last.then_inc(signal, 1)

            def act_T(signal):
                av = act_nat.rearrange("t (m k) -> t k m", k=FC)
                for k in range(FC):
                    last = tr(bank(5)[:, k * SLOTS:(k + 1) * SLOTS], av[SLOTS:2 * SLOTS, k, :], ident[SLOTS:2 * SLOTS, SLOTS:2 * SLOTS])
                last.then_inc(signal, 1)

            def down(s, signal):
                for k in range(FC):
                    for n in range(2):
                        last = mm(bank(6 + s)[n * SLOTS:(n + 1) * SLOTS, :], actT[s][:, k, :], w_dn[s][:, k, n * BANK:(n + 1) * BANK],
                                  start=(k == 0), stop=(k == FC - 1))
                last.then_inc(signal, 1)

            def rows_step(i, c):
                pe.wait_ge(hg_in[c % RING], loads(i, c, RING))
                if exists(i, c - 1):
                    pe.wait_ge(hgT_ready, num(i, c))
                if not isinstance(i, int):
                    alone(pe)
                rows_T(h_rows[c % RING], hgT_full)

            def down_step(i, c):
                pe.wait_ge(actT_ready, num(i, c + 1))
                if exists(i, c - 2):
                    pe.wait_ge(y_copied, num(i, c - 1))
                pe.wait_ge(dn_in[c % 2], loads(i, c, 2))
                down(c % 2, y_full)

            def expert(i, c, last=False):
                if not last:
                    rows_step(i, c + 1)
                pe.wait_ge(hgT_ready, num(i, c + 1))
                for m in range(2):
                    pe.wait_ge(gu_in[c % 2][m], loads(i, c, 2))
                gate_up(c % 2, gu_full)
                if exists(i, c - 1):
                    down_step(i, c - 1)
                pe.wait_ge(act_ready, num(i, c + 1))
                if not isinstance(i, int):
                    alone(pe)
                act_T(actT_full)

            rows_step(0, 0)
            for e in range(LEAD):
                expert(0, e)
            with pe.Fori(1, NE // RING - 1) as i:
                for q in range(RING):
                    expert(i, 1 + q)
            for e in range(NE - RING + 1, NE):
                expert(0, e, last=e == NE - 1)
            down_step(0, NE - 1)
            pe.nop().then_inc(ov_y, 1)
            pe.wait_ge(y_copied, NE)
            n_over = pe.value_load(over_i[0:1, OVER:OVER + 1], min_val=0, max_val=OVER)
            with pe.If(n_over > 0):
                with pe.Fori(0, n_over) as i:
                    pe.wait_ge(ov_w, i * 48 + 48)
                    pe.wait_ge(ov_rows, i * 16 + 16)
                    alone(pe)
                    rows_T(h_rows[0], ov_T)
                    pe.wait_ge(ov_Tc, i + 1)
                    gate_up(0, ov_gu)
                    pe.wait_ge(ov_act, i + 1)
                    alone(pe)
                    act_T(ov_aT)
                    pe.wait_ge(ov_aTc, i + 1)
                    down(0, ov_y)
            with pe.Else():
                pe.nop()
            pe.wait_ge(wpg_in, 16)
            for t in range(TILES):
                w = tile_width(t)
                pe.wait_ge(x3_ready, t + 1)
                for s in range(2):
                    if 2 * t + s >= 2:
                        pe.wait_ge(xT_ready, 2 * t + s - 1)
                    for c in range(4):
                        k = 4 * s + c
                        last = tr(bank(4 + s)[:, c * P:c * P + w], xn[t % 2][0:w, k * P:(k + 1) * P], ident[0:w, 0:w])
                    last.then_inc(xT_full, 1)
                pe.wait_ge(xT_ready, 2 * t + 2)
                if t >= 2:
                    pe.wait_ge(pg_sig, t - 1)
                for n in range(2):
                    for k in range(DC):
                        last = mm(bank(2 * (t % 2) + n)[0:w, :], xT[t % 2][:, k, 0:w], w_gate_ple[:, k, n * BANK:(n + 1) * BANK],
                                  start=(k == 0), stop=(k == DC - 1))
                last.then_inc(pg_full, 1)

        @block.vector
        def _(dve):
            step = Steps(dve, dve_step)
            v = nc.vector

            def tell(semaphore):
                dve.nop().then_inc(semaphore, 1)

            def root(dst, src, n):
                few = dst.shape[1] <= NB
                m, y = (r[0:dst.shape[0], 0:dst.shape[1]] for r in ((roots[:, 0, :], roots[:, 1, :]) if few else (root_m, root_y)))
                step(v.tensor_scalar(dst, src, 1.0 / n, EPS, ALU.mult, ALU.add))
                step(v.tensor_scalar(m, dst, -0.5, None, ALU.mult))
                step(v.tensor_scalar(y.bitcast(I32), dst.bitcast(I32), 1, None, ALU.logical_shift_right))
                step(v.tensor_scalar(y.bitcast(I32), y.bitcast(I32), -1, ROOT_GUESS, ALU.mult, ALU.add))
                for last in (False, False, False, True):
                    step(v.tensor_tensor(dst, y, y, ALU.mult))
                    step(v.tensor_tensor(dst, dst, m, ALU.mult))
                    step(v.scalar_tensor_tensor(out=dst if last else y, in0=dst, scalar=1.5, in1=y, op0=ALU.add, op1=ALU.mult))

            tell(kred)
            step(v.memset(f_nat, 0.0))
            wait_full(dve, "params")
            step(v.tensor_copy(params, fill("params")[:, 0:30]))
            dve.nop().then_inc(free_of("params"), 1)

            def norm_rows(t):
                w = tile_width(t)
                dve.wait_ge(ms_ready, t + 1)
                root(stats[0:w, 56 + t:57 + t], stats[0:w, t:t + 1], D)
                if t >= 2:
                    dve.wait_ge(xn_used, t - 1)
                v.tensor_scalar(xn[t % 2][0:w, :], x[0:w, t, :], stats[0:w, 56 + t:57 + t], None, ALU.mult).then_inc(xn_ready, 1)

            def copy_xT(t):
                w = tile_width(t)
                for s, half in enumerate("ab"):
                    name = f"x{t}{half}"
                    wait_full(dve, name)
                    src = fill(name).rearrange("p (c n) -> p c n", c=4)[:, :, 0:w]
                    v.tensor_tensor(hT[:, 4 * s:4 * s + 4, tile_cols(t)], src, inner(params[:, 4 * s:4 * s + 4], w), ALU.mult)\
                     .then_inc(free_of(name), 1)

            for t in range(TILES):
                norm_rows(t)
                if t:
                    copy_xT(t - 1)
            copy_xT(QT)
            wait_full(dve, "f")
            dve.wait_ge(consts_in, 16 * 16)
            step(v.tensor_tensor(f_nat[:, 0:QT, :], fill("f")[:, 0:QT * HC].rearrange("p (t h) -> p t h", h=HC), outer(bf_bc, QT), ALU.add))
            step(v.tensor_tensor(f_nat[0:NB, QT, :], fill("f")[0:NB, QT * HC:TILES * HC], bf_bc[0:NB, :], ALU.add))
            dve.nop().then_inc(free_of("f"), 1)
            step(v.tensor_scalar(f_a, f_nat, -1.0, None, ALU.mult))
            step(v.tensor_tensor(f_a, f_nat, f_a, ALU.max))
            tell(f_part)
            wait_full(dve, "ws")
            v.tensor_tensor(wsT, fill("ws").rearrange("p (h n) -> p h n", h=4), outer(tri[:, 0:P], 4), ALU.mult)\
             .then_inc(free_of("ws"), 1)
            dve.wait_ge(f_part, 2)
            step(v.tensor_scalar(f_c, f_b, 1.0, None, ALU.add))
            tell(f_part)
            step(v.tensor_scalar(f_a, f_c, -1.0, None, ALU.add))
            dve.wait_ge(f_part, 4)
            step(v.tensor_scalar(f_c, f_a, 0.0, None, ALU.is_equal))
            step(v.tensor_tensor(f_a, f_a, f_c, ALU.add))
            step(v.reciprocal(f_a, f_a))
            step(v.tensor_tensor(f_d, f_d, f_b, ALU.mult))
            step(v.tensor_tensor(f_d, f_d, f_a, ALU.mult))
            step(v.tensor_tensor(f_c, f_c, f_b, ALU.mult))
            step(v.tensor_tensor(f_d, f_d, f_c, ALU.add))
            step(v.scalar_tensor_tensor(out=f_nat, in0=f_nat, scalar=0.0, in1=f_d, op0=ALU.min, op1=ALU.subtract))
            tell(logf_ready)
            dve.wait_ge(sample_nat, 1)
            step(v.tensor_tensor(prod_s[0:NB, :], q_s[0:NB, :], k_s[0:NB, :], ALU.mult))
            step(v.tensor_reduce(new_s[0:NB, :], prod_s[0:NB, :].rearrange("p (h d) -> p h d", h=HC), AX.X, ALU.add))
            step(v.tensor_tensor(new_s[0:NB, :], new_s[0:NB, :], f_nat[0:NB, QT, :], ALU.subtract))
            tell(new_ready)
            for t in range(QT):
                wait_full(dve, f"v{t}")
                step(v.tensor_copy(v_nat[:, t, :], fill(f"v{t}")))
                dve.nop().then_inc(free_of(f"v{t}"), 1)
                tell(vn_ready)
            dve.wait_ge(lf_in, 16)
            for h in range(HC):
                ins = v.tensor_tensor_scan(decay[:, :, h], ones, logf_pages[:, :, h], 0.0, ALU.mult, ALU.add)
                step(ins)
            tell(suf_ready)
            wait_full(dve, "suffix")
            step(v.tensor_tensor(page_suf, fill("suffix")[:, 0:HC], decay[:, PAGE - 1, :], ALU.add))
            dve.nop().then_inc(free_of("suffix"), 1)
            step(v.tensor_tensor(decay, outer(page_suf, PAGE), decay, ALU.subtract))
            wait_full(dve, "newT")
            v.tensor_copy(newT_s[0:HC, :], fill("newT")[0:HC, 0:NB]).then_inc(free_of("newT"), 1)

            def reduce_keys(s, chunk_words, ready):
                dve.wait_ge(kmul, ready)
                v.tensor_reduce(chunk_words, ring[s].rearrange("p (a d) -> p a d", d=HD), AX.X, ALU.add).then_inc(kred, 1)

            units = 4 * HC
            for u in range(units + 3):
                if u < units:
                    h, t = u // QT, u % QT
                    nk = P * (t + 1)
                    sb = s_buf[u % 2]
                    dve.wait_ge(a_s, u + 1)
                    dve.wait_ge(ck_ready, h + 1)
                    if u >= 2:
                        dve.wait_ge(a_t, u - 1)
                    v.scalar_tensor_tensor(out=sb[:, 0:nk], in0=bank(u % 2)[:, 0:nk], scalar=SCALE, in1=ck_bc[h % 2][:, 0:nk],
                                           op0=ALU.mult, op1=ALU.subtract).then_inc(a_read, 1)
                    dve.wait_ge(a_read, u + 1)
                    step(v.tensor_tensor(sb[:, nk - P:nk], sb[:, nk - P:nk], mask, ALU.add))
                    v.tensor_reduce(stats[:, 8 + u % 2:9 + u % 2], sb[:, 0:nk], AX.X, ALU.max, negate=True).then_inc(a_m, 1)
                if u >= 3:
                    w = u - 3
                    h, t = w // QT, w % QT
                    dve.wait_ge(a_o, w + 1)
                    if w >= 2:
                        dve.wait_ge(a_of, w - 1)
                    step(v.reciprocal(stats[:, 20 + w % 2:21 + w % 2], stats[:, 16 + w % 4:17 + w % 4]))
                    v.tensor_scalar(y_c[:, t, h * HD:(h + 1) * HD], bank(6 - w % 2)[:, 0:HD], stats[:, 20 + w % 2:21 + w % 2], None,
                                    ALU.mult).then_inc(a_of, 1)
                if u % 4 == 3 and u < units:
                    j = u // 4
                    reduce_keys(j % 4, scores[:, j * KEYS * HC:(j + 1) * KEYS * HC], j + 1)
            with dve.Fori(2, CHUNKS // 4) as i:
                for s in range(4):
                    reduce_keys(s, scores[:, bass.ds(i * (4 * KEYS * HC) + s * KEYS * HC, KEYS * HC)], i * 4 + (s + 1))

            for name, tiles in (("vn01", (0, 1)), ("vn23", (2, 3)), ("vn4", (4,))):
                wait_full(dve, name)
                for n, t in enumerate(tiles):
                    w = tile_width(t)
                    src = fill(name)[0:w, n * WB:(n + 1) * WB]
                    step(v.bn_stats(bn[0:w, :], src))
                    step(v.bn_aggr(mv[0:w, :], bn[0:w, :]))
                    root(mv[0:w, 1:2], mv[0:w, 1:2], 1)
                    step(v.tensor_scalar(v_norm[0:w, t, :], src, mv[0:w, 0:1], mv[0:w, 1:2], ALU.subtract, ALU.mult))
                    if n == len(tiles) - 1:
                        dve.nop().then_inc(free_of(name), 1)
                    step(v.tensor_tensor(v_norm[0:w, t, :], v_norm[0:w, t, :], ln_g_bc[0:w, :], ALU.mult))
                    step(v.tensor_tensor(v_norm[0:w, t, :], v_norm[0:w, t, :], ln_b_bc[0:w, :], ALU.add))
                    tell(v_ready)
            wait_full(dve, "vnT")
            for hp in range(2):
                step(v.tensor_scalar(gate_s[:, hp, :], fill("vnT")[:, hp * NB:(hp + 1) * NB], w00[:, hp:hp + 1], bs_bc[:, hp, 0:1],
                                     ALU.mult, ALU.add))
            dve.nop().then_inc(free_of("vnT"), 1)
            step(v.tensor_tensor(mixT[:, 2:4, SEQ:NT], gate_s, projT[:, MT_U:MT_U + 2, SEQ:NT], ALU.mult))
            z = projT[:, 2:4, :]
            step(v.tensor_tensor(z, z, projT[:, 4:6, :], ALU.mult))
            tell(z_ready)
            wait_full(dve, "state")

            def tap(j, c):
                return params[:, 16 + 2 * j + c:17 + 2 * j + c]

            for c in range(2):
                y = mixT[:, c, :]
                step(v.tensor_scalar(y, z[:, c, :], tap(2, c), None, ALU.mult))
                for j in (1, 0):
                    d = 2 - j
                    step(v.scalar_tensor_tensor(out=y[:, d:SEQ], in0=z[:, c, 0:SEQ - d], scalar=tap(j, c), in1=y[:, d:SEQ],
                                                op0=ALU.mult, op1=ALU.add))
                    step(v.scalar_tensor_tensor(out=y[:, SEQ:NT], in0=fill("state")[:, (2 * j + c) * NB:(2 * j + c + 1) * NB],
                                                scalar=tap(j, c), in1=y[:, SEQ:NT], op0=ALU.mult, op1=ALU.add))
            dve.nop().then_inc(free_of("state"), 1)
            step(v.tensor_tensor(mixT[:, 0:2, :], mixT[:, 0:2, :], projT[:, 0:2, :], ALU.mult))
            tell(mix_ready)
            for hp in range(2):
                wait_full(dve, f"gate{hp}")
                y = mixT[:, 2 + hp, 0:SEQ]
                step(v.tensor_tensor(y.rearrange("p (t n) -> p t n", t=QT), fill(f"gate{hp}").rearrange("p (t n) -> p t n", t=QT),
                                     outer(bs_bc[:, hp, :], QT), ALU.add))
                dve.nop().then_inc(free_of(f"gate{hp}"), 1)
                step(v.tensor_tensor(y, y, projT[:, MT_U + hp, 0:SEQ], ALU.mult))
            tell(mix_ready)
            for name, width, chunks in (("normA", WA, (0, 1)), ("normB", WB, (2, 3)), ("normC", WC, (4, 5, 6, 7))):
                wait_full(dve, name)
                root(rms_bc, fill(name), width)
                dve.nop().then_inc(free_of(name), 1)
                for c in chunks:
                    ins = v.scalar_tensor_tensor(out=mixT[:, c, 0:SEQ], in0=mixT[:, c, 0:SEQ], scalar=params[:, 8 + c:9 + c],
                                                 in1=rms_bc, op0=ALU.mult, op1=ALU.mult)
                    step(ins)
            tell(mix_normed)

            dve.wait_ge(kred, CHUNKS + 1)
            s3 = scores.rearrange("p (k h) -> p k h", h=HC)
            by_head = scores.rearrange("p (k h) -> p h k", h=HC)
            step(v.tensor_tensor(s3, s3, decay, ALU.add))
            step(v.tensor_reduce(max_p, by_head, AX.X, ALU.max))
            tell(smp_req)
            wait_full(dve, "maxT")
            step(v.tensor_reduce(mT[0:HC, :], fill("maxT")[0:HC, 0:P].rearrange("p (b g) -> p b g", b=NB), AX.X, ALU.max))
            dve.nop().then_inc(free_of("maxT"), 1)
            step(v.tensor_tensor(mT[0:HC, :], mT[0:HC, :], newT_s[0:HC, :], ALU.max))
            step(v.tensor_copy(m_exp[0:HC, :].rearrange("p (b g) -> p b g", b=NB), inner(mT[0:HC, :], PAGES)))
            tell(smp_req)
            wait_full(dve, "maxB")
            step(v.tensor_copy(max_b, fill("maxB")[:, 0:HC]))
            dve.nop().then_inc(free_of("maxB"), 1)
            step(v.tensor_tensor(s3, s3, outer(max_b, PAGE), ALU.subtract))
            tell(smp_exp)
            wait_full(dve, "maxN")
            step(v.tensor_tensor(new_s[0:NB, :], new_s[0:NB, :], fill("maxN")[0:NB, 0:HC], ALU.subtract))
            dve.nop().then_inc(free_of("maxN"), 1)
            tell(smp_exp)
            dve.wait_ge(smp_p, 1)
            step(v.tensor_reduce(sum_p, by_head, AX.X, ALU.add))
            tell(smp_req)

            def spread_p(s, words, used):
                if used is not None:
                    dve.wait_ge(pv_done, used)
                v.tensor_tensor(p_exp[s], inner(words, NB), outer(col_sel, KEYS * HC), ALU.mult).then_inc(px_ready, 1)

            W = KEYS * HC

            def spread_step(i):
                for s in range(4):
                    spread_p(s, scores[:, (4 * i + s) * W:(4 * i + s + 1) * W], 4 * i + s - 3 if i else None)

            def add_out(t):
                w = tile_width(t)
                dve.wait_ge(wo_full, t + 1)
                pair = psum[0:w, 2 * (t % 2):2 * (t % 2) + 2, :]
                v.tensor_tensor(x[0:w, t, :].rearrange("p (a n) -> p a n", a=2), x[0:w, t, :].rearrange("p (a n) -> p a n", a=2), pair,
                                ALU.add).then_inc(wo_free, 1)

            def second_norm(t):
                w = tile_width(t)
                dve.wait_ge(x1_ms, t + 1)
                root(stats[0:w, 56:57], stats[0:w, 24 + t:25 + t], D)
                v.scalar_tensor_tensor(out=xn[t % 2][0:w, :], in0=x[0:w, t, :], scalar=stats[0:w, 56:57], in1=g_ffn_bc[0:w, :],
                                       op0=ALU.mult, op1=ALU.mult).then_inc(h2_ready, 1)

            def take_logits(t):
                w = tile_width(t)
                wait_full(dve, f"h{t}r")
                v.tensor_tensor(logits[0:w, t, :], fill(f"h{t}r")[0:w, 0:NG + NE], b_route[0:w, :], ALU.add)\
                 .then_inc(free_of(f"h{t}r"), 1)

            step(v.memset(logits, 0.0))
            spread_step(0)
            wait_full(dve, "sum")
            dve.wait_ge(smp_p, 2)
            step(v.tensor_tensor(sum_s[0:NB, :], fill("sum")[0:NB, 0:HC], pnew[0:NB, :], ALU.add))
            dve.nop().then_inc(free_of("sum"), 1)
            step(v.reciprocal(sum_s[0:NB, :], sum_s[0:NB, :]))
            add_out(0)
            second_norm(0)
            spread_step(1)
            add_out(1)
            second_norm(1)
            take_logits(0)
            for t in range(2, QT):
                with dve.Fori(2 * (t - 1), 2 * t) as i:
                    for s in range(4):
                        spread_p(s, scores[:, bass.ds(i * (4 * W) + s * W, W)], i * 4 + (s - 3))
                add_out(t)
                second_norm(t)
                take_logits(t - 1)
            spread_step(6)
            spread_step(7)
            take_logits(QT - 1)
            dve.wait_ge(pv_done, CHUNKS)
            pv = bank(7)[:, 0:4 * 2 * NB].rearrange("p (c q b) -> p c q b", c=4, q=2)
            step(v.tensor_copy(oT[0:HD, :, :], pv[0:HD, :, 0, :]))
            step(v.tensor_copy(oT[HD:P, :, :], pv[HD:P, :, 1, :]))
            tell(smp_req)
            q3, v3, o3 = (m[0:NB, :].rearrange("p (h d) -> p h d", h=HC) for m in (q_s, v_s, prod_s))
            step(v.tensor_tensor(q3, v3, inner(pnew[0:NB, :], HD), ALU.mult))
            wait_full(dve, "oN")
            step(v.tensor_tensor(prod_s[0:NB, :], fill("oN")[0:NB, :], q_s[0:NB, :], ALU.add))
            dve.nop().then_inc(free_of("oN"), 1)
            step(v.tensor_tensor(o3, o3, inner(sum_s[0:NB, :], HD), ALU.mult))
            tell(smp_req)
            wait_full(dve, "oT")
            step(v.tensor_copy(mixT[:, 4:8, SEQ:NT], fill("oT")[:, 0:4 * NB].rearrange("p (c b) -> p c b", c=4)))
            dve.nop().then_inc(free_of("oT"), 1)
            tell(mixs_ready)
            wait_full(dve, "normS")
            for g, (width, chunks) in enumerate(((WA, (0, 1)), (WB, (2, 3)), (WC, (4, 5, 6, 7)))):
                root(rms_bc[:, g * NB:(g + 1) * NB], fill("normS")[:, g * NB:(g + 1) * NB], width)
                for c in chunks:
                    step(v.scalar_tensor_tensor(out=mixT[:, c, SEQ:NT], in0=mixT[:, c, SEQ:NT], scalar=params[:, 8 + c:9 + c],
                                                in1=rms_bc[:, g * NB:(g + 1) * NB], op0=ALU.mult, op1=ALU.mult))
            dve.nop().then_inc(free_of("normS"), 1)
            tell(mixs_normed)
            add_out(QT)
            second_norm(QT)
            take_logits(QT)
            dve.wait_ge(free_of(f"h{QT}r"), AT[f"h{QT}r"][1] + 1)

            def first_of(one, scratch, index, src, top_value, n):
                step(v.tensor_tensor(scratch, src, inner(top_value, n), ALU.is_equal))
                step(v.tensor_scalar(scratch, scratch, -1.0, -BIG, ALU.add, ALU.mult))
                step(v.tensor_tensor(scratch, scratch, outer(iota[:, 0:n], TILES), ALU.add))
                step(v.tensor_reduce(index, scratch, AX.X, ALU.min))
                step(v.tensor_tensor(one, outer(iota[:, 0:n], TILES), inner(index, n), ALU.is_equal))

            grp, exp_ = logits[:, :, 0:NG], logits[:, :, NG:]
            g_top, g_idx, g_sum, p_g, gap, l1, l2, share, q_num, r_pos, base_e, t_num = r5
            step(v.tensor_reduce(g_top, grp, AX.X, ALU.max))
            step(v.tensor_tensor(eg, grp, inner(g_top, NG), ALU.subtract))
            tell(route_exp_in)
            first_of(g_one, gcand, g_idx, grp, g_top, NG)
            by_group = "p t (g e) -> p t g e"
            step(v.tensor_scalar(gcand, g_one, -1.0, BIG, ALU.add, ALU.mult))
            for t in range(TILES):
                dst = masked[:, t, :].rearrange("p (g e) -> p g e", g=NG)
                src = exp_[:, t, :].rearrange("p (g e) -> p g e", g=NG)
                step(v.tensor_tensor(dst, src, inner(g_one[:, t, :], NE // NG), ALU.mult))
                step(v.tensor_tensor(dst, dst, inner(gcand[:, t, :], NE // NG), ALU.add))
            step(v.tensor_reduce(l1, masked, AX.X, ALU.max))
            first_of(e_one[0], cand, e_idx[0], masked, l1, NE)
            step(v.tensor_scalar(cand, e_one[0], -BIG, None, ALU.mult))
            step(v.tensor_tensor(m2, masked, cand, ALU.add))
            step(v.tensor_reduce(l2, m2, AX.X, ALU.max))
            first_of(e_one[1], cand, e_idx[1], m2, l2, NE)
            step(v.tensor_tensor(gap, l2, l1, ALU.subtract))
            tell(route_exp_in)
            for e in e_one:
                step(v.tensor_tensor(e, e, inner(valid, NE), ALU.mult))
            step(v.tensor_tensor(chosen, e_one[0], e_one[1], ALU.add))
            tell(route_op)
            dve.wait_ge(route_exp_out, 2)
            step(v.tensor_reduce(g_sum, eg, AX.X, ALU.add))
            step(v.tensor_scalar(share, gap, 1.0, None, ALU.add))
            step(v.tensor_tensor(share, share, g_sum, ALU.mult))
            step(v.reciprocal(w_keep[0], share))
            step(v.tensor_tensor(w_keep[1], w_keep[0], gap, ALU.mult))
            wait_full(dve, "rank")
            step(v.tensor_copy(rank, fill("rank")[:, 0:TILES * NE].rearrange("p (t e) -> p t e", e=NE)))
            step(v.tensor_copy(count, fill("rank")[:, TILES * NE:(TILES + 1) * NE]))
            dve.nop().then_inc(free_of("rank"), 1)
            step(v.tensor_tensor(cmp8, inner(count, QMAX), outer(steps, NE), ALU.is_gt))
            step(v.tensor_reduce(tiles_over, cmp8, AX.X, ALU.add))
            step(v.tensor_tensor_scan(over_end, ones[:, 0:NE], tiles_over, 0.0, ALU.mult, ALU.add))
            step(v.tensor_tensor(over_base, over_end, tiles_over, ALU.subtract))
            for c, (one, tiles) in enumerate(zip(e_one, (tile_one, tile_one2))):
                step(v.tensor_tensor(prod_r, rank, one, ALU.mult))
                step(v.tensor_reduce(r_pos, prod_r, AX.X, ALU.add))
                step(v.tensor_tensor(prod_r, outer(over_base, TILES), one, ALU.mult))
                step(v.tensor_reduce(base_e, prod_r, AX.X, ALU.add))
                step(v.tensor_tensor(cmp5, inner(r_pos, QMAX), outer(steps, TILES), ALU.is_ge))
                step(v.tensor_reduce(q_num, cmp5, AX.X, ALU.add))
                step(v.scalar_tensor_tensor(out=r_pos, in0=q_num, scalar=-float(SLOTS), in1=r_pos, op0=ALU.mult, op1=ALU.add))
                step(v.tensor_tensor(slot_one[:, c, :, :], outer(iota, TILES), inner(r_pos, SLOTS), ALU.is_equal))
                step(v.tensor_tensor(base_e, base_e, q_num, ALU.add))
                step(v.tensor_scalar(base_e, base_e, float(NE - 1), None, ALU.add))
                step(v.tensor_tensor(base_e, base_e, e_idx[c], ALU.subtract))
                step(v.tensor_scalar(t_num, q_num, 0.0, None, ALU.is_gt))
                step(v.tensor_tensor(t_num, t_num, base_e, ALU.mult))
                step(v.tensor_tensor(t_num, t_num, e_idx[c], ALU.add))
                hit = tiles[:, :, 0:LIST]
                step(v.tensor_tensor(hit, outer(iota[:, 0:LIST], TILES), inner(t_num, LIST), ALU.is_equal))
                step(v.tensor_tensor(hit, hit, inner(valid, LIST), ALU.mult))
                step(v.tensor_tensor(tiles[:, :, LIST:], hit, inner(tokid, LIST), ALU.mult))
                step(v.tensor_scalar(share, tokid, 2.0, float(c + 1), ALU.mult, ALU.add))
                step(v.tensor_tensor(hit, hit, inner(share, LIST), ALU.mult))
            tell(route_op)
            step(v.tensor_tensor(cmp_over, outer(over_end, OVER), inner(iota[:, 0:OVER], NE), ALU.is_le))
            step(v.tensor_reduce(over_f[:, 0:OVER], cmp_over, AX.X, ALU.add))
            step(v.tensor_scalar(over_f[:, 0:OVER], over_f[:, 0:OVER], float(NE - 1), None, ALU.min))
            step(v.tensor_copy(over_f[:, OVER:OVER + 1], over_end[:, NE - 1:NE]))
            step(v.tensor_copy(over_i[:, 0:OVER + 1], over_f))
            wait_full(dve, "list")
            step(v.tensor_copy(list_f, fill("list")[:, 0:2 * LIST]))
            dve.nop().then_inc(free_of("list"), 1)
            step(v.tensor_copy(tok_list[:, :], list_f[:, LIST:]))
            step(v.tensor_scalar(list_f[:, LIST:], list_f[:, 0:LIST], 0.0, float(4 * PAIRS), ALU.is_equal, ALU.mult))
            step(v.tensor_scalar(list_f[:, 0:LIST], list_f[:, 0:LIST], 2.0, half_row, ALU.mult, ALU.add))
            step(v.tensor_tensor(list_f[:, 0:LIST], list_f[:, 0:LIST], list_f[:, LIST:], ALU.add))
            step(v.tensor_copy(row_list[:, :], list_f[:, 0:LIST]))
            dve.nop().then_inc(lists_ready, 1)

            upper = slice(SLOTS, 2 * SLOTS)

            def activate(i, c):
                dve.wait_ge(silu_ready, num(i, c + 1))
                if exists(i, c - 1):
                    dve.wait_ge(actT_full, num(i, c))
                v.tensor_tensor(act_nat[upper, :], silu[upper, :], bank(c % 2)[upper, :], ALU.mult).then_inc(act_ready, 1)
                dve.wait_ge(actT_full, num(i, c + 1))
                if exists(i, c - 2):
                    dve.wait_ge(y_full, num(i, c - 1))
                v.tensor_copy(actT[c % 2].rearrange("p k n -> p (k n)"), bank(5)[:, 0:FC * SLOTS]).then_inc(actT_ready, 1)

            for e in range(LEAD):
                activate(0, e)
            with dve.Fori(1, NE // RING - 1) as i:
                for q in range(RING):
                    activate(i, 1 + q)
            for e in range(NE - RING + 1, NE):
                activate(0, e)
            n_over = dve.value_load(over_i[0:1, OVER:OVER + 1], min_val=0, max_val=OVER)
            with dve.If(n_over > 0):
                with dve.Fori(0, n_over) as i:
                    dve.wait_ge(ov_silu, i + 1)
                    v.tensor_tensor(act_nat[upper, :], silu[upper, :], bank(0)[upper, :], ALU.mult).then_inc(ov_act, 1)
                    dve.wait_ge(ov_aT, i + 1)
                    v.tensor_copy(actT[0].rearrange("p k n -> p (k n)"), bank(5)[:, 0:FC * SLOTS]).then_inc(ov_aTc, 1)
            with dve.Else():
                dve.nop()

            def add_experts(t):
                w = tile_width(t)
                dve.wait_ge(pairs_ready[t % 2], 16 * (t // 2 + 1))
                for c in range(2):
                    step(v.scalar_tensor_tensor(out=x[0:w, t, :], in0=pairs_in[t % 2][0:w, c * D:(c + 1) * D],
                                                scalar=w_keep[c][0:w, t:t + 1], in1=x[0:w, t, :], op0=ALU.mult, op1=ALU.add))
                tell(x2_ready)
                dve.wait_ge(x2_ms, t + 1)
                root(stats[0:w, 57:58], stats[0:w, 32 + t:33 + t], D)
                v.tensor_scalar(xn[t % 2][0:w, :], x[0:w, t, :], stats[0:w, 57:58], None, ALU.mult).then_inc(x3_ready, 1)
                for s in range(2):
                    dve.wait_ge(xT_full, 2 * t + s + 1)
                    src = bank(4 + s).rearrange("p (c n) -> p c n", c=4)[:, :, 0:w]
                    v.tensor_tensor(xT[t % 2][:, 4 * s:4 * s + 4, 0:w], src, inner(params[:, 22 + 4 * s:26 + 4 * s], w), ALU.mult)\
                     .then_inc(xT_ready, 1)

            def finish(t):
                w = tile_width(t)
                dve.wait_ge(pg_sig, t + 1)
                g = ple_gate[t % 2][0:w, :]
                step(v.tensor_tensor(g, g, p_emb[0:w, t, :], ALU.mult))
                step(v.tensor_tensor(x[0:w, t, :], x[0:w, t, :], g, ALU.add))
                tell(x4_ready)
                dve.wait_ge(x4_ms, t + 1)
                root(stats[0:w, 58:59], stats[0:w, 48 + t:49 + t], D)
                v.scalar_tensor_tensor(out=xn[t % 2][0:w, :], in0=x[0:w, t, :], scalar=stats[0:w, 58:59], in1=g_fin[0:w, :],
                                       op0=ALU.mult, op1=ALU.mult).then_inc(y_final, 1)

            dve.wait_ge(gfin_in, 16)
            for t in range(TILES):
                add_experts(t)
                if t:
                    finish(t - 1)
            finish(QT)


INPUTS = ["x_prompt", "x_sample", "p_prompt", "p_sample", "cache_k", "cache_v", "cache_logf", "state_conv", "page_table",
          "g_mix", "w_in", "conv_w", "ln_g", "ln_b", "w_s", "b_s", "b_f", "g_out", "w_o", "g_ffn", "w_grp", "b_grp",
          "w_rt", "b_rt", "w_gate", "w_up", "w_down", "g_ple", "w_ple", "w_ple_gate", "g_final"]
OUTPUTS = [(1, SEQ, D), (NB, 1, D), (1, 1, SEQ, HC, HD), (1, 1, SEQ, HC, HD), (1, 1, SEQ, HC), (1, 1, 2, WA),
           (1, NB, 1, HC, HD), (1, NB, 1, HC, HD), (1, NB, 1, HC), (1, NB, 2, WA), (1, NB, 1, WB)]


def kernel(**inputs):
    import numpy as _np
    import concourse.bacc as _bacc
    from concourse.bass_utils import run_bass_kernel_spmd as _run

    nc = _bacc.Bacc("TRN2", target_bir_lowering=False, num_devices=1)
    arrays, a = {}, {}
    for name in INPUTS:
        arrays[f"in_{name}"] = _np.ascontiguousarray(inputs[name])
        dt = mybir.dt.from_np(arrays[f"in_{name}"].dtype)
        a[name] = nc.dram_tensor(f"in_{name}", arrays[f"in_{name}"].shape, dt, kind="ExternalInput").ap()
    o = [nc.dram_tensor(f"out_{i}", shape, F32, kind="ExternalOutput").ap() for i, shape in enumerate(OUTPUTS)]
    build(nc, a, o)
    r = _run(nc, [arrays], core_ids=[0])
    return tuple(r.results[0][f"out_{i}"] for i in range(len(OUTPUTS)))
```

```python
from contextlib import ExitStack

import concourse.bass as bass
from concourse import mybir

F32 = mybir.dt.float32
I32 = mybir.dt.int32
ALU = mybir.AluOpType
ACT = mybir.ActivationFunctionType
AX = mybir.AxisListType

P = 128
BANK = 512
D = 1024
DC = D // P
SEQ, NB = 512, 8
NT = SEQ + NB
QT = SEQ // P
TILES = QT + 1
HALF = NT // 2
WA, WB, WC, HC, HD = 256, 256, 512, 8, 64
MT_A, MT_U, MT_V, MT_Q, MT_K, MT_VC = 0, 6, 8, 10, 14, 18
NM = 22
GROUPS = NM // 2
FIRST = MT_Q // 2
PAGE, PAGES = 128, 16
EARLY = 8
KEYS = 4
CHUNKS = PAGE // KEYS
CW = KEYS * WC
NE, NG, DE = 32, 4, 512
FC = DE // P
SLOTS = 64
PAIRS = 2 * NT
OVER = (PAIRS - 2) // SLOTS
LIST = 50
QMAX = NT // SLOTS
RING = 4
DP = 256
EPS = 1e-6
BIG = 1.0e30
SCALE = HD ** -0.5
ROOT_GUESS = 0x5F3759DF

LEAD = RING + 1

GATE_HEAD = 2
LAST = [QT] + list(range(QT))

assert WA == WB and NE + OVER < LIST and HALF * 2 == NT


def tile_width(t):
    return P if t < QT else NB


def tile_cols(t):
    return slice(t * P, t * P + tile_width(t))


FILLS = (["params"] + [f"x{t}{s}" for t in range(TILES) for s in "ab"]
         + ["qs", "qb", "f", "ws", "ks", "vs", "suffix", "ct"] + [f"{n}{t}" for t in range(QT) for n in "kv"]
         + ["newT"]
         + [f"yc{t}" for t in range(QT)] + ["state", "vnT", "z", "gate0", "gate1"]
         + ["normC", "normA", "normB", "maxT", "maxB", "maxN"]
         + ["sum"] + [f"h{t}{s}" for t in (0, 1) for s in "abr"] + ["oN", "oT"] + [f"h2{s}" for s in "abr"] + ["normS"]
         + ["p01", "p23", "p4"] + [f"h{t}{s}" for t in (4, 3) for s in "abr"]
         + ["rank", "list"])
TURN = {0: 0, 1: 1, 2: 2, 4: 3, 3: 4}
NORMS = {"normC": (0, (4, 5, 6, 7)), "normA": (1, (0, 1)), "normB": (2, (2, 3))}
AT = {name: (n % 2, n // 2) for n, name in enumerate(FILLS)}


def build(nc, a, o):
    (y_prompt, y_sample, k_prompt, v_prompt, logf_prompt, conv_prompt,
     k_sample, v_sample, logf_sample, conv_sample, chunk_v_sample) = o
    h2_dram = nc.dram_tensor("h2_rows", [NT, D], F32, kind="Internal").ap()
    moe_dram = nc.dram_tensor("moe_rows", [2 * PAIRS, BANK], F32, kind="Internal").ap()

    with ExitStack() as ctx:
        arena_size = 53024
        arena = ctx.enter_context(nc.sbuf_tensor("arena", [P, arena_size], F32))
        psum = ctx.enter_context(nc.psum_tensor("psum", [P, 8, BANK], F32))

        def ints(name, n):
            return ctx.enter_context(nc.sbuf_tensor(name, [P, n], I32))

        top = [0]

        def place(n):
            top[0] += n
            assert top[0] <= arena_size, top[0]
            return top[0] - n

        def at(start, *shape):
            n = 1
            for s in shape:
                n *= s
            flat = arena[:, start:start + n]
            if len(shape) == 1:
                return flat
            if len(shape) == 2:
                return flat.rearrange("p (a b) -> p a b", a=shape[0])
            return flat.rearrange("p (a b c) -> p a b c", a=shape[0], b=shape[1])

        region_a = place(MT_V * NT + DC * D)
        region_b = place(3 * DC * BANK)
        region_c = place(DC * NT + 2 * DC * 2 * P + 4 * NT + PAGE * HC)

        projT = at(region_a, NM, NT)
        mix_ab = projT[:, 4:8, :]
        cT = at(region_a + NM * NT, SEQ)
        w_out = at(region_a + MT_V * NT, DC, D)
        ring = [at(region_b + s * CW, CW) for s in range(4)]
        b_tail = region_b + 4 * CW
        s_buf = [at(b_tail + s * SEQ, SEQ) for s in range(2)]
        pT_buf = [at(b_tail + (2 + s) * SEQ, SEQ) for s in range(2)]
        k_nat = [at(b_tail + (4 + s) * SEQ, SEQ) for s in range(2)]
        ck_bc = [at(b_tail + (6 + s) * SEQ, SEQ) for s in range(2)]
        junk = at(b_tail, D)
        ws_nat = at(b_tail + 2 * SEQ, 4, P)
        w_forget = at(b_tail + 3 * SEQ, DC, HC)
        rms_bc = at(b_tail + 6 * SEQ, SEQ)
        rms_t = at(b_tail + 6 * SEQ, 3 * QT)
        gate_tmp = rms_bc
        own_head = at(b_tail + 7 * SEQ, SEQ)
        root_y = at(b_tail + 7 * SEQ, SEQ)
        root_m = at(b_tail + 3 * SEQ, SEQ)
        hT = at(region_c, DC, NT)
        mixT = hT
        squares2 = at(region_c + DC * NT, 4, SEQ)
        c1 = region_c + DC * NT
        w_ring = [at(c1 + s * DC * 2 * P, DC, 2 * P) for s in range(2)]
        c2 = c1 + 2 * DC * 2 * P
        v_nat = at(c2, QT, WC)
        mixS = at(c2 + 4 * SEQ + DC * NB, DC, NB)
        squares = at(c2, 4, SEQ)
        squares_s = at(c2 + 4 * SEQ, DC, NB)
        c3 = c2 + 4 * NT
        scores = at(c3, PAGE * HC)

        p_emb = at(region_c, TILES, D)
        c4 = region_c + TILES * D
        h2T = [at(c4 + s * D, DC, P) for s in range(2)]
        hgT = [at(c4 + 2 * D + s * DC * SLOTS, DC, SLOTS) for s in range(2)]
        silu = at(c4 + 3 * D, DE)
        act_nat = at(c4 + 3 * D + DE, DE)
        actT = [at(c4 + 4 * D + s * FC * SLOTS, FC, SLOTS) for s in range(2)]
        assert c4 + 6 * D <= c3 + PAGE * HC
        pT = at(c4 + 2 * D, 2, NT)
        p_nat = at(c4 + 2 * D + 2 * NT, TILES, DP)

        w_gu = [[at(r + m * DC * BANK, DC, DE) for m in range(2)] for r in (region_b, region_a)]
        w_dn = [at(r + 2 * DC * BANK, FC, D) for r in (region_b, region_a)]
        w_gate_ple = at(region_b, DC, D)
        g_fin = at(region_b + DC * D, D)
        pairs_in = [at(region_a + s * 2 * D, 2 * D) for s in range(2)]
        ple_gate = [at(region_a + 4 * D + s * D, D) for s in range(2)]
        xT = [at(region_a + 6 * D + s * D, DC, P) for s in range(2)]
        y_buf = [at(region_a + 8 * D + s * D, D) for s in range(2)]
        junk2, junk4 = at(region_a + 10 * D, D), at(region_a + 11 * D, D)
        parts_o, parts_g = at(region_c, 3, BANK), at(c4 + 3 * D, 3, BANK)

        x = at(place(TILES * D), TILES, D)
        xn0 = place(2 * D)
        xn = [at(xn0 + s * D, D) for s in range(2)]
        y_c = at(xn0, QT, WC)
        g_ffn_bc = at(place(D), D)
        h_rows = [at(c4 + s * D, D) for s in range(2)] + [at(xn0 + s * D, D) for s in range(2)]
        y_rows = [at(c4 + 5 * D + s * BANK, BANK) for s in range(2)] + [g_ffn_bc[:, s * BANK:(s + 1) * BANK] for s in range(2)]
        ident = at(place(P), P)
        tri = at(place(SEQ), SEQ)
        ones = tri[:, P:2 * P]
        mask = at(place(P), P)
        strict = at(place(P), P)
        later = at(place(P), P)
        row_sel = at(place(P), P)
        col_sel = at(place(NB), NB)
        roots = at(place(2), 2, 1)
        params = at(place(30), 30)
        stats = at(place(64), 64)
        small0 = place(7120)
        small_top = [small0]

        def small(*shape):
            n = 1
            for s in shape:
                n *= s
            small_top[0] += n
            assert small_top[0] <= small0 + 7120, small_top[0] - small0
            return at(small_top[0] - n, *shape)

        params_nat = small(P)
        logf_pages = small(PAGE, HC)
        decay = small(PAGE, HC)
        f_nat = small(TILES, HC)
        f_a, f_b, f_c, f_d = (small(TILES, HC) for _ in range(4))
        q_s, k_s, v_s, prod_s = (small(WC) for _ in range(4))
        q_bc = small(WC)
        wsT = small(4, P)
        bs_bc = small(2, P)
        v_norm = at(b_tail + 4 * SEQ, QT, WB)
        v_norm_s = prod_s[:, WA:WA + WB]
        ln_g_bc, ln_b_bc = small(WB), small(WB)
        bf_bc = small(HC)
        w00 = small(2)
        state = small(2 * WA)
        z_rows = prod_s[:, 0:WA]
        new_s, newT_s, mT, pnew, m_nat, sum_s = (small(HC) for _ in range(6))
        m_exp = small(P)
        max_p, max_b, sum_p = (small(HC) for _ in range(3))
        page_suf = small(HC)
        head_sel = small(HC)
        own_sample = small(NB)
        vnT = small(2, NB)
        gate_s = small(2, NB)
        conv_tmp = small(2, NB)
        bn = small(6)
        mv = small(2)
        p_exp = [at(b_tail + 4 * SEQ + s * KEYS * HC * NB, KEYS * HC, NB) for s in range(4)]
        fT = at(b_tail + 4 * SEQ, NT)
        w_ple_sb = at(small0 + 7120 - 2 * D, 2, D)
        small_top[0] = small0
        logits = small(TILES, NG + NE)
        eg = small(TILES, NG)
        gcand = small(TILES, NG)
        g_one = small(TILES, NG)
        masked = small(TILES, NE)
        m2 = small(TILES, NE)
        cand = small(TILES, NE)
        e_pair = small(2 * TILES, NE)
        e_one = [e_pair[:, c * TILES:(c + 1) * TILES, :] for c in range(2)]
        chosen = small(TILES, NE)
        prod_r = small(2 * TILES, NE)
        rank = small(TILES, NE)
        cmp8 = small(NE, QMAX)
        tiles_over, over_end, over_base = small(NE), small(NE), small(NE)
        r5 = [small(TILES) for _ in range(7)]
        r10 = [small(2 * TILES) for _ in range(4)]
        e_idx_pair = small(2 * TILES)
        e_idx = [e_idx_pair[:, c * TILES:(c + 1) * TILES] for c in range(2)]
        cmp10 = small(2 * TILES, QMAX)
        slot_one = small(2 * TILES, SLOTS)
        tile_one = small(2 * TILES, 2 * LIST)
        list_f = small(2 * LIST)
        cmp_over = small(OVER, NE)
        over_f = small(OVER + 1)
        assert small_top[0] <= small0 + 7120 - 2 * D
        w_keep = [at(place(TILES), TILES) for _ in range(2)]
        iota = at(place(SLOTS), SLOTS)
        tokid = at(place(2 * TILES), 2 * TILES)
        rowid = at(place(2 * TILES), 2 * TILES)
        steps = at(place(QMAX), QMAX)
        valid = at(place(2 * TILES), 2 * TILES)
        b_route = at(place(NG + NE), NG + NE)
        w_route = at(place(DC * (NG + NE)), DC, NG + NE)
        half_row = at(place(1), 1)
        page_f = at(place(1), 1)
        chunk_f = at(place(4), 4)
        indices = ints("indices", 5 + 2 * RING)
        page_id = indices[:, 0:1]
        chunk_id = [indices[:, 1 + s:2 + s] for s in range(4)]
        tok_list, row_list = ints("tok_list", LIST), ints("row_list", LIST)
        tok_ix = [indices[:, 5 + s:6 + s] for s in range(RING)]
        row_ix = [indices[:, 5 + RING + s:6 + RING + s] for s in range(RING)]
        over_i = ints("over_i", OVER + 1)

        def sem(name):
            return ctx.enter_context(nc.semaphore(name))

        x_in = [sem(f"x_in{t}") for t in range(TILES)]
        rows_in, consts_in, wf_in, lf_in, page_in = (sem(n) for n in ("rows_in", "consts_in", "wf_in", "lf_in", "page_in"))
        route_w_in = sem("route_w_in")
        pool_step, act_step, dve_step = sem("pool_step"), sem("act_step"), sem("dve_step")
        consts_built = sem("consts_built")
        full = [sem("fill_ready0"), sem("fill_ready1")]
        free = [sem("fill_read0"), sem("fill_read1")]
        ms_ready, xn_ready, xn_used = sem("ms_ready"), sem("xn_ready"), sem("xn_used")
        f_full, f_free = sem("f_full"), sem("f_free")
        w_in_s = [sem("w_group_in0"), sem("w_group_in1")]
        half_full, half_free = sem("proj_half_ready"), sem("proj_half_copied")
        pj_full, pj_free = sem("proj_ready"), sem("proj_copied")
        kn_out, vn_ready = [sem("k_nat_stored0"), sem("k_nat_stored1")], sem("v_nat_ready")
        sample_nat = sem("sample_nat_ready")
        qb_ready = sem("q_bc_ready")
        logf_ready = sem("logf_ready")
        f_part = sem("f_part")
        kv_in = [sem(f"cache_in{s}") for s in range(4)]
        kmul, kred = sem("k_products"), sem("k_reduced")
        suf_ready = sem("suffix_parts_ready")
        ct_ready = sem("cT_ready")
        ck_full, ck_ready = sem("ck_full"), sem("ck_bc_ready")
        a_s, a_read, a_m, a_p, a_t, a_pt, a_o, a_of = (sem("att_" + n) for n in (
            "scores", "scores_read", "max", "probs", "probsT", "probsT_copied", "out", "out_copied"))
        v_ready, gv_full, gv_read = sem("v_norm_ready"), sem("gating_v_full"), sem("gating_v_read")
        z_ready = sem("z_ready")
        z_nat = sem("z_nat_ready")
        mix_ready = sem("mix_ready")
        sq_ready, norms_full, rms_ready = sem("squares_ready"), sem("norms_full"), sem("rms_ready")
        w_o_in = sem("w_o_in")
        wo_full, wo_free = sem("wo_full"), sem("wo_added")
        x1_ms, h2_ready, h2T_ready = sem("x1_ms"), sem("h2_ready"), sem("h2T_ready")
        h2_stored = [sem("h2_stored0"), sem("h2_stored1")]
        mix_normed, mixs_normed, new_ready = sem("mix_normed"), sem("mix_sample_normed"), sem("new_score_ready")
        smp_req, smp_exp, smp_p = sem("sample_operand"), sem("sample_exp_in"), sem("sample_exp_out")
        px_ready, pv_done, pv_read = sem("p_expanded"), sem("pv_done"), sem("pv_read")
        mixs_ready = sem("mix_sample_ready")
        route_op, route_exp_in, route_exp_out = sem("route_operand"), sem("route_exp_in"), sem("route_exp_out")
        lists_ready = sem("lists_ready")
        ple_in, pT_ready, pe_full, pe_free = sem("ple_in"), sem("pT_ready"), sem("p_emb_full"), sem("p_emb_copied")
        hg_in, y_out = ([sem(f"{n}{s}") for s in range(RING)] for n in ("rows_in", "y_out"))
        gu_in = [[sem(f"w_{m}{s}_in") for m in ("gate", "up")] for s in range(2)]
        dn_in = [sem("w_down0_in"), sem("w_down1_in")]
        hgT_full, hgT_ready, gu_full, silu_ready, act_ready, actT_full, actT_ready, y_full, y_copied = (sem("moe_" + n) for n in (
            "rowsT_full", "rowsT_ready", "gate_up", "silu", "act", "actT_full", "actT_ready", "y_full", "y_copied"))
        moe_done = sem("moe_done")
        ov_w, ov_rows, ov_T, ov_Tc, ov_gu, ov_silu, ov_act, ov_aT, ov_aTc, ov_y, ov_yc, ov_out = (sem("over_" + n) for n in (
            "weights_in", "rows_in", "rowsT", "rowsT_ready", "gate_up", "silu", "act", "actT", "actT_ready", "y", "y_ready", "stored"))
        parts_ready, parts_summed = sem("sample_parts_ready"), sem("sample_parts_summed")
        wpg_in, gfin_in, pairs_ready = sem("w_ple_gate_in"), sem("g_final_in"), [sem("pairs_in0"), sem("pairs_in1")]
        x2_ms, x3_ready, xT_full, xT_ready, pg_full, pg_sig, pg_free, x4_ms, y_final = (sem("post_" + n) for n in (
            "x2_ms", "xn", "xT_full", "xT", "gate_full", "gate_sigmoid", "gate_free", "x4_ms", "y"))
        x2_ready, x4_ready = sem("post_x2"), sem("post_x4")
        y_stored, out_act = [sem("y_stored0"), sem("y_stored1")], sem("stored_by_scalar")

        passed = sem("passed")

        block = ctx.enter_context(nc.Block())

        def bank(b):
            return psum[:, b, :]

        def fill(name):
            return bank(4 + AT[name][0])

        def wait_full(eng, name):
            b, n = AT[name]
            eng.wait_ge(full[b], n + 1)

        def free_of(name):
            return free[AT[name][0]]

        def wait_free(eng, name):
            b, n = AT[name]
            if n:
                eng.wait_ge(free[b], n)

        def alone(eng):
            eng.nop().then_inc(passed, 1)

        class Steps:

            def __init__(self, eng, semaphore):
                self.eng, self.sem, self.n, self.off = eng, semaphore, 0, 0

            def __call__(self, ins):
                self.n += 1
                ins.then_inc(self.sem, 1)
                self.eng.wait_ge(self.sem, self.n + self.off)
                if not isinstance(self.off, int):
                    alone(self.eng)

        def inner(ap, n):
            return ap.rearrange("p (a o) -> p a o", o=1).to_broadcast([ap.shape[0], ap.shape[1], n])

        def outer(ap, n):
            return ap.rearrange("p (o a) -> p o a", o=1).to_broadcast([ap.shape[0], n, ap.shape[1]])

        def num(i, c):
            return i * RING + c

        def loads(i, c, ring):
            return i * (16 * RING // ring) + 16 * (c // ring + 1)

        def exists(i, c):
            return not isinstance(i, int) or RING * i + c >= 0

        def bc_rows(src, n=P):
            return src.to_broadcast([n, src.shape[-1]])

        first_rest = GROUPS - FIRST
        rest_halves = 4 * FIRST
        rest_steps = [[] for _ in range(4 * HC)]
        for n in range(2 * rest_halves):
            rest_steps[n // 5 * 4 + max(n % 5 - 1, 0)].append(n)

        def sample_sums(mm, out, operand, weights):
            for k in range(DC):
                for n in range(2):
                    g = 2 * (k % 2) + n
                    last = mm(out[32 * g:32 * g + NB, :], operand[:, k, 0:NB], weights[:, k, n * BANK:(n + 1) * BANK],
                              start=(k < 2), stop=(k >= DC - 2))
            return last

        def copy_parts(act, dst, src):
            for g in range(1, 4):
                ins = act.activation(dst[0:NB, g - 1, :], src[32 * g:32 * g + NB, :], ACT.Copy)
                ins.then_inc(parts_ready, 1)

        def finish_gate(act, n):
            t = LAST[n]
            w = tile_width(t)
            act.wait_ge(pg_full, n + 1)
            gate = ple_gate[n % 2][0:w, :]
            if t == QT:
                copy_parts(act, parts_g, bank(2 * (n % 2)))
                act.wait_ge(parts_summed, 1)
                act.activation(gate, gate, ACT.Sigmoid).then_inc(pg_sig, 1)
            else:
                act.activation(gate.rearrange("p (a n) -> p a n", a=2), psum[0:w, 2 * (n % 2):2 * (n % 2) + 2, :],
                               ACT.Sigmoid).then_inc(pg_sig, 1)
            act.wait_ge(x4_ready, n + 1)
            act.activation(junk4[0:w, :], x[0:w, t, :], ACT.Square, accum_out=stats[0:w, 48 + t:49 + t]).then_inc(x4_ms, 1)

        @block.sync
        def _(sp):
            for t in range(QT):
                sp.dma_start(x[:, t, :], a["x_prompt"][0, t * P:(t + 1) * P, :]).then_inc(x_in[t], 16)
            sp.dma_start(x[0:NB, QT, :], a["x_sample"].rearrange("b l d -> (b l) d")).then_inc(x_in[QT], 16)
            w_in_v = a["w_in"][0].rearrange("(k p) n -> p k n", p=P)

            def w_group(n, slot):
                return w_ring[slot]

            def load_group(g, slot):
                sp.dma_start(w_ring[slot], w_in_v[:, :, bass.ds(g * (2 * P), 2 * P)]).then_inc(w_in_s[slot], 16)

            load_group(FIRST, 0)
            load_group(FIRST + 1, 1)
            with sp.Fori(1, (GROUPS - FIRST) // 2) as i:
                for s in range(2):
                    sp.wait_ge(pj_full, i * 4 + (2 * s - 2))
                    load_group(i * 2 + (FIRST + s), s)
            done = GROUPS - FIRST
            sp.wait_ge(pj_full, 2 * done - 2)
            load_group(FIRST - 1, 0)
            sp.wait_ge(pj_full, 2 * done)
            load_group(0, 1)
            for g in range(1, FIRST - 1):
                sp.wait_ge(half_full, 4 * g)
                load_group(g, 1 - g % 2)
            sp.wait_ge(a_o, 4 * HC)
            sp.wait_ge(gv_full, TILES)
            sp.dma_start(w_out, a["w_o"][0].rearrange("(k p) n -> p k n", p=P)).then_inc(w_o_in, 16)
            wg, wu, wd = (a[n][0].rearrange("g e d f -> (g e) d f") for n in ("w_gate", "w_up", "w_down"))

            def load_expert(e, s):
                sp.dma_start(w_gu[s][0], wg[bass.ds(e, 1)].rearrange("o (p k) f -> p (o k) f", k=DC)).then_inc(gu_in[s][0], 16)
                sp.dma_start(w_gu[s][1], wu[bass.ds(e, 1)].rearrange("o (p k) f -> p (o k) f", k=DC)).then_inc(gu_in[s][1], 16)

            def load_down(e, s):
                sp.dma_start(w_dn[s], wd[bass.ds(e, 1)].rearrange("o (p k) n -> p (o k) n", k=FC)).then_inc(dn_in[s], 16)

            sp.wait_ge(pv_done, CHUNKS)
            load_expert(0, 0)
            sp.wait_ge(mixs_normed, 1)
            load_down(0, 0)
            sp.wait_ge(wo_full, TILES)
            load_expert(1, 1)
            load_down(1, 1)
            sp.wait_ge(gu_full, 1)
            load_expert(2, 0)
            with sp.Fori(2, NE // 2) as i:
                for s in range(2):
                    sp.wait_ge(gu_full, i * 2 + (s - 2))
                    load_expert(i * 2 + (s - 1), 1 - s)
                    sp.wait_ge(y_full, i * 2 + (s - 3))
                    load_down(i * 2 + (s - 2), s)
            sp.wait_ge(gu_full, NE - 2)
            load_expert(NE - 1, 1)
            for e in (NE - 2, NE - 1):
                sp.wait_ge(y_full, e - 1)
                load_down(e, e % 2)
            sp.wait_ge(gu_full, NE - 1)
            sp.dma_start(w_gate_ple, a["w_ple_gate"][0].rearrange("(k p) n -> p k n", p=P)).then_inc(wpg_in, 16)
            sp.wait_ge(y_full, NE - 1)
            sp.dma_start(g_fin, bc_rows(a["g_final"].rearrange("(a n) -> a n", a=1))).then_inc(gfin_in, 16)
            sp.wait_ge(lists_ready, 1)
            sp.wait_ge(y_full, NE)
            n_over = sp.value_load(over_i[0:1, OVER:OVER + 1], min_val=0, max_val=OVER)
            with sp.If(n_over > 0):
                with sp.Fori(0, n_over) as i:
                    e = sp.value_load(over_i[0:1, bass.ds(i, 1)], min_val=0, max_val=NE - 1)
                    sp.wait_ge(ov_y, i + 1)
                    sp.dma_start(w_gu[1][0], wg[bass.ds(e, 1)].rearrange("o (p k) f -> p (o k) f", k=DC)).then_inc(ov_w, 16)
                    sp.dma_start(w_gu[1][1], wu[bass.ds(e, 1)].rearrange("o (p k) f -> p (o k) f", k=DC)).then_inc(ov_w, 16)
                    sp.dma_start(w_dn[1], wd[bass.ds(e, 1)].rearrange("o (p k) n -> p (o k) n", k=FC)).then_inc(ov_w, 16)
            with sp.Else():
                sp.nop()
            sp.wait_ge(moe_done, 1)
            for n, t in enumerate(LAST):
                w = tile_width(t)
                if n >= 2:
                    sp.wait_ge(x2_ready, n - 1)
                rows = moe_dram[4 * t * P:4 * (t * P + w), :].rearrange("(p k) d -> p (k d)", k=4)
                sp.dma_start(pairs_in[n % 2][0:w, :], rows).then_inc(pairs_ready[n % 2], 16)
            for n, t in enumerate(LAST):
                w = tile_width(t)
                sp.wait_ge(y_final, n + 1)
                dst = y_prompt[0, t * P:(t + 1) * P, :] if t < QT else y_sample.rearrange("b l d -> (b l) d")
                sp.dma_start(dst, y_buf[n % 2][0:w, :]).then_inc(y_stored[n % 2], 16)
            sp.wait_ge(y_stored[0], 48)
            sp.wait_ge(y_stored[1], 32)

        @block.gpsimd
        def _(pool):
            step = Steps(pool, pool_step)
            pool.dma_start(page_id[:, :], a["page_table"].rearrange("b (g o) -> (b g) o", o=1)).then_inc(page_in, 16)

            def select(out, op, fill_value, base, pattern, mult):
                step(pool.affine_select(out=out, in_=out, compare_op=op, fill=fill_value, base=base,
                                        pattern=pattern, channel_multiplier=mult))

            step(pool.memset(ident, 0.0))
            select(ident, ALU.not_equal, 1.0, 0, [[-1, P]], 1)
            step(pool.memset(tri, 1.0))
            select(tri, ALU.is_ge, 0.0, 0, [[1, SEQ]], -1)
            pool.nop().then_inc(consts_built, 1)
            pool.wait_ge(page_in, 16)
            pool.indirect_dma_start(logf_pages.rearrange("p k h -> p (k h)"), None,
                                    a["cache_logf"][0].rearrange("n k h -> n (k h)"),
                                    bass.IndirectOffsetOnAxis(ap=page_id[:, 0:1], axis=0)).then_inc(lf_in, 16)
            step(pool.tensor_copy(page_f, page_id[:, 0:1]))
            for s in range(4):
                step(pool.tensor_scalar(chunk_f[:, s:s + 1], page_f, float(CHUNKS), float(s), ALU.mult, ALU.add))
            caches = [a[n][0].rearrange("n (c k) h d -> (n c) (k h d)", k=KEYS) for n in ("cache_k", "cache_v")]

            def load_chunk(cache, s):
                step(pool.tensor_copy(chunk_id[s][:, 0:1], chunk_f[:, s:s + 1]))
                pool.indirect_dma_start(ring[s], None, caches[cache],
                                        bass.IndirectOffsetOnAxis(ap=chunk_id[s][:, 0:1], axis=0)).then_inc(kv_in[s], 16)
                step(pool.tensor_scalar(chunk_f[:, s:s + 1], chunk_f[:, s:s + 1], 4.0, None, ALU.add))

            for s in range(3):
                load_chunk(0, s)
            step(pool.memset(mask, 0.0))
            select(mask, ALU.is_ge, -BIG, 0, [[-1, P]], 1)
            step(pool.memset(strict, 1.0))
            select(strict, ALU.is_ge, 0.0, -1, [[1, P]], -1)
            lat = later.rearrange("p (b g) -> p b g", b=NB)
            step(pool.memset(later, 1.0))
            select(lat, ALU.is_ge, 0.0, -1, [[-PAGES, NB], [-1, PAGES]], 1)
            select(lat, ALU.is_ge, 0.0, PAGES - 1, [[PAGES, NB], [0, PAGES]], -1)
            rs = row_sel[0:NB, :].rearrange("p (b g) -> p b g", b=NB)
            step(pool.memset(row_sel, 0.0))
            select(rs, ALU.not_equal, 1.0, 0, [[-1, NB], [0, PAGES]], 1)
            step(pool.memset(col_sel, 1.0))
            select(col_sel, ALU.is_ge, 0.0, 0, [[-PAGES, NB]], 1)
            select(col_sel, ALU.is_ge, 0.0, PAGES - 1, [[PAGES, NB]], -1)
            step(pool.memset(head_sel, 0.0))
            step(pool.memset(own_sample, 0.0))
            for half in range(2):
                for k in range(HC):
                    select(own_sample, ALU.not_equal, 1.0, -(half * SLOTS + k * NB), [[-1, NB]], 1)
                    select(head_sel, ALU.not_equal, 1.0, -(half * SLOTS + k), [[-NB, HC]], 1)
            step(pool.iota(iota, pattern=[[1, SLOTS]], base=0, channel_multiplier=0, allow_small_or_imprecise_dtypes=True))
            step(pool.iota(tokid, pattern=[[0, 2], [P, TILES]], base=0, channel_multiplier=1, allow_small_or_imprecise_dtypes=True))
            step(pool.iota(rowid, pattern=[[1, 2], [2 * P, TILES]], base=1, channel_multiplier=2, allow_small_or_imprecise_dtypes=True))
            step(pool.iota(steps, pattern=[[SLOTS, QMAX]], base=SLOTS, channel_multiplier=0, allow_small_or_imprecise_dtypes=True))
            step(pool.memset(half_row, -2.0))
            select(half_row, ALU.is_ge, -1.0, SLOTS - 1, [[0, 1]], -1)
            step(pool.memset(valid, 1.0))
            for c in range(2):
                select(valid[:, c * TILES + QT:(c + 1) * TILES], ALU.is_ge, 0.0, NB - 1, [[0, 1]], -1)
            pool.nop().then_inc(consts_built, 1)

            pool.wait_ge(qb_ready, 1)
            q_rep = q_bc.rearrange("p (o n) -> p o n", o=1).to_broadcast([P, KEYS, WC])

            def products(s, count):
                pool.wait_ge(kv_in[s], count)
                r = ring[s].rearrange("p (k n) -> p k n", k=KEYS)
                pool.tensor_tensor(r, r, q_rep, ALU.mult).then_inc(kmul, 1)

            base = step.n
            per = 8
            with pool.Fori(0, CHUNKS // 4 - 1) as i:
                step.off = i * per
                for s in range(4):
                    products(s, i * 16 + 16)
                    pool.wait_ge(kred, i * 4 + (s + 1))
                    alone(pool)
                    load_chunk(0, (s + 3) % 4)
            assert step.n == base + per
            step.n, step.off = base + per * (CHUNKS // 4 - 1), 0
            for s in range(4):
                products(s, 16 * (CHUNKS // 4))
                pool.wait_ge(kred, CHUNKS - 4 + s + 1)
                if s == 0:
                    load_chunk(0, 3)
                    for r in range(4):
                        step(pool.tensor_scalar(chunk_f[:, r:r + 1], page_f, float(CHUNKS), float(r), ALU.mult, ALU.add))
                else:
                    load_chunk(1, s - 1)
            pool.wait_ge(kred, CHUNKS + 1)
            load_chunk(1, 3)
            base = step.n
            with pool.Fori(1, CHUNKS // 4) as i:
                step.off = (i - 1) * per
                for s in range(4):
                    pool.wait_ge(pv_done, i * 4 + (s - 3))
                    alone(pool)
                    load_chunk(1, s)
            step.n, step.off = base + per * (CHUNKS // 4 - 1), 0

            pool.wait_ge(lists_ready, 1)
            pool.wait_ge(h2_stored[0], 48)
            pool.wait_ge(h2_stored[1], 32)

            def gather(i, c):
                s, e = c % RING, num(i, c)
                step(pool.tensor_copy(tok_ix[s][0:SLOTS, 0:1], tok_list[0:SLOTS, bass.ds(e, 1)]))
                pool.indirect_dma_start(h_rows[s][0:SLOTS, :], None, h2_dram,
                                        bass.IndirectOffsetOnAxis(ap=tok_ix[s][0:SLOTS, 0:1], axis=0)).then_inc(hg_in[s], 16)

            def scatter(e, s):
                step(pool.tensor_copy(row_ix[s][:, 0:1], row_list[:, bass.ds(e, 1)]))
                return pool.indirect_dma_start(moe_dram, bass.IndirectOffsetOnAxis(ap=row_ix[s][:, 0:1], axis=0),
                                               y_rows[s], None, bounds_check=2 * PAIRS - 1, oob_is_err=False)

            def move_rows(i, c, last=False):
                if not last:
                    pool.wait_ge(hgT_full, num(i, c + 1))
                    if not isinstance(i, int):
                        alone(pool)
                    gather(i, c + RING)
                if exists(i, c - 2):
                    pool.wait_ge(y_copied, num(i, c - 1))
                    if not isinstance(i, int):
                        alone(pool)
                    scatter(num(i, c - 2), (c - 2) % RING).then_inc(y_out[(c - 2) % RING], 16)

            for c in range(RING):
                gather(0, c)
            for c in range(RING):
                move_rows(0, c)
            base = step.n
            with pool.Fori(1, NE // RING - 1) as i:
                step.off = (i - 1) * (2 * RING)
                for c in range(RING):
                    move_rows(i, c)
            step.n, step.off = base + 2 * RING * (NE // RING - 2), 0
            for e in range(NE - RING, NE + 2):
                move_rows(0, e, last=True)
            for s in range(RING):
                pool.wait_ge(y_out[s], 16 * (NE // RING))
            n_over = pool.value_load(over_i[0:1, OVER:OVER + 1], min_val=0, max_val=OVER)
            with pool.If(n_over > 0):
                with pool.Fori(0, n_over) as i:
                    step.off = i * 2
                    step(pool.tensor_copy(tok_ix[0][0:SLOTS, 0:1], tok_list[0:SLOTS, bass.ds(i + NE, 1)]))
                    pool.indirect_dma_start(h_rows[0][0:SLOTS, :], None, h2_dram,
                                            bass.IndirectOffsetOnAxis(ap=tok_ix[0][0:SLOTS, 0:1], axis=0)).then_inc(ov_rows, 16)
                    pool.wait_ge(ov_yc, i + 1)
                    alone(pool)
                    scatter(i + NE, 0).then_inc(ov_out, 16)
                    pool.wait_ge(ov_out, i * 16 + 16)
                step.off = 0
            with pool.Else():
                pool.nop()
            pool.nop().then_inc(moe_done, 1)

        @block.scalar
        def _(act):
            step = Steps(act, act_step)
            for n, (name, rows) in enumerate((("g_mix", 8), ("g_out", 8))):
                act.dma_start(params_nat[8 * n:8 * n + rows, :], a[name][0].rearrange("(c p) -> c p", p=P)).then_inc(rows_in, 16)
            act.dma_start(params_nat[16:22, :], a["conv_w"][0].rearrange("j (c p) -> (j c) p", p=P)).then_inc(rows_in, 16)
            act.dma_start(params_nat[22:30, :], a["g_ple"][0].rearrange("(c p) -> c p", p=P)).then_inc(rows_in, 16)
            w_f = a["w_in"][0].rearrange("(k p) n -> p k n", p=P)[:, :, NM * P:NM * P + HC]
            act.dma_start(w_forget, w_f).then_inc(wf_in, 16)

            def square(t, m):
                w = tile_width(t)
                act.wait_ge(x_in[t], 16)
                act.activation(junk[0:w, :], x[0:w, t, :], ACT.Square, accum_out=stats[0:w, t:t + 1]).then_inc(ms_ready, 1)

            for t in range(TILES):
                if t:
                    act.wait_ge(ms_ready, t)
                square(t, 0)

            n_consts = [0]

            def const(dst, src):
                n_consts[0] += 1
                act.dma_start(dst, src).then_inc(consts_in, 16)

            const(ws_nat, a["w_s"][0].rearrange("h t s -> t h s"))
            const(bf_bc, bc_rows(a["b_f"]))
            const(ln_g_bc, bc_rows(a["ln_g"]))
            const(ln_b_bc, bc_rows(a["ln_b"]))
            for h in range(4):
                q = (h % 2) * HD
                const(bs_bc[q:q + HD, h // 2, :], bc_rows(a["b_s"][0, h:h + 1, :], HD))
                const(w00[q:q + HD, h // 2:h // 2 + 1], bc_rows(a["w_s"][0, h, 0:1, 0:1], HD))
            const(state[0:NB, :], a["state_conv"][0].rearrange("b j c -> b (j c)"))
            const(b_route[:, 0:NG], bc_rows(a["b_grp"]))
            const(b_route[:, NG:], bc_rows(a["b_rt"].rearrange("l g e -> l (g e)")))
            const(g_ffn_bc, bc_rows(a["g_ffn"]))
            act.dma_start(w_route[:, :, 0:NG], a["w_grp"][0].rearrange("(k p) n -> p k n", p=P)).then_inc(route_w_in, 16)
            act.dma_start(w_route[:, :, NG:], a["w_rt"][0].rearrange("(k p) g e -> p k (g e)", p=P)).then_inc(route_w_in, 16)
            act.wait_ge(f_full, 1)
            act.activation(fT[0:HC, :].rearrange("p (a n) -> p a n", a=2), psum[0:HC, 2:4, 0:HALF], ACT.Copy).then_inc(f_free, 1)

            def copy_proj(m, parity, ready):
                act.wait_ge(pj_full, ready)
                dst = projT[:, bass.ds(m, 1), :].rearrange("p o (a n) -> p (o a) n", a=2)
                act.activation(dst, psum[:, 2 * parity:2 * parity + 2, 0:HALF], ACT.Copy).then_inc(pj_free, 1)

            for q in range(4):
                copy_proj(MT_Q + q, q % 2, q + 1)
            wait_full(act, "qs")
            act.activation(q_s[0:NB, :], fill("qs")[0:NB, :], ACT.Copy, scale=SCALE).then_inc(free_of("qs"), 1)
            wait_full(act, "qb")
            act.activation(q_bc, fill("qb"), ACT.Copy).then_inc(free_of("qb"), 1)
            act.wait_ge(free_of("qb"), AT["qb"][1] + 1)
            act.nop().then_inc(qb_ready, 1)
            act.wait_ge(f_part, 1)
            act.activation(f_b, f_a, ACT.Exp, scale=-1.0).then_inc(f_part, 1)
            act.wait_ge(f_part, 3)
            act.activation(f_d, f_c, ACT.Ln).then_inc(f_part, 1)
            with act.Fori(1, (GROUPS - FIRST) // 2) as i:
                for q in range(4):
                    copy_proj(i * 4 + (MT_Q + q), q % 2, i * 4 + (q + 1))
            wait_full(act, "ks")
            act.activation(k_s[0:NB, :], fill("ks")[0:NB, :], ACT.Copy).then_inc(free_of("ks"), 1)
            wait_full(act, "vs")
            act.activation(v_s[0:NB, :], fill("vs")[0:NB, :], ACT.Copy).then_inc(free_of("vs"), 1)
            act.wait_ge(free_of("ks"), AT["ks"][1] + 1)
            act.wait_ge(free_of("vs"), AT["vs"][1] + 1)
            act.nop().then_inc(sample_nat, 1)
            flat = "l b t h d -> (l b t) (h d)"
            act.dma_start(k_sample.rearrange(flat), k_s[0:NB, :]).then_inc(out_act, 16)
            act.dma_start(v_sample.rearrange(flat), v_s[0:NB, :]).then_inc(out_act, 16)
            stored = [2]
            wait_full(act, "ct")
            act.activation(cT[0:HC, :], fill("ct")[0:HC, :], ACT.Copy).then_inc(free_of("ct"), 1)
            act.wait_ge(free_of("ct"), AT["ct"][1] + 1)
            act.nop().then_inc(ct_ready, 1)
            for t in range(QT):
                wait_full(act, f"k{t}")
                if t >= 2:
                    act.wait_ge(kn_out[t % 2], 16)
                act.activation(k_nat[t % 2], fill(f"k{t}"), ACT.Copy).then_inc(free_of(f"k{t}"), 1)
                act.wait_ge(free_of(f"k{t}"), AT[f"k{t}"][1] + 1)
                rows = slice(t * P, (t + 1) * P)
                act.dma_start(k_prompt[0, 0, rows].rearrange("t h d -> t (h d)"), k_nat[t % 2]).then_inc(kn_out[t % 2], 16)
            for t in range(QT):
                act.wait_ge(vn_ready, t + 1)
                act.dma_start(v_prompt[0, 0, t * P:(t + 1) * P].rearrange("t h d -> t (h d)"), v_nat[:, t, :]).then_inc(out_act, 16)
                stored[0] += 1
            act.wait_ge(logf_ready, 1)
            act.dma_start(logf_prompt[0, 0].rearrange("(t p) h -> p t h", p=P), f_nat[:, 0:QT, :]).then_inc(out_act, 16)
            act.dma_start(logf_sample.rearrange("l b t h -> (l b t) h"), f_nat[0:NB, QT, :]).then_inc(out_act, 16)
            stored[0] += 2
            for s in range(2):
                act.wait_ge(kn_out[s], 16 * (QT // 2))

            def copy_ck(h):
                act.wait_ge(ck_full, h + 1)
                if h >= 2:
                    act.wait_ge(a_read, 4 * (h - 1))
                act.activation(ck_bc[h % 2], bank(7), ACT.Copy).then_inc(ck_ready, 1)

            def copy_half(j):
                m = (MT_V + j // 2) if j < 4 else j // 2 - 2
                act.wait_ge(half_full, j + 1)
                ins = act.activation(projT[:, m, j % 2 * HALF:(j % 2 + 1) * HALF], bank(4)[:, 0:HALF], ACT.Copy)
                ins.then_inc(half_free, 1)

            copy_ck(0)
            units = 4 * HC
            for u in range(units + 1):
                if u < units:
                    nk = P * (u % QT + 1)
                    act.wait_ge(a_m, u + 1)
                    act.activation(s_buf[u % 2][:, 0:nk], s_buf[u % 2][:, 0:nk], ACT.Exp, bias=stats[:, 8 + u % 2:9 + u % 2],
                                   accum_out=stats[:, 16 + u % 4:17 + u % 4]).then_inc(a_p, 1)
                if u >= 1:
                    w = u - 1
                    nk = P * (w % QT + 1)
                    act.wait_ge(a_t, w + 1)
                    if w >= 2:
                        act.wait_ge(a_o, w - 1)
                    act.activation(pT_buf[w % 2][:, 0:nk], bank(2 + w % 2)[:, 0:nk], ACT.Copy).then_inc(a_pt, 1)
                if u < units:
                    for n in rest_steps[u]:
                        if n % 2:
                            copy_half(n // 2)
                if u % QT == 2 and u // QT + 1 < HC:
                    copy_ck(u // QT + 1)

            for t in range(QT):
                wait_full(act, f"yc{t}")
                act.activation(mixT[:, 4:8, t * P:(t + 1) * P], fill(f"yc{t}").rearrange("p (c n) -> p c n", c=4),
                               ACT.Copy).then_inc(free_of(f"yc{t}"), 1)
            for t in range(QT):
                act.wait_ge(free_of(f"yc{t}"), AT[f"yc{t}"][1] + 1)
            act.activation(squares2, mixT[:, 4:8, 0:SEQ], ACT.Square).then_inc(sq_ready, 1)
            act.wait_ge(out_act, 16 * stored[0])
            wait_full(act, "z")
            step(act.activation(z_rows[32:34, :], fill("z")[0:2, 0:WA], ACT.Copy))
            act.activation(z_rows[0:NB, :], fill("z")[0:NB, WA:2 * WA], ACT.Copy).then_inc(free_of("z"), 1)
            act.wait_ge(free_of("z"), AT["z"][1] + 1)
            act.dma_start(conv_prompt[0, 0], z_rows[32:34, :]).then_inc(out_act, 16)
            act.dma_start(conv_sample[0, :, 0, :], state[0:NB, WA:2 * WA]).then_inc(out_act, 16)
            act.dma_start(conv_sample[0, :, 1, :], z_rows[0:NB, :]).then_inc(out_act, 16)
            act.wait_ge(v_ready, TILES)
            act.dma_start(chunk_v_sample.rearrange("l b t c -> (l b t) c"), v_norm_s[0:NB, :]).then_inc(out_act, 16)
            stored[0] += 4
            act.wait_ge(z_ready, 2)
            act.activation(squares[:, 0:2, :], mix_ab[:, 0:2, 0:SEQ], ACT.Square).then_inc(sq_ready, 1)
            act.wait_ge(mix_ready, 1)
            act.activation(squares[:, 2:4, :], mix_ab[:, 2:4, 0:SEQ], ACT.Square).then_inc(sq_ready, 1)

            act.wait_ge(smp_exp, 1)
            act.activation(scores, scores, ACT.Exp).then_inc(smp_p, 1)
            act.wait_ge(smp_exp, 2)
            act.activation(pnew[0:NB, :], new_s[0:NB, :], ACT.Exp).then_inc(smp_p, 1)
            act.wait_ge(mix_normed, 1)
            act.dma_start(p_nat[:, 0:QT, :], a["p_prompt"][0, 0].rearrange("(t p) n -> p t n", p=P)).then_inc(ple_in, 16)
            act.dma_start(p_nat[0:NB, QT, :], a["p_sample"][0].rearrange("b l n -> (b l) n")).then_inc(ple_in, 16)

            def second_norm(t):
                w = tile_width(t)
                if t == QT:
                    act.wait_ge(wo_full, TURN[t] + 1)
                    copy_parts(act, parts_o, bank(2 * (t % 2)))
                act.wait_ge(wo_free, TURN[t] + 1)
                act.activation(xn[t % 2][0:w, :], x[0:w, t, :], ACT.Square, accum_out=stats[0:w, 24 + t:25 + t]).then_inc(x1_ms, 1)

            def store_h2(t):
                act.wait_ge(h2_ready, TURN[t] + 1)
                act.dma_start(h2_dram[tile_cols(t), :], xn[t % 2][0:tile_width(t), :]).then_inc(h2_stored[t % 2], 16)

            def copy_h2T(t):
                w = tile_width(t)
                for s, half in enumerate("ab"):
                    wait_full(act, f"h{t}{half}")
                    if s == 0 and t >= 2:
                        wait_full(act, f"h{t - 2}r")
                    act.activation(h2T[t % 2][:, 4 * s:4 * s + 4, 0:w],
                                   fill(f"h{t}{half}").rearrange("p (c n) -> p c n", c=4)[:, :, 0:w], ACT.Copy)\
                       .then_inc(free_of(f"h{t}{half}"), 1)
                act.wait_ge(free_of(f"h{t}b"), AT[f"h{t}b"][1] + 1)
                act.wait_ge(free_of(f"h{t}a"), AT[f"h{t}a"][1] + 1)
                act.nop().then_inc(h2T_ready, 1)

            act.wait_ge(out_act, 16 * stored[0])
            for t in range(QT - 1):
                if t >= 2:
                    act.wait_ge(h2_stored[t % 2], 16)
                second_norm(t)
                store_h2(t)
                copy_h2T(t)
            act.wait_ge(mixs_ready, 1)
            step(act.activation(squares_s[:, 0:4, :], mix_ab[:, :, SEQ:NT], ACT.Square))
            act.activation(squares_s[:, 4:8, :], mixT[:, 4:8, SEQ:NT], ACT.Square).then_inc(sq_ready, 1)
            act.dma_start(w_ple_sb, a["w_ple"][0].rearrange("(k p) n -> p k n", p=P)).then_inc(ple_in, 16)
            for name, t0, n in (("p01", 0, 2), ("p23", 2, 2), ("p4", 4, 1)):
                wait_full(act, name)
                w = n * P if n == 2 else NB
                act.activation(pT[:, :, t0 * P:t0 * P + w], fill(name).rearrange("p (k n) -> p k n", k=2)[:, :, 0:w],
                               ACT.Copy).then_inc(free_of(name), 1)
            for name in ("p23", "p4"):
                act.wait_ge(free_of(name), AT[name][1] + 1)
            act.nop().then_inc(pT_ready, 1)
            act.wait_ge(h2_stored[0], 32)
            second_norm(QT)
            store_h2(QT)
            act.wait_ge(h2_stored[1], 16)
            second_norm(QT - 1)
            copy_h2T(QT)
            store_h2(QT - 1)
            copy_h2T(QT - 1)

            def copy_p_emb(t):
                w = tile_width(t)
                act.wait_ge(pe_full, t + 1)
                pair = psum[0:w, 2 * (t % 2):2 * (t % 2) + 2, :]
                act.activation(p_emb[0:w, t, :].rearrange("p (a n) -> p a n", a=2), pair, ACT.Copy).then_inc(pe_free, 1)

            copy_p_emb(0)
            copy_p_emb(1)
            act.wait_ge(route_exp_in, 1)
            act.activation(eg, eg, ACT.Exp).then_inc(route_exp_out, 1)
            act.wait_ge(route_exp_in, 2)
            act.activation(r5[4], r5[4], ACT.Exp).then_inc(route_exp_out, 1)
            for t in range(2, TILES):
                copy_p_emb(t)

            def copy_rows(i, c):
                act.wait_ge(hgT_full, num(i, c + 1))
                act.activation(hgT[c % 2].rearrange("p k n -> p (k n)"), bank(4), ACT.Copy).then_inc(hgT_ready, 1)

            def gate(i, c):
                act.wait_ge(gu_full, num(i, c + 1))
                if exists(i, c - 1):
                    act.wait_ge(act_ready, num(i, c))
                act.activation(silu[SLOTS:2 * SLOTS, :], bank(c % 2)[0:SLOTS, :], ACT.Silu).then_inc(silu_ready, 1)

            def copy_y(i, c):
                act.wait_ge(y_full, num(i, c + 1))
                if exists(i, c - RING):
                    act.wait_ge(y_out[c % RING], loads(i, c - RING, RING))
                act.activation(y_rows[c % RING], bank(6 + c % 2), ACT.Copy).then_inc(y_copied, 1)

            def expert(i, c, last=False):
                if not last:
                    copy_rows(i, c + 1)
                gate(i, c)
                if exists(i, c - 1):
                    copy_y(i, c - 1)

            copy_rows(0, 0)
            for e in range(LEAD):
                expert(0, e)
            with act.Fori(1, NE // RING - 1) as i:
                for q in range(RING):
                    expert(i, 1 + q)
            for e in range(NE - RING + 1, NE):
                expert(0, e, last=e == NE - 1)
            copy_y(0, NE - 1)
            n_over = act.value_load(over_i[0:1, OVER:OVER + 1], min_val=0, max_val=OVER)
            with act.If(n_over > 0):
                with act.Fori(0, n_over) as i:
                    act.wait_ge(ov_T, i + 1)
                    act.activation(hgT[1].rearrange("p k n -> p (k n)"), bank(4), ACT.Copy).then_inc(ov_Tc, 1)
                    act.wait_ge(ov_gu, i + 1)
                    act.activation(silu[SLOTS:2 * SLOTS, :], bank(1)[0:SLOTS, :], ACT.Silu).then_inc(ov_silu, 1)
                    act.wait_ge(ov_y, i + 2)
                    act.activation(y_rows[0], bank(7), ACT.Copy).then_inc(ov_yc, 1)
            with act.Else():
                act.nop()
            def square_x2(n):
                t = LAST[n]
                w = tile_width(t)
                act.wait_ge(x2_ready, n + 1)
                act.activation(junk2[0:w, :], x[0:w, t, :], ACT.Square, accum_out=stats[0:w, 32 + t:33 + t]).then_inc(x2_ms, 1)

            square_x2(0)
            square_x2(1)
            for n in range(TILES):
                if n + 2 < TILES:
                    square_x2(n + 2)
                finish_gate(act, n)
            act.wait_ge(out_act, 16 * stored[0])

        @block.tensor
        def _(pe):
            mm = nc.tensor.matmul
            tr = nc.tensor.transpose

            def done(ins, name):
                ins.then_inc(full[AT[name][0]], 1)

            pe.wait_ge(consts_built, 1)
            pe.wait_ge(rows_in, 64)
            done(tr(fill("params")[:, 0:30], params_nat[0:30, :], ident[0:30, 0:30]), "params")
            for t in range(TILES):
                w = tile_width(t)
                pe.wait_ge(xn_ready, t + 1)
                for s, half in enumerate("ab"):
                    name = f"x{t}{half}"
                    wait_free(pe, name)
                    for c in range(4):
                        k = 4 * s + c
                        last = tr(fill(name)[:, c * P:c * P + w], xn[t % 2][0:w, k * P:(k + 1) * P], ident[0:w, 0:w])
                    done(last, name)
                pe.nop().then_inc(xn_used, 1)
            pe.wait_ge(wf_in, 16)
            for s in range(2):
                pe.wait_ge(free[s], AT["x4a" if AT["x4a"][0] == s else "x4b"][1] + 1)
            for s in range(2):
                for k in range(DC):
                    last = mm(psum[0:HC, 2 + s, 0:HALF], w_forget[:, k, :], hT[:, k, s * HALF:(s + 1) * HALF],
                              start=(k == 0), stop=(k == DC - 1))
            last.then_inc(f_full, 1)

            def project(s, q, loaded, copied):
                if q == 0:
                    pe.wait_ge(w_in_s[s], loaded)
                if copied is not None:
                    pe.wait_ge(pj_free, copied)
                for half in range(2):
                    for k in range(DC):
                        last = mm(psum[:, 2 * q + half, 0:HALF], w_ring[s][:, k, q * P:(q + 1) * P],
                                  hT[:, k, half * HALF:(half + 1) * HALF], start=(k == 0), stop=(k == DC - 1))
                last.then_inc(pj_full, 1)

            pe.wait_ge(f_free, 1)
            for s in range(2):
                for q in range(2):
                    project(s, q, 16, None if s == 0 else q + 1)
            def natural(name, m, t):
                w = tile_width(t)
                wait_free(pe, name)
                for c in range(4):
                    last = tr(fill(name)[0:w, c * P:(c + 1) * P], projT[:, m + c, tile_cols(t)], ident)
                done(last, name)

            pe.wait_ge(pj_free, 4)
            natural("qs", MT_Q, QT)
            wait_free(pe, "qb")
            pe.wait_ge(free_of("qs"), AT["qs"][1] + 1)
            pe.wait_ge(consts_built, 2)
            done(mm(fill("qb"), row_sel[0:NB, :], q_s[0:NB, :], start=True, stop=True), "qb")
            wait_free(pe, "f")
            for t in range(TILES):
                w = tile_width(t)
                last = tr(fill("f")[0:w, t * HC:(t + 1) * HC], fT[0:HC, tile_cols(t)], ident[0:HC, 0:HC])
            done(last, "f")
            wait_free(pe, "ws")
            pe.wait_ge(consts_in, 16 * 16)
            for h in range(4):
                last = tr(fill("ws")[:, h * P:(h + 1) * P], ws_nat[:, h, :], ident)
            done(last, "ws")
            with pe.Fori(1, (GROUPS - FIRST) // 2) as i:
                for s in range(2):
                    for q in range(2):
                        project(s, q, i * 16 + 16, i * 4 + (2 * s + q - 1))
            pe.wait_ge(pj_free, 2 * (GROUPS - FIRST))

            natural("ks", MT_K, QT)
            natural("vs", MT_VC, QT)
            wait_free(pe, "suffix")
            pe.wait_ge(suf_ready, 1)
            done(mm(fill("suffix")[:, 0:HC], later, decay[:, PAGE - 1, :], start=True, stop=True), "suffix")
            wait_free(pe, "ct")
            pe.wait_ge(logf_ready, 1)
            for t in range(QT):
                last = mm(fill("ct")[0:HC, t * P:SEQ], f_nat[:, t, :], tri[:, 0:SEQ - t * P], start=(t == 0), stop=(t == QT - 1))
            done(last, "ct")
            for t in range(QT):
                natural(f"k{t}", MT_K, t)
                natural(f"v{t}", MT_VC, t)
            wait_free(pe, "newT")
            pe.wait_ge(new_ready, 1)
            done(tr(fill("newT")[0:NB, 0:HC], new_s[0:NB, :], ident[0:NB, 0:NB]), "newT")

            pe.wait_ge(ct_ready, 1)

            def spread_ck(h):
                if h:
                    pe.wait_ge(ck_ready, h)
                if h > GATE_HEAD + 1:
                    pe.wait_ge(gv_read, h - GATE_HEAD - 1)
                mm(bank(7), ident[0:HC, h:h + 1].to_broadcast([HC, P]), cT[0:HC, :], start=True, stop=True).then_inc(ck_full, 1)

            def rest_step(n):
                half, tile = n // 2 % 2, n // 4
                g, q = first_rest + tile // 2, tile % 2
                if n == 0:
                    pe.wait_ge(free[0], max(AT[m][1] for m in ("suffix", "ct", "k3", "v3", "newT") if AT[m][0] == 0) + 1)
                if n % 2 == 0 and n:
                    pe.wait_ge(half_free, n // 2)
                if n % 8 == 0:
                    pe.wait_ge(w_in_s[g % 2], 16 * (g // 2 + 1))
                for k in range(4 * (n % 2), 4 * (n % 2) + 4):
                    last = mm(bank(4)[:, 0:HALF], w_ring[g % 2][:, k, q * P:(q + 1) * P], hT[:, k, half * HALF:(half + 1) * HALF],
                              start=(k == 0), stop=(k == DC - 1))
                if n % 2:
                    last.then_inc(half_full, 1)

            spread_ck(0)
            units = 4 * HC
            for u in range(units + 2):
                if u < units:
                    h, t = u // QT, u % QT
                    c, q0 = h // 2, (h % 2) * HD
                    if u >= 2:
                        pe.wait_ge(a_read, u - 1)
                    mm(bank(u % 2)[:, 0:P * (t + 1)], projT[q0:q0 + HD, MT_Q + c, t * P:(t + 1) * P],
                       projT[q0:q0 + HD, MT_K + c, 0:P * (t + 1)], start=True, stop=True).then_inc(a_s, 1)
                if u < units:
                    rest_step(rest_steps[u][0])
                if u % QT == 1 and u // QT + 1 < HC:
                    spread_ck(u // QT + 1)
                if 1 <= u <= units:
                    w = u - 1
                    t = w % QT
                    pe.wait_ge(a_p, w + 1)
                    if w >= 2:
                        pe.wait_ge(a_pt, w - 1)
                    for k in range(t + 1):
                        last = tr(bank(2 + w % 2)[:, k * P:(k + 1) * P], s_buf[w % 2][:, k * P:(k + 1) * P], ident)
                    last.then_inc(a_t, 1)
                if u >= 2:
                    w = u - 2
                    h, t = w // QT, w % QT
                    pe.wait_ge(a_pt, w + 1)
                    if w == 0:
                        pe.wait_ge(vn_ready, QT)
                    if w == 1:
                        pe.wait_ge(free[1], max(n for n, name in ((AT[m][1], m) for m in ("suffix", "ct", "newT")) if AT[name][0]) + 1)
                    if w >= 2:
                        pe.wait_ge(a_of, w - 1)
                    for k in range(t + 1):
                        last = mm(bank(6 - w % 2)[:, 0:HD], pT_buf[w % 2][:, k * P:(k + 1) * P],
                                  v_nat[:, k, h * HD:(h + 1) * HD], start=(k == 0), stop=(k == t))
                    last.then_inc(a_o, 1)
                if u < units:
                    for n in rest_steps[u][1:]:
                        rest_step(n)
                if u < units and u % QT == QT - 1 and 0 <= u // QT - GATE_HEAD < TILES:
                    t = u // QT - GATE_HEAD
                    w = tile_width(t)
                    pe.wait_ge(ck_ready, u // QT + 2)
                    pe.wait_ge(half_free, 4)
                    for c in range(2):
                        last = tr(bank(7)[0:w, c * P:(c + 1) * P], projT[:, MT_V + c, tile_cols(t)], ident)
                    last.then_inc(gv_full, 1)

            def values(s, loaded, spread, first=False, last_one=False):
                pe.wait_ge(kv_in[s], loaded)
                pe.wait_ge(px_ready, spread)
                for k in range(KEYS):
                    half = slice((k % 2) * SLOTS, (k % 2 + 1) * SLOTS)
                    ins = mm(bank(7)[half, :], p_exp[s][:, k * HC:(k + 1) * HC, :], ring[s][:, k * WC:(k + 1) * WC],
                             start=(first and k < 2), stop=(last_one and k >= 2), skip_group_check=True)
                ins.then_inc(pv_done, 1)

            k_loads = 16 * (CHUNKS // 4)

            def values_step(i, **flags):
                for s in range(4):
                    values(s, k_loads + 16 * (i + 1), 4 * i + s + 1, flags.get("first", False) and s == 0,
                           flags.get("last_one", False) and s == 3)

            pe.wait_ge(a_read, units)
            pe.wait_ge(a_pt, units)
            pe.wait_ge(a_of, units)
            pe.wait_ge(half_free, rest_halves)

            for t in range(QT):
                wait_free(pe, f"yc{t}")
                for c in range(4):
                    last = tr(fill(f"yc{t}")[:, c * P:(c + 1) * P], y_c[:, t, c * P:(c + 1) * P], ident)
                done(last, f"yc{t}")

            def norm_sums(name):
                n, chunks = NORMS[name]
                pe.wait_ge(sq_ready, n + 1)
                for t in range(QT):
                    for i, c in enumerate(chunks):
                        last = mm(bank(2 if name == "normB" else 3)[:, n * QT + t:n * QT + t + 1], (squares if c < 4 else squares2)[:, c % 4, t * P:(t + 1) * P],
                                  ones[:, 0:1], start=(i == 0), stop=(i == len(chunks) - 1))
                last.then_inc(norms_full, 1)

            def spread_norm(name):
                n = NORMS[name][0]
                pe.wait_ge(rms_ready, 2 if name == "normB" else 1)
                wait_free(pe, name)
                for t in range(QT):
                    last = mm(fill(name)[:, t * P:(t + 1) * P], rms_t[:, n * QT + t:n * QT + t + 1].to_broadcast([P, P]), ident,
                              start=True, stop=True)
                done(last, name)

            wait_free(pe, "state")
            for c in range(4):
                last = tr(fill("state")[:, c * NB:(c + 1) * NB], state[0:NB, c * P:(c + 1) * P], ident[0:NB, 0:NB])
            done(last, "state")
            wait_free(pe, "vnT")
            pe.wait_ge(v_ready, TILES)
            for c in range(2):
                last = tr(fill("vnT")[:, c * NB:(c + 1) * NB], v_norm_s[0:NB, c * P:(c + 1) * P], ident[0:NB, 0:NB])
            done(last, "vnT")
            norm_sums("normC")
            wait_free(pe, "z")
            pe.wait_ge(z_ready, 1)
            for c in range(2):
                tr(fill("z")[0:2, c * P:(c + 1) * P], projT[:, 2 + c, SEQ - 2:SEQ], ident)
                last = tr(fill("z")[0:NB, WA + c * P:WA + (c + 1) * P], projT[:, 2 + c, SEQ:NT], ident)
            done(last, "z")
            for hp in range(2):
                name = f"gate{hp}"
                wait_free(pe, name)
                for t in range(QT):
                    for q in range(2):
                        h = 2 * hp + q
                        last = mm(fill(name)[q * HD:(q + 1) * HD, t * P:(t + 1) * P], v_norm[:, t, h * HD:(h + 1) * HD],
                                  wsT[:, h, :], start=True, stop=True)
                done(last, name)
            def softmax_T(name, need, dst, src):
                wait_free(pe, name)
                pe.wait_ge(smp_req, need)
                n = src.shape[0]
                done(tr(fill(name)[dst, 0:n], src, ident[0:n, 0:n]), name)

            def mix_out(t, quarters=(0, 1, 2, 3)):
                w = tile_width(t)
                if t >= 2 and 0 in quarters:
                    pe.wait_ge(wo_free, t - 1)
                if t == QT:
                    sample_sums(mm, bank(2 * (t % 2)), mixS, w_out).then_inc(wo_full, 1)
                    return
                for m in quarters:
                    n = m // 2
                    for k in range(m % 2 * 4, m % 2 * 4 + 4):
                        heads = (mix_ab if k < 4 else mixT)[:, k, tile_cols(t)]
                        last = mm(bank(2 * (t % 2) + n)[0:w, :], heads, w_out[:, k, n * BANK:(n + 1) * BANK],
                                  start=(k == 0), stop=(k == DC - 1))
                if 3 in quarters:
                    last.then_inc(wo_full, 1)

            def route(t):
                w = tile_width(t)
                pe.wait_ge(h2_ready, TURN[t] + 1)
                for s, half in enumerate("ab"):
                    name = f"h{t}{half}"
                    wait_free(pe, name)
                    for c in range(4):
                        k = 4 * s + c
                        last = tr(fill(name)[:, c * P:c * P + w], xn[t % 2][0:w, k * P:(k + 1) * P], ident[0:w, 0:w])
                    done(last, name)
                name = f"h{t}r"
                wait_free(pe, name)
                pe.wait_ge(h2T_ready, TURN[t] + 1)
                for k in range(DC):
                    last = mm(fill(name)[0:w, 0:NG + NE], h2T[t % 2][:, k, 0:w], w_route[:, k, :], start=(k == 0), stop=(k == DC - 1))
                done(last, name)

            norm_sums("normA")
            norm_sums("normB")
            spread_norm("normC")
            spread_norm("normA")
            spread_norm("normB")
            pe.wait_ge(mix_normed, 1)
            pe.wait_ge(w_o_in, 16)
            pe.wait_ge(route_w_in, 32)
            mix_out(0, (0, 1, 2))
            softmax_T("maxT", 1, slice(0, HC), max_p)
            softmax_T("maxB", 2, slice(0, P), m_exp[0:HC, :])
            softmax_T("maxN", 2, slice(0, NB), mT[0:HC, :])
            mix_out(0, (3,))
            mix_out(1, (0,))
            wait_free(pe, "sum")
            pe.wait_ge(smp_req, 3)
            done(mm(fill("sum")[0:NB, 0:HC], col_sel, sum_p, start=True, stop=True), "sum")
            pe.wait_ge(ck_ready, HC)
            values_step(0, first=True)
            mix_out(1, (1,))
            values_step(1)
            mix_out(1, (2, 3))
            values_step(2)
            route(0)
            for m in range(4):
                values_step(3 + m)
                mix_out(2, (m,))
            route(1)
            values_step(7, last_one=True)
            wait_free(pe, "oN")
            pe.wait_ge(smp_req, 4)
            done(mm(fill("oN")[0:NB, :], own_sample, own_head, start=True, stop=True), "oN")
            mix_out(QT - 1, (0, 1))
            wait_free(pe, "oT")
            pe.wait_ge(smp_req, 5)
            for c in range(4):
                last = tr(fill("oT")[:, c * NB:(c + 1) * NB], prod_s[0:NB, c * P:(c + 1) * P], ident[0:NB, 0:NB])
            done(last, "oT")
            route(QT - 2)
            wait_free(pe, "normS")
            pe.wait_ge(sq_ready, 4)
            for g, chunks in enumerate(((0, 1), (2, 3), (4, 5, 6, 7))):
                for n, c in enumerate(chunks):
                    last = mm(fill("normS")[:, g * NB:(g + 1) * NB], ones, squares_s[:, c, :], start=(n == 0), stop=(n == len(chunks) - 1))
            done(last, "normS")
            mix_out(QT - 1, (2,))
            pe.wait_ge(ple_in, 48)
            pes = (("p01", (0, 1)), ("p23", (2, 3)), ("p4", (4,)))
            for name, tiles in pes:
                wait_free(pe, name)
                for n, t in enumerate(tiles):
                    w = tile_width(t)
                    for k in range(2):
                        last = tr(fill(name)[:, k * 2 * P + n * P:k * 2 * P + n * P + w], p_nat[0:w, t, k * P:(k + 1) * P],
                                  ident[0:w, 0:w])
                done(last, name)
            pe.wait_ge(mixs_normed, 1)
            mix_out(QT)
            mix_out(QT - 1, (3,))
            route(QT)

            def embed(t):
                w = tile_width(t)
                if t == 0:
                    pe.wait_ge(pT_ready, 1)
                    pe.wait_ge(wo_free, TILES - 1)
                if t == 1:
                    pe.wait_ge(wo_free, TILES)
                if t >= 2:
                    pe.wait_ge(pe_free, t - 1)
                for n in range(2):
                    for k in range(2):
                        last = mm(bank(2 * (t % 2) + n)[0:w, :], pT[:, k, tile_cols(t)], w_ple_sb[:, k, n * BANK:(n + 1) * BANK],
                                  start=(k == 0), stop=(k == 1))
                last.then_inc(pe_full, 1)

            embed(0)
            route(QT - 1)
            embed(1)
            wait_free(pe, "rank")
            pe.wait_ge(route_op, 1)
            for n, before in enumerate((strict, ones)):
                last = mm(fill("rank")[:, n * TILES * NE:(n + 1) * TILES * NE], before, chosen.rearrange("p t e -> p (t e)"),
                          start=True, stop=True)
            done(last, "rank")
            embed(2)

            wait_free(pe, "list")
            pe.wait_ge(route_op, 2)
            for n in range(2 * TILES):
                for half in range(2):
                    last = mm(fill("list")[half * SLOTS:(half + 1) * SLOTS, 0:2 * LIST], slot_one[:, n, :], tile_one[:, n, :],
                              start=(n == 0), stop=(n == 2 * TILES - 1))
            done(last, "list")
            embed(3)
            embed(4)
            pe.wait_ge(pe_free, TILES)
            for name in ("list", "rank"):
                pe.wait_ge(free_of(name), AT[name][1] + 1)

            def rows_T(rows, signal):
                hv = rows.rearrange("t (m k) -> t k m", k=DC)
                for k in range(DC):
                    last = tr(bank(4)[:, k * SLOTS:(k + 1) * SLOTS], hv[0:SLOTS, k, :], ident[0:SLOTS, 0:SLOTS])
                last.then_inc(signal, 1)

            def gate_up(s, signal):
                for k in range(DC):
                    for m in range(2):
                        last = mm(bank(s)[m * SLOTS:(m + 1) * SLOTS, :], hgT[s][:, k, :], w_gu[s][m][:, k, :],
                                  start=(k == 0), stop=(k == DC - 1))
                last.then_inc(signal, 1)

            def act_T(signal):
                av = act_nat.rearrange("t (m k) -> t k m", k=FC)
                for k in range(FC):
                    last = tr(bank(5)[:, k * SLOTS:(k + 1) * SLOTS], av[SLOTS:2 * SLOTS, k, :], ident[SLOTS:2 * SLOTS, SLOTS:2 * SLOTS])
                last.then_inc(signal, 1)

            def down(s, signal):
                for k in range(FC):
                    for n in range(2):
                        last = mm(bank(6 + s)[n * SLOTS:(n + 1) * SLOTS, :], actT[s][:, k, :], w_dn[s][:, k, n * BANK:(n + 1) * BANK],
                                  start=(k == 0), stop=(k == FC - 1))
                last.then_inc(signal, 1)

            def rows_step(i, c):
                pe.wait_ge(hg_in[c % RING], loads(i, c, RING))
                if exists(i, c - 1):
                    pe.wait_ge(hgT_ready, num(i, c))
                if not isinstance(i, int):
                    alone(pe)
                rows_T(h_rows[c % RING], hgT_full)

            def down_step(i, c):
                pe.wait_ge(actT_ready, num(i, c + 1))
                if exists(i, c - 2):
                    pe.wait_ge(y_copied, num(i, c - 1))
                pe.wait_ge(dn_in[c % 2], loads(i, c, 2))
                down(c % 2, y_full)

            def expert(i, c, last=False):
                if not last:
                    rows_step(i, c + 1)
                pe.wait_ge(hgT_ready, num(i, c + 1))
                for m in range(2):
                    pe.wait_ge(gu_in[c % 2][m], loads(i, c, 2))
                gate_up(c % 2, gu_full)
                if exists(i, c - 1):
                    down_step(i, c - 1)
                pe.wait_ge(act_ready, num(i, c + 1))
                if not isinstance(i, int):
                    alone(pe)
                act_T(actT_full)

            rows_step(0, 0)
            for e in range(LEAD):
                expert(0, e)
            with pe.Fori(1, NE // RING - 1) as i:
                for q in range(RING):
                    expert(i, 1 + q)
            for e in range(NE - RING + 1, NE):
                expert(0, e, last=e == NE - 1)
            down_step(0, NE - 1)
            pe.nop().then_inc(ov_y, 1)
            pe.wait_ge(y_copied, NE)
            n_over = pe.value_load(over_i[0:1, OVER:OVER + 1], min_val=0, max_val=OVER)
            with pe.If(n_over > 0):
                with pe.Fori(0, n_over) as i:
                    pe.wait_ge(ov_w, i * 48 + 48)
                    pe.wait_ge(ov_rows, i * 16 + 16)
                    alone(pe)
                    rows_T(h_rows[0], ov_T)
                    pe.wait_ge(ov_Tc, i + 1)
                    gate_up(1, ov_gu)
                    pe.wait_ge(ov_act, i + 1)
                    alone(pe)
                    act_T(ov_aT)
                    pe.wait_ge(ov_aTc, i + 1)
                    down(1, ov_y)
            with pe.Else():
                pe.nop()
            pe.wait_ge(wpg_in, 16)
            def transpose_x(i):
                w = tile_width(LAST[i])
                pe.wait_ge(x3_ready, i + 1)
                for s in range(2):
                    if 2 * i + s >= 2:
                        pe.wait_ge(xT_ready, 2 * i + s - 1)
                    for c in range(4):
                        k = 4 * s + c
                        last = tr(bank(4 + s)[:, c * P:c * P + w], xn[i % 2][0:w, k * P:(k + 1) * P], ident[0:w, 0:w])
                    last.then_inc(xT_full, 1)

            transpose_x(0)
            pe.wait_ge(xT_ready, 2)
            sample_sums(mm, bank(0), xT[0], w_gate_ple).then_inc(pg_full, 1)
            transpose_x(1)
            for i in range(1, TILES):
                pe.wait_ge(xT_ready, 2 * i + 2)
                if i >= 2:
                    pe.wait_ge(pg_sig, i - 1)
                for n in range(2):
                    for k in range(DC):
                        if (n, k) == (1, DC // 2) and i + 1 < TILES:
                            transpose_x(i + 1)
                        last = mm(bank(2 * (i % 2) + n), xT[i % 2][:, k, :], w_gate_ple[:, k, n * BANK:(n + 1) * BANK],
                                  start=(k == 0), stop=(k == DC - 1))
                last.then_inc(pg_full, 1)

        @block.vector
        def _(dve):
            step = Steps(dve, dve_step)
            v = nc.vector

            def tell(semaphore):
                dve.nop().then_inc(semaphore, 1)

            def root(dst, src, scale):
                few = dst.shape[1] == 1
                m, y = (r[0:dst.shape[0], 0:dst.shape[1]] for r in ((roots[:, 0, :], roots[:, 1, :]) if few else (root_m, root_y)))
                step(v.tensor_scalar(dst, src, scale, EPS, ALU.mult, ALU.add))
                step(v.tensor_scalar(m, dst, -0.5, None, ALU.mult))
                step(v.tensor_scalar(y.bitcast(I32), dst.bitcast(I32), 1, None, ALU.logical_shift_right))
                step(v.tensor_scalar(y.bitcast(I32), y.bitcast(I32), -1, ROOT_GUESS, ALU.mult, ALU.add))
                for last in (False, False, True):
                    if dst.shape[1] == 1:
                        step(v.tensor_scalar(dst, y, y, m, ALU.mult, ALU.mult))
                    else:
                        step(v.tensor_tensor(dst, y, y, ALU.mult))
                        step(v.tensor_tensor(dst, dst, m, ALU.mult))
                    step(v.scalar_tensor_tensor(out=dst if last else y, in0=dst, scalar=1.5, in1=y, op0=ALU.add, op1=ALU.mult))

            tell(kred)
            step(v.memset(f_nat, 0.0))
            wait_full(dve, "params")
            step(v.tensor_copy(params, fill("params")[:, 0:30]))
            dve.nop().then_inc(free_of("params"), 1)

            def norm_rows(t):
                w = tile_width(t)
                dve.wait_ge(ms_ready, t + 1)
                root(stats[0:w, 56 + t:57 + t], stats[0:w, t:t + 1], 1.0 / D)
                if t >= 2:
                    dve.wait_ge(xn_used, t - 1)
                v.tensor_scalar(xn[t % 2][0:w, :], x[0:w, t, :], stats[0:w, 56 + t:57 + t], None, ALU.mult).then_inc(xn_ready, 1)

            def copy_xT(t):
                w = tile_width(t)
                for s, half in enumerate("ab"):
                    name = f"x{t}{half}"
                    wait_full(dve, name)
                    src = fill(name).rearrange("p (c n) -> p c n", c=4)[:, :, 0:w]
                    v.tensor_tensor(hT[:, 4 * s:4 * s + 4, tile_cols(t)], src, inner(params[:, 4 * s:4 * s + 4], w), ALU.mult)\
                     .then_inc(free_of(name), 1)

            for t in range(TILES):
                norm_rows(t)
                if t:
                    copy_xT(t - 1)
            copy_xT(QT)

            def reduce_keys(s, chunk_words, ready):
                dve.wait_ge(kmul, ready)
                v.tensor_reduce(chunk_words, ring[s].rearrange("p (a d) -> p a d", d=HD), AX.X, ALU.add).then_inc(kred, 1)

            def reduce_static(j):
                reduce_keys(j % 4, scores[:, j * KEYS * HC:(j + 1) * KEYS * HC], j + 1)

            def reduce_loop(first, last):
                with dve.Fori(first, last) as i:
                    for s in range(4):
                        reduce_keys(s, scores[:, bass.ds(i * (4 * KEYS * HC) + s * KEYS * HC, KEYS * HC)], i * 4 + (s + 1))

            wait_full(dve, "f")
            dve.wait_ge(consts_in, 16 * 16)
            step(v.tensor_tensor(f_nat[:, 0:QT, :], fill("f")[:, 0:QT * HC].rearrange("p (t h) -> p t h", h=HC), outer(bf_bc, QT), ALU.add))
            step(v.tensor_tensor(f_nat[0:NB, QT, :], fill("f")[0:NB, QT * HC:TILES * HC], bf_bc[0:NB, :], ALU.add))
            dve.nop().then_inc(free_of("f"), 1)
            step(v.tensor_scalar(f_a, f_nat, -1.0, None, ALU.mult))
            step(v.tensor_tensor(f_a, f_nat, f_a, ALU.max))
            tell(f_part)
            wait_full(dve, "ws")
            v.tensor_tensor(wsT, fill("ws").rearrange("p (h n) -> p h n", h=4), outer(tri[:, 0:P], 4), ALU.mult)\
             .then_inc(free_of("ws"), 1)
            dve.wait_ge(f_part, 2)
            step(v.tensor_scalar(f_c, f_b, 1.0, None, ALU.add))
            tell(f_part)
            step(v.tensor_scalar(f_a, f_c, -1.0, None, ALU.add))
            dve.wait_ge(f_part, 4)
            step(v.tensor_scalar(f_c, f_a, 0.0, None, ALU.is_equal))
            step(v.tensor_tensor(f_a, f_a, f_c, ALU.add))
            step(v.reciprocal(f_a, f_a))
            step(v.tensor_tensor(f_d, f_d, f_b, ALU.mult))
            step(v.tensor_tensor(f_d, f_d, f_a, ALU.mult))
            step(v.tensor_tensor(f_c, f_c, f_b, ALU.mult))
            step(v.tensor_tensor(f_d, f_d, f_c, ALU.add))
            step(v.scalar_tensor_tensor(out=f_nat, in0=f_nat, scalar=0.0, in1=f_d, op0=ALU.min, op1=ALU.subtract))
            tell(logf_ready)
            dve.wait_ge(lf_in, 16)
            for h in range(HC):
                ins = v.tensor_tensor_scan(decay[:, :, h], ones, logf_pages[:, :, h], 0.0, ALU.mult, ALU.add)
                step(ins)
            tell(suf_ready)
            reduce_loop(0, EARLY // 4)
            dve.wait_ge(sample_nat, 1)
            step(v.tensor_tensor(prod_s[0:NB, :], q_s[0:NB, :], k_s[0:NB, :], ALU.mult))
            step(v.tensor_reduce(new_s[0:NB, :], prod_s[0:NB, :].rearrange("p (h d) -> p h d", h=HC), AX.X, ALU.add))
            step(v.tensor_tensor(new_s[0:NB, :], new_s[0:NB, :], f_nat[0:NB, QT, :], ALU.subtract))
            tell(new_ready)
            wait_full(dve, "suffix")
            step(v.tensor_tensor(page_suf, fill("suffix")[:, 0:HC], decay[:, PAGE - 1, :], ALU.add))
            dve.nop().then_inc(free_of("suffix"), 1)
            step(v.tensor_tensor(decay, outer(page_suf, PAGE), decay, ALU.subtract))
            for t in range(QT):
                wait_full(dve, f"v{t}")
                step(v.tensor_copy(v_nat[:, t, :], fill(f"v{t}")))
                dve.nop().then_inc(free_of(f"v{t}"), 1)
                tell(vn_ready)
                if t % 2:
                    reduce_static(EARLY + t // 2)
            wait_full(dve, "newT")
            v.tensor_copy(newT_s[0:HC, :], fill("newT")[0:HC, 0:NB]).then_inc(free_of("newT"), 1)

            def layer_norm(t):
                w = tile_width(t)
                src, dst = bank(7)[0:w, 0:WB], v_norm[:, t, :] if t < QT else v_norm_s[0:w, :]
                dve.wait_ge(gv_full, t + 1)
                step(v.bn_stats(bn[0:w, :], src))
                step(v.bn_aggr(mv[0:w, :], bn[0:w, :]))
                root(mv[0:w, 1:2], mv[0:w, 1:2], 1.0)
                step(v.tensor_scalar(dst, src, mv[0:w, 0:1], mv[0:w, 1:2], ALU.subtract, ALU.mult))
                tell(gv_read)
                step(v.tensor_tensor(dst, dst, ln_g_bc[0:w, :], ALU.mult))
                step(v.tensor_tensor(dst, dst, ln_b_bc[0:w, :], ALU.add))
                tell(v_ready)

            units = 4 * HC
            for u in range(units + 3):
                if u < units:
                    h, t = u // QT, u % QT
                    nk = P * (t + 1)
                    sb = s_buf[u % 2]
                    dve.wait_ge(a_s, u + 1)
                    dve.wait_ge(ck_ready, h + 1)
                    if u >= 2:
                        dve.wait_ge(a_t, u - 1)
                    v.scalar_tensor_tensor(out=sb[:, 0:nk], in0=bank(u % 2)[:, 0:nk], scalar=SCALE, in1=ck_bc[h % 2][:, 0:nk],
                                           op0=ALU.mult, op1=ALU.subtract).then_inc(a_read, 1)
                    dve.wait_ge(a_read, u + 1)
                    step(v.tensor_tensor(sb[:, nk - P:nk], sb[:, nk - P:nk], mask, ALU.add))
                    v.tensor_reduce(stats[:, 8 + u % 2:9 + u % 2], sb[:, 0:nk], AX.X, ALU.max, negate=True).then_inc(a_m, 1)
                if u >= 3:
                    w = u - 3
                    h, t = w // QT, w % QT
                    dve.wait_ge(a_o, w + 1)
                    if w >= 2:
                        dve.wait_ge(a_of, w - 1)
                    step(v.reciprocal(stats[:, 20 + w % 2:21 + w % 2], stats[:, 16 + w % 4:17 + w % 4]))
                    v.tensor_scalar(y_c[:, t, h * HD:(h + 1) * HD], bank(6 - w % 2)[:, 0:HD], stats[:, 20 + w % 2:21 + w % 2], None,
                                    ALU.mult).then_inc(a_of, 1)
                if u < units and u % QT == 0 and 0 <= u // QT - GATE_HEAD - 1 < TILES:
                    layer_norm(u // QT - GATE_HEAD - 1)
                if u % 2 == 1 and u < units:
                    reduce_static(EARLY + 2 + u // 2)
            left = EARLY + 2 + 2 * HC
            reduce_static(left)
            dve.wait_ge(half_free, rest_halves - 4)
            z = projT[:, 2:4, :]
            step(v.tensor_tensor(z, z, projT[:, 4:6, :], ALU.mult))
            tell(z_ready)
            wait_full(dve, "state")

            def tap(j, c):
                return params[:, 16 + 2 * j + c:17 + 2 * j + c]

            for c in range(2):
                y = mix_ab[:, c, :]
                step(v.tensor_scalar(y, z[:, c, :], tap(2, c), None, ALU.mult))
                for j in (1, 0):
                    d = 2 - j
                    step(v.scalar_tensor_tensor(out=y[:, d:SEQ], in0=z[:, c, 0:SEQ - d], scalar=tap(j, c), in1=y[:, d:SEQ],
                                                op0=ALU.mult, op1=ALU.add))
                    step(v.scalar_tensor_tensor(out=y[:, SEQ:NT], in0=fill("state")[:, (2 * j + c) * NB:(2 * j + c + 1) * NB],
                                                scalar=tap(j, c), in1=y[:, SEQ:NT], op0=ALU.mult, op1=ALU.add))
            dve.nop().then_inc(free_of("state"), 1)
            step(v.tensor_tensor(mix_ab[:, 0:2, :], mix_ab[:, 0:2, :], projT[:, 0:2, :], ALU.mult))
            tell(z_ready)
            reduce_static(left + 1)
            wait_full(dve, "vnT")
            for hp in range(2):
                step(v.tensor_scalar(gate_s[:, hp, :], fill("vnT")[:, hp * NB:(hp + 1) * NB], w00[:, hp:hp + 1], bs_bc[:, hp, 0:1],
                                     ALU.mult, ALU.add))
            dve.nop().then_inc(free_of("vnT"), 1)
            dve.wait_ge(half_free, rest_halves)
            step(v.tensor_tensor(mix_ab[:, 2:4, SEQ:NT], gate_s, projT[:, MT_U:MT_U + 2, SEQ:NT], ALU.mult))
            for hp in range(2):
                wait_full(dve, f"gate{hp}")
                g = gate_tmp.rearrange("p (t n) -> p t n", t=QT)
                step(v.tensor_tensor(g, fill(f"gate{hp}").rearrange("p (t n) -> p t n", t=QT), outer(bs_bc[:, hp, :], QT), ALU.add))
                dve.nop().then_inc(free_of(f"gate{hp}"), 1)
                y = mix_ab[:, 2 + hp, 0:SEQ]
                step(v.tensor_tensor(y, y, gate_tmp, ALU.mult))
            tell(mix_ready)

            def normalise(name):
                wait_full(dve, name)
                for c in NORMS[name][1]:
                    y = (mix_ab if c < 4 else mixT)[:, c, 0:SEQ]
                    step(v.scalar_tensor_tensor(out=y, in0=y, scalar=params[:, 8 + c:9 + c], in1=fill(name), op0=ALU.mult, op1=ALU.mult))
                dve.nop().then_inc(free_of(name), 1)

            first = rms_t[:, 0:2 * QT]
            dve.wait_ge(norms_full, 2)
            step(v.tensor_copy(first, bank(3)[:, 0:2 * QT]))
            step(v.tensor_scalar(first[:, 0:QT], first[:, 0:QT], WA / WC, None, ALU.mult))
            root(first, first, 1.0 / WA)
            tell(rms_ready)
            reduce_static(left + 2)
            normalise("normC")
            normalise("normA")
            dve.wait_ge(norms_full, 3)
            root(rms_t[:, 2 * QT:], bank(2)[:, 2 * QT:3 * QT], 1.0 / WA)
            tell(rms_ready)
            reduce_static(left + 3)
            normalise("normB")
            tell(mix_normed)
            reduce_static(left + 4)
            reduce_static(left + 5)
            assert left + 6 == CHUNKS
            dve.wait_ge(kred, CHUNKS + 1)
            s3 = scores.rearrange("p (k h) -> p k h", h=HC)
            by_head = scores.rearrange("p (k h) -> p h k", h=HC)
            step(v.tensor_tensor(s3, s3, decay, ALU.add))
            step(v.tensor_reduce(max_p, by_head, AX.X, ALU.max))
            tell(smp_req)
            wait_full(dve, "maxT")
            step(v.tensor_reduce(mT[0:HC, :], fill("maxT")[0:HC, 0:P].rearrange("p (b g) -> p b g", b=NB), AX.X, ALU.max))
            dve.nop().then_inc(free_of("maxT"), 1)
            step(v.tensor_tensor(mT[0:HC, :], mT[0:HC, :], newT_s[0:HC, :], ALU.max))
            step(v.tensor_copy(m_exp[0:HC, :].rearrange("p (b g) -> p b g", b=NB), inner(mT[0:HC, :], PAGES)))
            tell(smp_req)
            wait_full(dve, "maxB")
            step(v.tensor_copy(max_b, fill("maxB")[:, 0:HC]))
            dve.nop().then_inc(free_of("maxB"), 1)
            step(v.tensor_tensor(s3, s3, outer(max_b, PAGE), ALU.subtract))
            tell(smp_exp)
            wait_full(dve, "maxN")
            step(v.tensor_tensor(new_s[0:NB, :], new_s[0:NB, :], fill("maxN")[0:NB, 0:HC], ALU.subtract))
            dve.nop().then_inc(free_of("maxN"), 1)
            tell(smp_exp)
            def spread_p(s, words, used):
                if used is not None:
                    dve.wait_ge(pv_done, used)
                v.tensor_tensor(p_exp[s], inner(words, NB), outer(col_sel, KEYS * HC), ALU.mult).then_inc(px_ready, 1)

            W = KEYS * HC

            def spread_step(i):
                for s in range(4):
                    spread_p(s, scores[:, (4 * i + s) * W:(4 * i + s + 1) * W], 4 * i + s - 3 if i else None)

            def add_out(t):
                w = tile_width(t)
                dve.wait_ge(wo_full, TURN[t] + 1)
                if t == QT:
                    mine = x[0:NB, QT, :]
                    step(v.tensor_tensor(mine[:, 0:BANK], mine[:, 0:BANK], bank(2 * (t % 2))[0:NB, :], ALU.add))
                    dve.wait_ge(parts_ready, 3)
                    step(v.tensor_tensor(mine[:, BANK:D], mine[:, BANK:D], parts_o[0:NB, 0, :], ALU.add))
                    v.tensor_tensor(mine.rearrange("p (a n) -> p a n", a=2), mine.rearrange("p (a n) -> p a n", a=2),
                                    parts_o[0:NB, 1:3, :], ALU.add).then_inc(wo_free, 1)
                    return
                pair = psum[0:w, 2 * (t % 2):2 * (t % 2) + 2, :]
                v.tensor_tensor(x[0:w, t, :].rearrange("p (a n) -> p a n", a=2), x[0:w, t, :].rearrange("p (a n) -> p a n", a=2), pair,
                                ALU.add).then_inc(wo_free, 1)

            def second_norm(t):
                w = tile_width(t)
                dve.wait_ge(x1_ms, TURN[t] + 1)
                root(stats[0:w, 56:57], stats[0:w, 24 + t:25 + t], 1.0 / D)
                v.scalar_tensor_tensor(out=xn[t % 2][0:w, :], in0=x[0:w, t, :], scalar=stats[0:w, 56:57], in1=g_ffn_bc[0:w, :],
                                       op0=ALU.mult, op1=ALU.mult).then_inc(h2_ready, 1)

            def take_logits(t):
                w = tile_width(t)
                wait_full(dve, f"h{t}r")
                v.tensor_tensor(logits[0:w, t, :], fill(f"h{t}r")[0:w, 0:NG + NE], b_route[0:w, :], ALU.add)\
                 .then_inc(free_of(f"h{t}r"), 1)

            step(v.memset(logits, 0.0))
            dve.wait_ge(smp_p, 1)
            step(v.tensor_reduce(sum_p, by_head, AX.X, ALU.add))
            tell(smp_req)
            spread_step(0)
            wait_full(dve, "sum")
            dve.wait_ge(smp_p, 2)
            step(v.tensor_tensor(sum_s[0:NB, :], fill("sum")[0:NB, 0:HC], pnew[0:NB, :], ALU.add))
            dve.nop().then_inc(free_of("sum"), 1)
            step(v.reciprocal(sum_s[0:NB, :], sum_s[0:NB, :]))
            add_out(0)
            second_norm(0)
            spread_step(1)
            spread_step(2)
            add_out(1)
            second_norm(1)
            spread_step(3)
            take_logits(0)
            for i in range(4, 8):
                spread_step(i)
            add_out(2)
            take_logits(1)
            second_norm(2)
            dve.wait_ge(pv_done, CHUNKS)
            step(v.tensor_tensor(own_head.rearrange("p (h d) -> p h d", h=HC), bank(7).rearrange("p (h d) -> p h d", h=HC),
                                 inner(head_sel, HD), ALU.mult))
            tell(smp_req)
            q3, v3, o3 = (m[0:NB, :].rearrange("p (h d) -> p h d", h=HC) for m in (q_s, v_s, prod_s))
            step(v.tensor_tensor(q3, v3, inner(pnew[0:NB, :], HD), ALU.mult))
            wait_full(dve, "oN")
            step(v.tensor_tensor(prod_s[0:NB, :], fill("oN")[0:NB, :], q_s[0:NB, :], ALU.add))
            dve.nop().then_inc(free_of("oN"), 1)
            step(v.tensor_tensor(o3, o3, inner(sum_s[0:NB, :], HD), ALU.mult))
            tell(smp_req)
            wait_full(dve, "oT")
            step(v.tensor_copy(mixT[:, 4:8, SEQ:NT], fill("oT")[:, 0:4 * NB].rearrange("p (c b) -> p c b", c=4)))
            dve.nop().then_inc(free_of("oT"), 1)
            tell(mixs_ready)
            take_logits(QT - 2)
            wait_full(dve, "normS")
            sums = rms_bc[:, 0:3 * NB]
            step(v.tensor_copy(sums, fill("normS")[:, 0:3 * NB]))
            step(v.tensor_scalar(sums[:, 2 * NB:], sums[:, 2 * NB:], WA / WC, None, ALU.mult))
            root(sums, sums, 1.0 / WA)
            for g, chunks in enumerate(((0, 1), (2, 3), (4, 5, 6, 7))):
                for c in chunks:
                    step(v.scalar_tensor_tensor(out=mixS[:, c, :], in0=(mix_ab if c < 4 else mixT)[:, c, SEQ:NT],
                                                scalar=params[:, 8 + c:9 + c], in1=sums[:, g * NB:(g + 1) * NB],
                                                op0=ALU.mult, op1=ALU.mult))
            dve.nop().then_inc(free_of("normS"), 1)
            tell(mixs_normed)
            add_out(QT)
            second_norm(QT)
            add_out(QT - 1)
            second_norm(QT - 1)
            take_logits(QT)
            take_logits(QT - 1)
            for t in (QT - 1, QT):
                dve.wait_ge(free_of(f"h{t}r"), AT[f"h{t}r"][1] + 1)

            def first_of(one, scratch, index, src, top_value, n):
                step(v.tensor_tensor(scratch, src, inner(top_value, n), ALU.is_equal))
                step(v.tensor_scalar(scratch, scratch, -1.0, -BIG, ALU.add, ALU.mult))
                step(v.tensor_tensor(scratch, scratch, outer(iota[:, 0:n], TILES), ALU.add))
                step(v.tensor_reduce(index, scratch, AX.X, ALU.min))
                step(v.tensor_tensor(one, outer(iota[:, 0:n], TILES), inner(index, n), ALU.is_equal))

            grp, exp_ = logits[:, :, 0:NG], logits[:, :, NG:]
            g_top, g_idx, g_sum, l1, gap, l2, share = r5
            q_num, r_pos, base_e, t_num = r10
            step(v.tensor_reduce(g_top, grp, AX.X, ALU.max))
            step(v.tensor_tensor(eg, grp, inner(g_top, NG), ALU.subtract))
            tell(route_exp_in)
            first_of(g_one, gcand, g_idx, grp, g_top, NG)
            step(v.tensor_scalar(gcand, g_one, -1.0, BIG, ALU.add, ALU.mult))
            step(v.tensor_copy(masked.rearrange("p t (g e) -> p (t g) e", g=NG), inner(gcand.rearrange("p t g -> p (t g)"), NE // NG)))
            step(v.tensor_tensor(masked, masked, exp_, ALU.add))
            step(v.tensor_reduce(l1, masked, AX.X, ALU.max))
            first_of(e_one[0], cand, e_idx[0], masked, l1, NE)
            step(v.tensor_scalar(cand, e_one[0], -BIG, None, ALU.mult))
            step(v.tensor_tensor(m2, masked, cand, ALU.add))
            step(v.tensor_reduce(l2, m2, AX.X, ALU.max))
            first_of(e_one[1], cand, e_idx[1], m2, l2, NE)
            step(v.tensor_tensor(gap, l2, l1, ALU.subtract))
            tell(route_exp_in)
            step(v.tensor_tensor(e_pair, e_pair, inner(valid, NE), ALU.mult))
            step(v.tensor_tensor(chosen, e_one[0], e_one[1], ALU.add))
            tell(route_op)
            wait_full(dve, "rank")
            step(v.tensor_copy(rank, fill("rank")[:, 0:TILES * NE].rearrange("p (t e) -> p t e", e=NE)))
            step(v.tensor_copy(masked, fill("rank")[:, TILES * NE:2 * TILES * NE].rearrange("p (t e) -> p t e", e=NE)))
            dve.nop().then_inc(free_of("rank"), 1)
            for t in range(1, TILES):
                step(v.tensor_tensor(masked[:, t, :], masked[:, t, :], masked[:, t - 1, :], ALU.add))
            step(v.tensor_tensor(rank[:, 1:TILES, :], rank[:, 1:TILES, :], masked[:, 0:QT, :], ALU.add))
            count = masked[:, QT, :]
            step(v.tensor_tensor(cmp8, inner(count, QMAX), outer(steps, NE), ALU.is_gt))
            step(v.tensor_reduce(tiles_over, cmp8, AX.X, ALU.add))
            step(v.tensor_tensor_scan(over_end, ones[:, 0:NE], tiles_over, 0.0, ALU.mult, ALU.add))
            step(v.tensor_tensor(over_base, over_end, tiles_over, ALU.subtract))
            both = "p (c n) e -> p c (n e)"
            step(v.tensor_tensor(prod_r.rearrange(both, c=2), outer(rank.rearrange("p t e -> p (t e)"), 2), e_pair.rearrange(both, c=2),
                                 ALU.mult))
            step(v.tensor_reduce(r_pos, prod_r, AX.X, ALU.add))
            step(v.tensor_tensor(prod_r, outer(over_base, 2 * TILES), e_pair, ALU.mult))
            step(v.tensor_reduce(base_e, prod_r, AX.X, ALU.add))
            step(v.tensor_tensor(cmp10, inner(r_pos, QMAX), outer(steps, 2 * TILES), ALU.is_ge))
            step(v.tensor_reduce(q_num, cmp10, AX.X, ALU.add))
            step(v.scalar_tensor_tensor(out=r_pos, in0=q_num, scalar=-float(SLOTS), in1=r_pos, op0=ALU.mult, op1=ALU.add))
            step(v.tensor_tensor(slot_one, outer(iota, 2 * TILES), inner(r_pos, SLOTS), ALU.is_equal))
            step(v.scalar_tensor_tensor(out=base_e, in0=base_e, scalar=float(NE - 1), in1=q_num, op0=ALU.add, op1=ALU.add))
            step(v.tensor_tensor(base_e, base_e, e_idx_pair, ALU.subtract))
            step(v.scalar_tensor_tensor(out=t_num, in0=q_num, scalar=0.0, in1=base_e, op0=ALU.is_gt, op1=ALU.mult))
            step(v.tensor_tensor(t_num, t_num, e_idx_pair, ALU.add))
            hit = tile_one[:, :, 0:LIST]
            step(v.tensor_tensor(hit, outer(iota[:, 0:LIST], 2 * TILES), inner(t_num, LIST), ALU.is_equal))
            step(v.tensor_tensor(hit, hit, inner(valid, LIST), ALU.mult))
            step(v.tensor_tensor(tile_one[:, :, LIST:], hit, inner(tokid, LIST), ALU.mult))
            step(v.tensor_tensor(hit, hit, inner(rowid, LIST), ALU.mult))
            tell(route_op)
            dve.wait_ge(route_exp_out, 2)
            step(v.tensor_reduce(g_sum, eg, AX.X, ALU.add))
            step(v.tensor_scalar(share, gap, 1.0, None, ALU.add))
            step(v.tensor_tensor(share, share, g_sum, ALU.mult))
            step(v.reciprocal(w_keep[0], share))
            step(v.tensor_tensor(w_keep[1], w_keep[0], gap, ALU.mult))
            step(v.tensor_tensor(cmp_over, outer(over_end, OVER), inner(iota[:, 0:OVER], NE), ALU.is_le))
            step(v.tensor_reduce(over_f[:, 0:OVER], cmp_over, AX.X, ALU.add))
            step(v.tensor_scalar(over_f[:, 0:OVER], over_f[:, 0:OVER], float(NE - 1), None, ALU.min))
            step(v.tensor_copy(over_f[:, OVER:OVER + 1], over_end[:, NE - 1:NE]))
            step(v.tensor_copy(over_i[:, 0:OVER + 1], over_f))
            wait_full(dve, "list")
            step(v.tensor_copy(list_f, fill("list")[:, 0:2 * LIST]))
            dve.nop().then_inc(free_of("list"), 1)
            step(v.tensor_copy(tok_list[:, :], list_f[:, LIST:]))
            step(v.tensor_scalar(list_f[:, LIST:], list_f[:, 0:LIST], 0.0, float(4 * PAIRS), ALU.is_equal, ALU.mult))
            step(v.tensor_scalar(list_f[:, 0:LIST], list_f[:, 0:LIST], 2.0, half_row, ALU.mult, ALU.add))
            step(v.tensor_tensor(list_f[:, 0:LIST], list_f[:, 0:LIST], list_f[:, LIST:], ALU.add))
            step(v.tensor_copy(row_list[:, :], list_f[:, 0:LIST]))
            dve.nop().then_inc(lists_ready, 1)

            upper = slice(SLOTS, 2 * SLOTS)

            def activate(i, c):
                dve.wait_ge(silu_ready, num(i, c + 1))
                if exists(i, c - 1):
                    dve.wait_ge(actT_full, num(i, c))
                v.tensor_tensor(act_nat[upper, :], silu[upper, :], bank(c % 2)[upper, :], ALU.mult).then_inc(act_ready, 1)
                dve.wait_ge(actT_full, num(i, c + 1))
                if exists(i, c - 2):
                    dve.wait_ge(y_full, num(i, c - 1))
                v.tensor_copy(actT[c % 2].rearrange("p k n -> p (k n)"), bank(5)[:, 0:FC * SLOTS]).then_inc(actT_ready, 1)

            for e in range(LEAD):
                activate(0, e)
            with dve.Fori(1, NE // RING - 1) as i:
                for q in range(RING):
                    activate(i, 1 + q)
            for e in range(NE - RING + 1, NE):
                activate(0, e)
            n_over = dve.value_load(over_i[0:1, OVER:OVER + 1], min_val=0, max_val=OVER)
            with dve.If(n_over > 0):
                with dve.Fori(0, n_over) as i:
                    dve.wait_ge(ov_silu, i + 1)
                    v.tensor_tensor(act_nat[upper, :], silu[upper, :], bank(1)[upper, :], ALU.mult).then_inc(ov_act, 1)
                    dve.wait_ge(ov_aT, i + 1)
                    v.tensor_copy(actT[1].rearrange("p k n -> p (k n)"), bank(5)[:, 0:FC * SLOTS]).then_inc(ov_aTc, 1)
            with dve.Else():
                dve.nop()

            def add_experts(n):
                t = LAST[n]
                w = tile_width(t)
                dve.wait_ge(pairs_ready[n % 2], 16 * (n // 2 + 1))
                for c in range(2):
                    step(v.scalar_tensor_tensor(out=x[0:w, t, :], in0=pairs_in[n % 2][0:w, c * D:(c + 1) * D],
                                                scalar=w_keep[c][0:w, t:t + 1], in1=x[0:w, t, :], op0=ALU.mult, op1=ALU.add))
                tell(x2_ready)

            def norm_x2(n):
                t = LAST[n]
                w = tile_width(t)
                dve.wait_ge(x2_ms, n + 1)
                root(stats[0:w, 57:58], stats[0:w, 32 + t:33 + t], 1.0 / D)
                v.tensor_scalar(xn[n % 2][0:w, :], x[0:w, t, :], stats[0:w, 57:58], None, ALU.mult).then_inc(x3_ready, 1)

            def scale_xT(n):
                w = tile_width(LAST[n])
                for s in range(2):
                    dve.wait_ge(xT_full, 2 * n + s + 1)
                    src = bank(4 + s).rearrange("p (c n) -> p c n", c=4)[:, :, 0:w]
                    v.tensor_tensor(xT[n % 2][:, 4 * s:4 * s + 4, 0:w], src, inner(params[:, 22 + 4 * s:26 + 4 * s], w), ALU.mult)\
                     .then_inc(xT_ready, 1)

            def add_gated(n):
                t = LAST[n]
                w = tile_width(t)
                g = ple_gate[n % 2][0:w, :]
                if t == QT:
                    dve.wait_ge(parts_ready, 6)
                    step(v.tensor_tensor(g[:, 0:BANK], parts_g[0:NB, 1, :], bank(2 * (n % 2))[0:NB, :], ALU.add))
                    step(v.tensor_tensor(g[:, BANK:D], parts_g[0:NB, 0, :], parts_g[0:NB, 2, :], ALU.add))
                    tell(parts_summed)
                dve.wait_ge(pg_sig, n + 1)
                step(v.tensor_tensor(g, g, p_emb[0:w, t, :], ALU.mult))
                step(v.tensor_tensor(x[0:w, t, :], x[0:w, t, :], g, ALU.add))
                tell(x4_ready)

            def norm_out(n):
                t = LAST[n]
                w = tile_width(t)
                dve.wait_ge(x4_ms, n + 1)
                root(stats[0:w, 58:59], stats[0:w, 48 + t:49 + t], 1.0 / D)
                if n >= 2:
                    dve.wait_ge(y_stored[n % 2], 16 * (n // 2))
                v.scalar_tensor_tensor(out=y_buf[n % 2][0:w, :], in0=x[0:w, t, :], scalar=stats[0:w, 58:59], in1=g_fin[0:w, :],
                                       op0=ALU.mult, op1=ALU.mult).then_inc(y_final, 1)

            dve.wait_ge(gfin_in, 16)
            for n in range(2):
                add_experts(n)
                norm_x2(n)
                scale_xT(n)
            add_experts(2)
            norm_x2(2)
            add_gated(0)
            scale_xT(2)
            norm_out(0)
            for n in range(1, TILES):
                ahead = n + 2 < TILES
                if ahead:
                    add_experts(n + 2)
                add_gated(n)
                if ahead:
                    norm_x2(n + 2)
                norm_out(n)
                if ahead:
                    scale_xT(n + 2)


INPUTS = ["x_prompt", "x_sample", "p_prompt", "p_sample", "cache_k", "cache_v", "cache_logf", "state_conv", "page_table",
          "g_mix", "w_in", "conv_w", "ln_g", "ln_b", "w_s", "b_s", "b_f", "g_out", "w_o", "g_ffn", "w_grp", "b_grp",
          "w_rt", "b_rt", "w_gate", "w_up", "w_down", "g_ple", "w_ple", "w_ple_gate", "g_final"]
OUTPUTS = [(1, SEQ, D), (NB, 1, D), (1, 1, SEQ, HC, HD), (1, 1, SEQ, HC, HD), (1, 1, SEQ, HC), (1, 1, 2, WA),
           (1, NB, 1, HC, HD), (1, NB, 1, HC, HD), (1, NB, 1, HC), (1, NB, 2, WA), (1, NB, 1, WB)]


def kernel(**inputs):
    import numpy as _np
    import concourse.bacc as _bacc
    from concourse.bass_utils import run_bass_kernel_spmd as _run

    nc = _bacc.Bacc("TRN2", target_bir_lowering=False, num_devices=1)
    arrays, a = {}, {}
    for name in INPUTS:
        arrays[f"in_{name}"] = _np.ascontiguousarray(inputs[name])
        dt = mybir.dt.from_np(arrays[f"in_{name}"].dtype)
        a[name] = nc.dram_tensor(f"in_{name}", arrays[f"in_{name}"].shape, dt, kind="ExternalInput").ap()
    o = [nc.dram_tensor(f"out_{i}", shape, F32, kind="ExternalOutput").ap() for i, shape in enumerate(OUTPUTS)]
    build(nc, a, o)
    r = _run(nc, [arrays], core_ids=[0])
    return tuple(r.results[0][f"out_{i}"] for i in range(len(OUTPUTS)))
```
